# Optimizing a Trainium2 kernel written in Bass

```python
import math
import jax
import jax.numpy as jnp
from jax import lax
import numpy as np
import jax, jax.numpy as jnp

D_MODEL = 1024
BATCH = 1
SEQ = 256
DEPTH = 1

GRID_W = 64
CTX_LEN = 256
NORM_EPS = 1e-6
N_MOD = 6

NA_HEADS = 16
NA_HEAD_DIM = 64
NA_WIDTH = NA_HEADS * NA_HEAD_DIM
NA_KH = 8
NA_KW = 16
ROPE_BASE = 10000.0

SSD_WIDTH = 2 * D_MODEL
SSD_HEAD_DIM = 64
SSD_HEADS = SSD_WIDTH // SSD_HEAD_DIM
SSD_GROUPS = 4
SSD_STATE = 128
SSD_CONV = 5
SSD_CHUNK = 128
SSD_XBC = SSD_WIDTH + 2 * SSD_GROUPS * SSD_STATE

N_EXPERTS = 16
EXPERT_FF = 2048
EC_CAPACITY_FACTOR = 2

IN_COLS = 3 * NA_WIDTH + SSD_WIDTH + SSD_XBC + 2 * SSD_HEADS + 2 * D_MODEL


def _rmsnorm(x, g):
    xf = x.astype(jnp.float32)
    xf = xf * lax.rsqrt(jnp.mean(xf * xf, axis=-1, keepdims=True) + NORM_EPS)
    return (xf * g.astype(jnp.float32)).astype(x.dtype)

def _modulate(x, g, shift, scale):
    return _rmsnorm(x, g) * (1 + scale) + shift

def _ada(cvec, w_ada, b_ada):
    mod = jax.nn.silu(cvec) @ w_ada + b_ada
    return jnp.split(mod, N_MOD, axis=-1)

def _split_in(p):
    offs = np.cumsum([NA_WIDTH, NA_WIDTH, NA_WIDTH, SSD_WIDTH, SSD_XBC, 2 * SSD_HEADS])
    return jnp.split(p, [int(o) for o in offs], axis=-1)

def _heads(t):
    return t.reshape(t.shape[0], t.shape[1], NA_HEADS, NA_HEAD_DIM)

def _rotate(t, pos):
    half = t.shape[-1] // 2
    inv_freq = ROPE_BASE ** (-jnp.arange(half, dtype=jnp.float32) / half)
    ang = pos.astype(jnp.float32)[:, None] * inv_freq[None, :]
    cos = jnp.cos(ang)[:, None, :].astype(t.dtype)
    sin = jnp.sin(ang)[:, None, :].astype(t.dtype)
    t1, t2 = t[..., :half], t[..., half:]
    return jnp.concatenate([t1 * cos - t2 * sin, t1 * sin + t2 * cos], axis=-1)

def _rope_2d(t, rows, cols):
    da = t.shape[-1] // 2
    return jnp.concatenate([_rotate(t[..., :da], rows), _rotate(t[..., da:], cols)], axis=-1)

def _neighbourhood_attention(q, k, v, k_ctx, v_ctx, rpb):
    Bsz, L, H, Dh = q.shape
    rows = L // GRID_W
    kh = min(NA_KH, rows)
    n_loc = kh * GRID_W
    scale = Dh ** -0.5
    qg = q.reshape(Bsz, rows, GRID_W, H, Dh)
    kg = k.reshape(Bsz, rows, GRID_W, H, Dh)
    vg = v.reshape(Bsz, rows, GRID_W, H, Dh)
    col = jnp.arange(GRID_W)
    col_start = jnp.clip(col - NA_KW // 2, 0, GRID_W - NA_KW)
    col_ok = (col[None, :] >= col_start[:, None]) & (col[None, :] < col_start[:, None] + NA_KW)
    col_idx = jnp.clip(col[None, :] - col[:, None] + NA_KW - 1, 0, 2 * NA_KW - 2)
    rpb_col = rpb[:, :, col_idx]
    mask = jnp.tile(col_ok, (1, kh))

    def row_block(r):
        r0 = jnp.clip(r - kh // 2, 0, rows - kh)
        q_r = lax.dynamic_index_in_dim(qg, r, axis=1, keepdims=False)
        k_r = lax.dynamic_slice_in_dim(kg, r0, kh, axis=1).reshape(Bsz, n_loc, H, Dh)
        v_r = lax.dynamic_slice_in_dim(vg, r0, kh, axis=1).reshape(Bsz, n_loc, H, Dh)
        bias = jnp.take(rpb_col, r0 + jnp.arange(kh) - r + NA_KH - 1, axis=1)
        bias = jnp.transpose(bias, (0, 2, 1, 3)).reshape(H, GRID_W, n_loc).astype(jnp.float32)
        s_loc = jnp.einsum('bqhd,bkhd->bhqk', q_r, k_r).astype(jnp.float32) * scale + bias
        s_loc = jnp.where(mask, s_loc, -jnp.inf)
        s_ctx = jnp.einsum('bqhd,bkhd->bhqk', q_r, k_ctx).astype(jnp.float32) * scale
        p = jax.nn.softmax(jnp.concatenate([s_loc, s_ctx], axis=-1), axis=-1).astype(v.dtype)
        return (jnp.einsum('bhqk,bkhd->bqhd', p[..., :n_loc], v_r)
                + jnp.einsum('bhqk,bkhd->bqhd', p[..., n_loc:], v_ctx))

    out = lax.map(row_block, jnp.arange(rows))
    return jnp.moveaxis(out, 0, 1).reshape(Bsz, L, H * Dh)

def _context_attention(q, k, v):
    Bsz, T, H, Dh = q.shape
    s = jnp.einsum('bqhd,bkhd->bhqk', q, k).astype(jnp.float32) * Dh ** -0.5
    p = jax.nn.softmax(s, axis=-1).astype(v.dtype)
    return jnp.einsum('bhqk,bkhd->bqhd', p, v).reshape(Bsz, T, H * Dh)

def _dwconv(x, w, b):
    nch = x.shape[-1]
    out = lax.conv_general_dilated(x, w.astype(x.dtype)[:, None, :], window_strides=(1,),
                                   padding=[(SSD_CONV // 2, SSD_CONV // 2)],
                                   dimension_numbers=('NWC', 'WIO', 'NWC'),
                                   feature_group_count=nch)
    return out + b

def _ssd_prep(xbc, dt_raw, conv_w, conv_b, dtb_f, dtb_b):
    Bsz, L, _ = xbc.shape
    xbc = jax.nn.silu(_dwconv(xbc, conv_w, conv_b))
    xs, Bm, Cm = jnp.split(xbc, [SSD_WIDTH, SSD_WIDTH + SSD_GROUPS * SSD_STATE], axis=-1)
    xs = xs.reshape(Bsz, L, SSD_HEADS, SSD_HEAD_DIM)
    Bm = Bm.reshape(Bsz, L, SSD_GROUPS, SSD_STATE)
    Cm = Cm.reshape(Bsz, L, SSD_GROUPS, SSD_STATE)
    dt_f = jax.nn.softplus(dt_raw[..., :SSD_HEADS] + dtb_f)
    dt_b = jax.nn.softplus(dt_raw[..., SSD_HEADS:] + dtb_b)
    return xs, Bm, Cm, dt_f, dt_b

def _ssd_scan(xs, dt, A, Bm, Cm, h0, return_y):
    Bsz, L, H, P = xs.shape
    nc = L // SSD_CHUNK
    R = H // SSD_GROUPS
    x = (xs * dt[..., None]).reshape(Bsz, nc, SSD_CHUNK, SSD_GROUPS, R, P)
    a = (dt * A).astype(jnp.float32).reshape(Bsz, nc, SSD_CHUNK, SSD_GROUPS, R)
    a_cs = jnp.cumsum(jnp.moveaxis(a, 2, -1), axis=-1)
    Bc = Bm.reshape(Bsz, nc, SSD_CHUNK, SSD_GROUPS, SSD_STATE)
    decay_to_end = jnp.exp(a_cs[..., -1:] - a_cs).astype(xs.dtype)
    states = jnp.einsum('bclgn,bcgrl,bclgrp->bcgrpn', Bc, decay_to_end, x)
    chunk_decay = jnp.exp(a_cs[..., -1]).astype(xs.dtype)

    def step(h, inp):
        dec, st = inp
        return dec[..., None, None] * h + st, h

    h_last, h_prev = lax.scan(step, h0.reshape(Bsz, SSD_GROUPS, R, P, SSD_STATE),
                              (jnp.moveaxis(chunk_decay, 1, 0), jnp.moveaxis(states, 1, 0)))
    h_last = h_last.reshape(Bsz, H, P, SSD_STATE)
    if not return_y:
        return None, h_last
    Cc = Cm.reshape(Bsz, nc, SSD_CHUNK, SSD_GROUPS, SSD_STATE)
    lower = jnp.tril(jnp.ones((SSD_CHUNK, SSD_CHUNK), dtype=bool))
    seg = a_cs[..., :, None] - a_cs[..., None, :]
    Lm = jnp.exp(jnp.where(lower, seg, -jnp.inf)).astype(xs.dtype)
    cb = jnp.einsum('bclgn,bcsgn->bcgls', Cc, Bc)
    y_diag = jnp.einsum('bcgls,bcgrls,bcsgrp->bclgrp', cb, Lm, x)
    y_off = jnp.einsum('bclgn,bcgrpn,bcgrl->bclgrp', Cc, jnp.moveaxis(h_prev, 0, 1),
                       jnp.exp(a_cs).astype(xs.dtype))
    return (y_diag + y_off).reshape(Bsz, L, H, P), h_last

def _bidir_ssd(xs, Bm, Cm, dt_f, dt_b, A_f, A_b, d_skip, h0_f, h0_b, return_y):
    flip = lambda t: jnp.flip(t, axis=1)
    y_f, h_f = _ssd_scan(xs, dt_f, A_f, Bm, Cm, h0_f, return_y)
    y_b, h_b = _ssd_scan(flip(xs), flip(dt_b), A_b, flip(Bm), flip(Cm), h0_b, return_y)
    if not return_y:
        return None, h_f, h_b
    return y_f + flip(y_b) + d_skip[:, None] * xs, h_f, h_b

def _ssd_gated_norm(y, z, g):
    Bsz, L = y.shape[:2]
    u = (y.reshape(Bsz, L, SSD_WIDTH) * jax.nn.silu(z)).astype(jnp.float32)
    u = u.reshape(Bsz, L, SSD_GROUPS, SSD_WIDTH // SSD_GROUPS)
    u = u * lax.rsqrt(jnp.mean(u * u, axis=-1, keepdims=True) + NORM_EPS)
    return (u.reshape(Bsz, L, SSD_WIDTH) * g.astype(jnp.float32)).astype(y.dtype)

def _merge(o_na, y_ssd, gates, w_br_na, w_br_ssd, w_out):
    g_na, g_ssd = jnp.split(gates, 2, axis=-1)
    u = jax.nn.sigmoid(g_na) * (o_na @ w_br_na) + jax.nn.sigmoid(g_ssd) * (y_ssd @ w_br_ssd)
    return u @ w_out

def _token_mixer(h, hc, w_in, na_rpb, conv_w, conv_b, a_log_f, a_log_b, dtb_f, dtb_b, d_skip,
                 ssd_norm, w_br_na, w_br_ssd, w_out, update_ctx):
    Bsz, L, _ = h.shape
    q, k, v, z, xbc, dt_raw, gates = _split_in(h @ w_in)
    qc, kc, vc, zc, xbcc, dtc, gates_c = _split_in(hc @ w_in)
    pos = jnp.arange(L)
    rows, cols = pos // GRID_W, pos % GRID_W
    o_na = _neighbourhood_attention(_rope_2d(_heads(q), rows, cols), _rope_2d(_heads(k), rows, cols),
                                    _heads(v), _heads(kc), _heads(vc), na_rpb)
    A_f, A_b = -jnp.exp(a_log_f), -jnp.exp(a_log_b)
    h0 = jnp.zeros((Bsz, SSD_HEADS, SSD_HEAD_DIM, SSD_STATE), h.dtype)
    y_c, hf_c, hb_c = _bidir_ssd(*_ssd_prep(xbcc, dtc, conv_w, conv_b, dtb_f, dtb_b),
                                 A_f, A_b, d_skip, h0, h0, update_ctx)
    y, _, _ = _bidir_ssd(*_ssd_prep(xbc, dt_raw, conv_w, conv_b, dtb_f, dtb_b),
                         A_f, A_b, d_skip, hf_c, hb_c, True)
    mix = _merge(o_na, _ssd_gated_norm(y, z, ssd_norm), gates, w_br_na, w_br_ssd, w_out)
    if not update_ctx:
        return mix, None
    o_na_c = _context_attention(_heads(qc), _heads(kc), _heads(vc))
    mix_c = _merge(o_na_c, _ssd_gated_norm(y_c, zc, ssd_norm), gates_c, w_br_na, w_br_ssd, w_out)
    return mix, mix_c

def _ec_moe(h, w_router, w_eg, w_eu, w_ed):
    Bsz, T, _ = h.shape
    cap = EC_CAPACITY_FACTOR * T // N_EXPERTS
    aff = jax.nn.softmax((h @ w_router).astype(jnp.float32), axis=-1)
    gate, idx = lax.top_k(jnp.transpose(aff, (0, 2, 1)), cap)
    b_idx = jnp.arange(Bsz)[:, None, None]
    xg = h[b_idx, idx]
    hid = jax.nn.silu(jnp.einsum('becd,edf->becf', xg, w_eg)) * jnp.einsum('becd,edf->becf', xg, w_eu)
    yo = jnp.einsum('becf,efd->becd', hid, w_ed) * gate[..., None].astype(h.dtype)
    return jnp.zeros_like(h).at[b_idx, idx].add(yo)

def _layer(x, ctx, c, c_ctx, w_ada, b_ada, n_pre_mix, n_post_mix, n_pre_ffn, n_post_ffn, w_in, na_rpb,
           conv_w, conv_b, a_log_f, a_log_b, dtb_f, dtb_b, d_skip, ssd_norm, w_br_na, w_br_ssd, w_out,
           w_router, w_eg, w_eu, w_ed, update_ctx):
    sh1, sc1, ga1, sh2, sc2, ga2 = _ada(c[:, None, :], w_ada, b_ada)
    csh1, csc1, cga1, csh2, csc2, cga2 = _ada(c_ctx, w_ada, b_ada)
    mix, mix_c = _token_mixer(_modulate(x, n_pre_mix, sh1, sc1), _modulate(ctx, n_pre_mix, csh1, csc1),
                              w_in, na_rpb, conv_w, conv_b, a_log_f, a_log_b, dtb_f, dtb_b, d_skip,
                              ssd_norm, w_br_na, w_br_ssd, w_out, update_ctx)
    x = x + ga1 * _rmsnorm(mix, n_post_mix)
    x = x + ga2 * _rmsnorm(_ec_moe(_modulate(x, n_pre_ffn, sh2, sc2), w_router, w_eg, w_eu, w_ed), n_post_ffn)
    if update_ctx:
        ctx = ctx + cga1 * _rmsnorm(mix_c, n_post_mix)
        ctx = ctx + cga2 * _rmsnorm(_ec_moe(_modulate(ctx, n_pre_ffn, csh2, csc2), w_router, w_eg, w_eu, w_ed),
                                    n_post_ffn)
    return x, ctx

def first_inputs(seed: int = 0) -> dict:
    key = jax.random.key(seed)
    ks = jax.random.split(key, 26)
    f32 = jnp.float32

    def nrm(k, shape, s):
        return jax.random.normal(k, shape, f32) * s

    dt0 = jnp.exp(jax.random.uniform(ks[14], (DEPTH, 2, SSD_HEADS), f32, math.log(1e-3), math.log(1e-1)))
    dt_bias = dt0 + jnp.log(-jnp.expm1(-dt0))
    a_log = jnp.log(jax.random.uniform(ks[15], (DEPTH, 2, SSD_HEADS), f32, 1.0, 16.0))
    return {
        'x': nrm(ks[0], (BATCH, SEQ, D_MODEL), 1.0),
        'c': nrm(ks[1], (BATCH, D_MODEL), 1.0),
        'ctx': nrm(ks[2], (BATCH, CTX_LEN, D_MODEL), 1.0),
        'c_ctx': nrm(ks[3], (D_MODEL,), 1.0),
        'w_ada': nrm(ks[4], (DEPTH, D_MODEL, N_MOD * D_MODEL), 0.5 * D_MODEL ** -0.5),
        'b_ada': nrm(ks[5], (DEPTH, N_MOD * D_MODEL), 0.02),
        'norm_pre_mix': 1.0 + nrm(ks[6], (DEPTH, D_MODEL), 0.02),
        'norm_post_mix': 1.0 + nrm(ks[7], (DEPTH, D_MODEL), 0.02),
        'norm_pre_ffn': 1.0 + nrm(ks[8], (DEPTH, D_MODEL), 0.02),
        'norm_post_ffn': 1.0 + nrm(ks[9], (DEPTH, D_MODEL), 0.02),
        'w_in': nrm(ks[10], (DEPTH, D_MODEL, IN_COLS), D_MODEL ** -0.5),
        'na_rpb': nrm(ks[11], (DEPTH, NA_HEADS, 2 * NA_KH - 1, 2 * NA_KW - 1), 0.1),
        'ssd_conv_w': nrm(ks[12], (DEPTH, SSD_CONV, SSD_XBC), SSD_CONV ** -0.5),
        'ssd_conv_b': nrm(ks[13], (DEPTH, SSD_XBC), 0.02),
        'ssd_a_log_fwd': a_log[:, 0],
        'ssd_a_log_bwd': a_log[:, 1],
        'ssd_dt_bias_fwd': dt_bias[:, 0],
        'ssd_dt_bias_bwd': dt_bias[:, 1],
        'ssd_d_skip': 1.0 + nrm(ks[16], (DEPTH, SSD_HEADS), 0.02),
        'ssd_norm': 1.0 + nrm(ks[17], (DEPTH, SSD_WIDTH), 0.02),
        'w_branch_na': nrm(ks[18], (DEPTH, NA_WIDTH, D_MODEL), NA_WIDTH ** -0.5),
        'w_branch_ssd': nrm(ks[19], (DEPTH, SSD_WIDTH, D_MODEL), SSD_WIDTH ** -0.5),
        'w_out': nrm(ks[20], (DEPTH, D_MODEL, D_MODEL), D_MODEL ** -0.5),
        'w_router': nrm(ks[21], (DEPTH, D_MODEL, N_EXPERTS), D_MODEL ** -0.5),
        'w_exp_gate': nrm(ks[22], (DEPTH, N_EXPERTS, D_MODEL, EXPERT_FF), D_MODEL ** -0.5),
        'w_exp_up': nrm(ks[23], (DEPTH, N_EXPERTS, D_MODEL, EXPERT_FF), D_MODEL ** -0.5),
        'w_exp_down': nrm(ks[24], (DEPTH, N_EXPERTS, EXPERT_FF, D_MODEL), EXPERT_FF ** -0.5),
    }

def first_block(x, c, ctx, c_ctx, w_ada, b_ada, norm_pre_mix, norm_post_mix, norm_pre_ffn, norm_post_ffn,
              w_in, na_rpb, ssd_conv_w, ssd_conv_b, ssd_a_log_fwd, ssd_a_log_bwd, ssd_dt_bias_fwd,
              ssd_dt_bias_bwd, ssd_d_skip, ssd_norm, w_branch_na, w_branch_ssd, w_out, w_router,
              w_exp_gate, w_exp_up, w_exp_down):
    for i in range(DEPTH):
        x, ctx = _layer(x, ctx, c, c_ctx, w_ada[i], b_ada[i], norm_pre_mix[i], norm_post_mix[i],
                        norm_pre_ffn[i], norm_post_ffn[i], w_in[i], na_rpb[i], ssd_conv_w[i], ssd_conv_b[i],
                        ssd_a_log_fwd[i], ssd_a_log_bwd[i], ssd_dt_bias_fwd[i], ssd_dt_bias_bwd[i],
                        ssd_d_skip[i], ssd_norm[i], w_branch_na[i], w_branch_ssd[i], w_out[i], w_router[i],
                        w_exp_gate[i], w_exp_up[i], w_exp_down[i], i < DEPTH - 1)
    return x


DEPTH_2 = 2

HEAD_DIM = 64
A_HEADS = 4
A_VDIM = 2 * HEAD_DIM
B_HEADS = 8
B_BRANCHES = ((128, 1), (512, 4), (2048, 16))
B_BLOCK = 128
C_HEADS = 16
C_Q_RANK = 384
C_KV_RANK = 256
C_NOPE = 64
C_ROPE = 32
C_VDIM = 64
C_SCALE = (C_NOPE + C_ROPE) ** -0.5
IDX_HEADS = 8
IDX_DIM = 64
IDX_ROPE = 32
TOPK_MAX = 256
Q_BLOCK = 128
D_FF = 4 * D_MODEL
PLE_DIM = 256
ROPE_THETA = 10000.0
EPS = 1e-6
N_EVEN = (DEPTH_2 + 1) // 2
N_ODD = DEPTH_2 // 2
AB_SPLITS = (A_HEADS * 2 * HEAD_DIM, A_HEADS * 2 * HEAD_DIM, A_HEADS * A_VDIM,
             B_HEADS * HEAD_DIM, B_HEADS * HEAD_DIM, B_HEADS * HEAD_DIM)
AB_IN = sum(AB_SPLITS)
AB_OUT = A_HEADS * A_VDIM + B_HEADS * HEAD_DIM
C_SPLITS = (C_Q_RANK, C_KV_RANK, C_ROPE, IDX_DIM, IDX_HEADS)
C_IN = sum(C_SPLITS)
C_OUT = C_HEADS * C_VDIM


F32 = jnp.float32

def rms(x, g):
    xf = x.astype(F32)
    y = xf * lax.rsqrt(jnp.mean(xf * xf, axis=-1, keepdims=True) + EPS) * g.astype(F32)
    return y.astype(x.dtype)

def rope(x, pos):
    half = x.shape[-1] // 2
    inv = ROPE_THETA ** (-jnp.arange(half, dtype=F32) / half)
    ang = pos.astype(F32)[:, None] * inv[None, :]
    cos = jnp.cos(ang)[:, None, :]
    sin = jnp.sin(ang)[:, None, :]
    x1 = x[..., :half].astype(F32)
    x2 = x[..., half:].astype(F32)
    return jnp.concatenate([x1 * cos - x2 * sin, x1 * sin + x2 * cos], axis=-1).astype(x.dtype)

def split_cols(t, sizes):
    offs = np.cumsum(sizes)[:-1].tolist()
    return jnp.split(t, offs, axis=-1)

def diff_attention(q, k, v, lam):
    S = q.shape[3]
    scale = HEAD_DIM ** -0.5
    outs = []
    for start in range(0, S, Q_BLOCK):
        end = start + Q_BLOCK
        s = jnp.einsum('bhmqd,bhmkd->bhmqk', q[:, :, :, start:end], k[:, :, :, :end]).astype(F32) * scale
        causal = jnp.arange(start, end)[:, None] >= jnp.arange(end)[None, :]
        pr = jax.nn.softmax(jnp.where(causal, s, -jnp.inf), axis=-1)
        a = pr[:, :, 0] - lam * pr[:, :, 1]
        outs.append(jnp.einsum('bhqk,bhkd->bhqd', a.astype(v.dtype), v[:, :, :end]))
    return jnp.concatenate(outs, axis=2)

def dilated_branch(q, k, v, window, dilation):
    Bn, H, S, dh = q.shape
    steps = window // dilation
    L = S // dilation
    nb = -(-L // B_BLOCK)
    Lp = nb * B_BLOCK

    def strided(t):
        t = t.reshape(Bn, H, L, dilation, dh).transpose(0, 1, 3, 2, 4)
        t = jnp.pad(t, ((0, 0), (0, 0), (0, 0), (0, Lp - L), (0, 0)))
        return t.reshape(Bn, H, dilation, nb, B_BLOCK, dh)

    def with_prev(t):
        prev = jnp.pad(t, ((0, 0), (0, 0), (0, 0), (1, 0), (0, 0), (0, 0)))[:, :, :, :-1]
        return jnp.concatenate([prev, t], axis=-2)

    qb = strided(q)
    kk = with_prev(strided(k))
    vv = with_prev(strided(v))
    s = jnp.einsum('bhcnqd,bhcnkd->bhcnqk', qb, kk).astype(F32) * dh ** -0.5
    ki = jnp.arange(2 * B_BLOCK)[None, :]
    dist = (jnp.arange(B_BLOCK)[:, None] + B_BLOCK) - ki
    blk = jnp.arange(nb)[:, None, None]
    ok = (dist >= 0) & (dist <= steps) & ((blk > 0) | (ki >= B_BLOCK))
    s = jnp.where(ok, s, -jnp.inf)
    lse = jax.nn.logsumexp(s, axis=-1)
    pr = jnp.exp(s - lse[..., None])
    o = jnp.einsum('bhcnqk,bhcnkd->bhcnqd', pr.astype(v.dtype), vv)
    o = o.reshape(Bn, H, dilation, Lp, dh)[:, :, :, :L].transpose(0, 1, 3, 2, 4).reshape(Bn, H, S, dh)
    lse = lse.reshape(Bn, H, dilation, Lp)[..., :L].transpose(0, 1, 3, 2).reshape(Bn, H, S)
    return o, lse

def dilated_attention(q, k, v):
    res = [dilated_branch(q, k, v, w, d) for (w, d) in B_BRANCHES]
    outs = jnp.stack([r[0] for r in res]).astype(F32)
    lses = jnp.stack([r[1] for r in res])
    wts = jax.nn.softmax(lses, axis=0)
    return jnp.einsum('gbhs,gbhsd->bhsd', wts, outs)

def mixer_ab(h, pos, w_in, w_out, lq1, lk1, lq2, lk2, g_sub, lam_init):
    Bn, S, _ = h.shape
    aq, ak, av, bq, bk, bv = split_cols(h @ w_in, AB_SPLITS)
    def a_qk(t):
        t = rope(t.reshape(Bn, S, A_HEADS * 2, HEAD_DIM), pos)
        return t.reshape(Bn, S, A_HEADS, 2, HEAD_DIM).transpose(0, 2, 3, 1, 4)
    av = av.reshape(Bn, S, A_HEADS, A_VDIM).transpose(0, 2, 1, 3)
    lam = (jnp.exp(jnp.sum(lq1.astype(F32) * lk1.astype(F32)))
           - jnp.exp(jnp.sum(lq2.astype(F32) * lk2.astype(F32))) + lam_init)
    ao = diff_attention(a_qk(aq), a_qk(ak), av, lam)
    ao = rms(ao, g_sub) * (1.0 - lam_init)
    ao = ao.transpose(0, 2, 1, 3).reshape(Bn, S, A_HEADS * A_VDIM)
    def b_heads(t, rot):
        t = t.reshape(Bn, S, B_HEADS, HEAD_DIM)
        t = rope(t, pos) if rot else t
        return t.transpose(0, 2, 1, 3)
    bo = dilated_attention(b_heads(bq, True), b_heads(bk, True), b_heads(bv, False))
    bo = bo.transpose(0, 2, 1, 3).reshape(Bn, S, B_HEADS * HEAD_DIM).astype(h.dtype)
    return jnp.concatenate([ao.astype(h.dtype), bo], axis=-1) @ w_out

def partial_rope(t, pos):
    return jnp.concatenate([rope(t[..., :IDX_ROPE], pos), t[..., IDX_ROPE:]], axis=-1)

def mixer_c(h, pos, w_in, g_cq, g_ckv, w_uq, w_qi, w_uk, w_uv, w_out):
    Bn, S, _ = h.shape
    cq, ckv, krope, kidx, widx = split_cols(h @ w_in, C_SPLITS)
    cq = rms(cq, g_cq)
    ckv = rms(ckv, g_ckv)
    q = (cq @ w_uq).reshape(Bn, S, C_HEADS, C_NOPE + C_ROPE)
    q_lat = jnp.einsum('bshd,chd->bshc', q[..., :C_NOPE], w_uk)
    q_full = jnp.concatenate([q_lat, rope(q[..., C_NOPE:], pos)], axis=-1)
    k_rope = rope(krope[:, :, None, :], pos)[:, :, 0]
    kv = jnp.concatenate([ckv, k_rope], axis=-1)
    qi = partial_rope((cq @ w_qi).reshape(Bn, S, IDX_HEADS, IDX_DIM), pos)
    ki = partial_rope(kidx[:, :, None, :], pos)[:, :, 0]
    wi = widx.astype(F32) * IDX_HEADS ** -0.5
    k_sel = min(TOPK_MAX, S // 4)
    nb = S // Q_BLOCK

    def blocks(t):
        return t.reshape((Bn, nb, Q_BLOCK) + t.shape[2:]).swapaxes(0, 1)

    def one_block(args):
        qf, qib, wib, start = args
        tq = start + jnp.arange(Q_BLOCK)
        dots = jnp.einsum('bqhd,bsd->bqhs', qib, ki).astype(F32)
        score = jnp.einsum('bqh,bqhs->bqs', wib, jax.nn.relu(dots)) * IDX_DIM ** -0.5
        causal = jnp.arange(S)[None, :] <= tq[:, None]
        score = jnp.where(causal, score, -jnp.inf)
        _, idx = lax.top_k(score, k_sel)
        valid = idx <= tq[None, :, None]
        sel = jax.vmap(lambda kvb, ib: kvb[ib])(kv, idx)
        s = jnp.einsum('bqhc,bqkc->bqhk', qf, sel).astype(F32) * C_SCALE
        pr = jax.nn.softmax(jnp.where(valid[:, :, None, :], s, -jnp.inf), axis=-1)
        o_lat = jnp.einsum('bqhk,bqkc->bqhc', pr.astype(sel.dtype), sel[..., :C_KV_RANK])
        return jnp.einsum('bqhc,chd->bqhd', o_lat, w_uv)

    o = lax.map(one_block, (blocks(q_full), blocks(qi), blocks(wi), jnp.arange(nb) * Q_BLOCK))
    o = o.swapaxes(0, 1).reshape(Bn, S, C_OUT)
    return o @ w_out

def second_inputs(seed: int = 0) -> dict:
    key = jax.random.key(seed)
    ks = iter(jax.random.split(key, 32))

    def nrm(shape, fan_in):
        return jax.random.normal(next(ks), shape, F32) * fan_in ** -0.5

    def gain(shape):
        return 1.0 + 0.02 * jax.random.normal(next(ks), shape, F32)

    def small(shape):
        return 0.1 * jax.random.normal(next(ks), shape, F32)

    return {
        "x": jax.random.normal(next(ks), (BATCH, SEQ, D_MODEL), F32),
        "p": jax.random.normal(next(ks), (DEPTH_2, BATCH, SEQ, PLE_DIM), F32),
        "g_mix_pre": gain((DEPTH_2, D_MODEL)),
        "g_mix_post": gain((DEPTH_2, D_MODEL)),
        "g_mlp_pre": gain((DEPTH_2, D_MODEL)),
        "g_mlp_post": gain((DEPTH_2, D_MODEL)),
        "w_mlp_in": nrm((DEPTH_2, D_MODEL, D_FF), D_MODEL),
        "w_mlp_out": nrm((DEPTH_2, D_FF, D_MODEL), D_FF),
        "w_ple_proj": nrm((DEPTH_2, PLE_DIM, D_MODEL), PLE_DIM),
        "w_ple_gate": nrm((DEPTH_2, D_MODEL, D_MODEL), D_MODEL),
        "w_in_ab": nrm((N_EVEN, D_MODEL, AB_IN), D_MODEL),
        "w_out_ab": nrm((N_EVEN, AB_OUT, D_MODEL), AB_OUT),
        "diff_lq1": small((N_EVEN, HEAD_DIM)),
        "diff_lk1": small((N_EVEN, HEAD_DIM)),
        "diff_lq2": small((N_EVEN, HEAD_DIM)),
        "diff_lk2": small((N_EVEN, HEAD_DIM)),
        "g_diff_sub": gain((N_EVEN, A_VDIM)),
        "w_in_c": nrm((N_ODD, D_MODEL, C_IN), D_MODEL),
        "g_cq": gain((N_ODD, C_Q_RANK)),
        "g_ckv": gain((N_ODD, C_KV_RANK)),
        "w_uq": nrm((N_ODD, C_Q_RANK, C_HEADS * (C_NOPE + C_ROPE)), C_Q_RANK),
        "w_qi": nrm((N_ODD, C_Q_RANK, IDX_HEADS * IDX_DIM), C_Q_RANK),
        "w_uk": nrm((N_ODD, C_KV_RANK, C_HEADS, C_NOPE), C_KV_RANK),
        "w_uv": nrm((N_ODD, C_KV_RANK, C_HEADS, C_VDIM), C_KV_RANK),
        "w_out_c": nrm((N_ODD, C_OUT, D_MODEL), C_OUT),
    }

def second_block(x, p, g_mix_pre, g_mix_post, g_mlp_pre, g_mlp_post, w_mlp_in, w_mlp_out,
              w_ple_proj, w_ple_gate, w_in_ab, w_out_ab, diff_lq1, diff_lk1, diff_lq2,
              diff_lk2, g_diff_sub, w_in_c, g_cq, g_ckv, w_uq, w_qi, w_uk, w_uv, w_out_c):
    S = x.shape[1]
    pos = jnp.arange(S)
    h = x
    for i in range(DEPTH_2):
        hn = rms(h, g_mix_pre[i])
        j = i // 2
        if i % 2 == 0:
            lam_init = 0.8 - 0.6 * math.exp(-0.3 * i)
            y = mixer_ab(hn, pos, w_in_ab[j], w_out_ab[j], diff_lq1[j], diff_lk1[j],
                         diff_lq2[j], diff_lk2[j], g_diff_sub[j], lam_init)
        else:
            y = mixer_c(hn, pos, w_in_c[j], g_cq[j], g_ckv[j], w_uq[j], w_qi[j],
                        w_uk[j], w_uv[j], w_out_c[j])
        h = h + rms(y, g_mix_post[i])
        hn = rms(h, g_mlp_pre[i])
        y = jnp.square(jax.nn.relu(hn @ w_mlp_in[i])) @ w_mlp_out[i]
        h = h + rms(y, g_mlp_post[i])
        gate = jax.nn.sigmoid(h @ w_ple_gate[i])
        h = h + gate * (p[i] @ w_ple_proj[i])
    return h


def setup_inputs(seed=0):
    out = dict(first_inputs(seed))
    for name, value in second_inputs(seed + 1).items():
        if name != "x":
            out[name + "_2"] = value
    return out


def reference(
    x, c, ctx, c_ctx, w_ada, b_ada, norm_pre_mix, norm_post_mix, norm_pre_ffn, norm_post_ffn,
    w_in, na_rpb, ssd_conv_w, ssd_conv_b, ssd_a_log_fwd, ssd_a_log_bwd, ssd_dt_bias_fwd,
    ssd_dt_bias_bwd, ssd_d_skip, ssd_norm, w_branch_na, w_branch_ssd, w_out, w_router,
    w_exp_gate, w_exp_up, w_exp_down, p_2, g_mix_pre_2, g_mix_post_2, g_mlp_pre_2, g_mlp_post_2,
    w_mlp_in_2, w_mlp_out_2, w_ple_proj_2, w_ple_gate_2, w_in_ab_2, w_out_ab_2, diff_lq1_2,
    diff_lk1_2, diff_lq2_2, diff_lk2_2, g_diff_sub_2, w_in_c_2, g_cq_2, g_ckv_2, w_uq_2, w_qi_2,
    w_uk_2, w_uv_2, w_out_c_2,
):
    x = first_block(
        x, c, ctx, c_ctx, w_ada, b_ada, norm_pre_mix, norm_post_mix, norm_pre_ffn,
        norm_post_ffn, w_in, na_rpb, ssd_conv_w, ssd_conv_b, ssd_a_log_fwd, ssd_a_log_bwd,
        ssd_dt_bias_fwd, ssd_dt_bias_bwd, ssd_d_skip, ssd_norm, w_branch_na, w_branch_ssd,
        w_out, w_router, w_exp_gate, w_exp_up, w_exp_down,
    )
    return second_block(
        x, p_2, g_mix_pre_2, g_mix_post_2, g_mlp_pre_2, g_mlp_post_2, w_mlp_in_2, w_mlp_out_2,
        w_ple_proj_2, w_ple_gate_2, w_in_ab_2, w_out_ab_2, diff_lq1_2, diff_lk1_2, diff_lq2_2,
        diff_lk2_2, g_diff_sub_2, w_in_c_2, g_cq_2, g_ckv_2, w_uq_2, w_qi_2, w_uk_2, w_uv_2,
        w_out_c_2,
    )


_drawn_inputs = setup_inputs


def setup_inputs(seed=0):
    import zlib

    import numpy as np

    out = dict(_drawn_inputs(seed))
    spreads = {}
    factors = {'norm_post_ffn': 3.268,
     'na_rpb': 7.136,
     'ssd_d_skip': 4.442,
     'g_cq_2': 2.743,
     'g_ckv_2': 5.435}
    for name, (base, spread) in spreads.items():
        noise = np.random.default_rng([zlib.crc32(name.encode()), seed]).standard_normal(out[name].shape)
        drawn = base * np.exp(spread * noise) if base else spread * noise
        out[name] = jnp.asarray(drawn.astype(out[name].dtype))
    for name, factor in factors.items():
        out[name] = (out[name] * factor).astype(out[name].dtype)
    return out
```

```python
from contextlib import ExitStack

import numpy as np
import concourse.bass as bass
from concourse import mybir

F32 = mybir.dt.float32
BF16 = mybir.dt.bfloat16
ALU = mybir.AluOpType
ACT = mybir.ActivationFunctionType
AX = mybir.AxisListType

P = 128
L = 256
TT = L // P
D = 1024
KT = D // P
EPS = 1e-6
NEG = -1e30
HD = 64
SLOTS = 4
SLOT = 4096
WORK = 27392

NA_HEADS, GRID_W, NA_KH, NA_KW = 16, 64, 8, 16
SSD_W, SSD_HEADS, SSD_G, SSD_N, CONV = 2048, 32, 4, 128, 5
GB = SSD_W // SSD_G // P
GH = SSD_HEADS // SSD_G
NE, FF, CAP = 16, 2048, 32
A_HEADS, B_HEADS = 4, 8
C_HEADS, CQ, CKV, CROPE, CNOPE = 16, 384, 256, 32, 64
IDX_HEADS, TOPK = 8, 64
C_SCALE = (CNOPE + CROPE) ** -0.5
DFF = 4096
LAM_INIT = 0.2

PCOL = {}
_at = 0
for _name, _n in (("b_ada", 48), ("pre_mix", 8), ("post_mix", 8), ("pre_ffn", 8), ("post_ffn", 8),
                  ("conv_w", 24 * CONV), ("conv_b", 24), ("ssd_norm", 16), ("d_skip", 16),
                  ("mix_pre2", 16), ("mlp_pre2", 16), ("cq", 3), ("ckv", 2), ("sub", 1)):
    PCOL[_name] = _at
    _at += _n
NPCOL = _at

CST = ["ident", "ones", "le", "ge", "gt", "lt", "swap16", "swap32", "mask_f", "mask_b"]
NCST = len(CST) * P + CAP
TAB = ["na_qc", "na_qs", "na_kc", "na_ks", "ab_qc", "ab_qs", "ab_kc", "ab_ks",
       "cr_c", "cr_s", "ci_c", "ci_s"]


def constants():
    f = np.float32
    i = np.arange(P)
    r, c = i[:, None], i[None, :]
    one = lambda m: m.astype(f)
    mats = {
        "ident": one(r == c), "ones": np.ones((P, P), f), "le": one(r <= c), "ge": one(r >= c),
        "gt": one(r > c), "lt": one(r < c), "swap16": one(r == (c ^ 16)), "swap32": one(r == (c ^ 32)),
        "mask_f": np.where(c >= r, 0, NEG).astype(f), "mask_b": np.where(c <= r, 0, NEG).astype(f),
    }
    cst = np.concatenate([mats[m] for m in CST] + [np.tile(np.arange(1, CAP + 1, dtype=f), (P, 1))], 1)
    tok = np.arange(L)

    def angles(pos, half):
        inv = (f(10000.0) ** (-np.arange(half, dtype=f) / f(half))).astype(f)
        a = pos.astype(f)[:, None] * inv[None, :]
        return np.cos(a).astype(f), np.sin(a).astype(f)

    def table(pos_of, half, width, rope_width):
        cs, sn = np.ones((P, L), f), np.zeros((P, L), f)
        for p in range(P):
            d = p % width
            if d < rope_width:
                cc, ss = angles(pos_of(d), half)
                j = d % (2 * half)
                cs[p] = cc[:, j % half]
                sn[p] = ss[:, j % half] * (-1 if j < half else 1)
        return cs, sn

    na = table(lambda d: tok // GRID_W if d < 32 else tok % GRID_W, 16, 64, 64)
    ab = table(lambda d: tok, 32, 64, 64)
    cr = table(lambda d: tok, 16, 32, 32)
    ci = table(lambda d: tok, 16, 64, 32)
    s = f(HD ** -0.5)
    tab = np.stack([na[0] * s, na[1] * s, na[0], na[1], ab[0] * s, ab[1] * s, ab[0], ab[1],
                    cr[0], cr[1], ci[0], ci[1]], 1)
    cc, ss = angles(tok, 16)
    tokt = np.stack([np.concatenate([cc] * 4, 1), np.concatenate([-ss, ss] * 2, 1)], 1)
    tokt = tokt.reshape(TT, P, 2, 64).transpose(1, 0, 2, 3)
    q, k = tok[:, None], tok[None, :]
    causal = q >= k
    count = ((causal & (q - k <= 128)).astype(int) + (causal & ((q - k) % 4 == 0))
             + (causal & ((q - k) % 16 == 0)))
    cmask = np.where(causal, 0, NEG)
    wmask = np.where(count > 0, np.log(np.maximum(count, 1)), NEG)
    masks = np.stack([np.concatenate([m[:P, :P], m[P:, :]], 1) for m in (cmask, wmask)], 1).astype(f)
    return {"cst": cst, "tab": np.ascontiguousarray(tab.astype(f)), "tokt": np.ascontiguousarray(tokt),
            "masks": np.ascontiguousarray(masks)}


def layouts(v):
    a = {k: np.asarray(x) for k, x in v.items()}
    f = np.float32
    out = constants()
    col = lambda x: np.ascontiguousarray(x.reshape(-1, P).T)
    out["x"], out["ctx"] = a["x"][0], a["ctx"][0]
    out["cc"] = np.stack([col(a["c"][0]), col(a["c_ctx"])], 2)
    gb = SSD_W // SSD_G
    order = np.concatenate([np.concatenate([np.arange(g * gb, (g + 1) * gb),
                                            SSD_W + np.arange(g * SSD_N, (g + 1) * SSD_N),
                                            SSD_W + SSD_G * SSD_N + np.arange(g * SSD_N, (g + 1) * SSD_N)])
                            for g in range(SSD_G)])
    cw = a["ssd_conv_w"][0][:, order]
    pc = [col(a["b_ada"][0])] + [col(a["norm_" + n][0]) for n in ("pre_mix", "post_mix", "pre_ffn", "post_ffn")]
    pc += [cw.reshape(CONV, -1, P).transpose(2, 1, 0).reshape(P, -1), col(a["ssd_conv_b"][0][order])]
    pc += [col(a["ssd_norm"][0]), col(np.repeat(a["ssd_d_skip"][0], HD))]
    pc += [col(a["g_mix_pre_2"].ravel()), col(a["g_mlp_pre_2"].ravel()), col(a["g_cq_2"][0]),
           col(a["g_ckv_2"][0]), col(a["g_diff_sub_2"][0])]
    out["pcol"] = np.ascontiguousarray(np.concatenate(pc, 1))
    out["heads"] = np.concatenate([a[n][0] for n in ("ssd_a_log_fwd", "ssd_a_log_bwd", "ssd_dt_bias_fwd",
                                                     "ssd_dt_bias_bwd", "diff_lq1_2", "diff_lk1_2",
                                                     "diff_lq2_2", "diff_lk2_2")])[None, :]
    out["g_post"] = np.stack([a["g_mix_post_2"][0], a["g_mlp_post_2"][0],
                              a["g_mix_post_2"][1], a["g_mlp_post_2"][1]])
    tok = np.arange(L)
    r, w = tok // GRID_W, tok % GRID_W
    start = np.clip(w - NA_KW // 2, 0, GRID_W - NA_KW)
    ok = (w[None, :] >= start[:, None]) & (w[None, :] < start[:, None] + NA_KW)
    dr = r[None, :] - r[:, None] + NA_KH - 1
    dc = np.clip(w[None, :] - w[:, None] + NA_KW - 1, 0, 2 * NA_KW - 2)
    bias = np.where(ok[None], a["na_rpb"][0][:, dr, dc], f(NEG)).astype(f)
    out["na_bias"] = np.ascontiguousarray(bias.reshape(NA_HEADS, TT, P, L).transpose(0, 2, 1, 3))
    out["w_ada"], out["w_in"] = a["w_ada"][0], a["w_in"][0]
    out["w_na"], out["w_ssd"], out["w_out"] = a["w_branch_na"][0], a["w_branch_ssd"][0], a["w_out"][0]
    out["w_router"] = a["w_router"][0]
    for n in ("gate", "up", "down"):
        out["w_e" + n] = a["w_exp_" + n][0]
    out["pT"] = np.ascontiguousarray(a["p_2"][:, 0].transpose(0, 2, 1))
    for n in ("mlp_in", "mlp_out", "ple_proj", "ple_gate"):
        out["w_" + n] = a["w_" + n + "_2"]
    out["w_ab"], out["w_oab"] = a["w_in_ab_2"][0], a["w_out_ab_2"][0]
    out["w_c"], out["w_oc"] = a["w_in_c_2"][0], a["w_out_c_2"][0]
    uq = a["w_uq_2"][0].reshape(CQ, C_HEADS, CNOPE + CROPE)
    out["w_uqn"] = np.ascontiguousarray(uq[:, :, :CNOPE].reshape(CQ, -1))
    out["w_uqr"] = np.ascontiguousarray(uq[:, :, CNOPE:].reshape(CQ, -1))
    out["w_qi"] = a["w_qi_2"][0]
    out["w_ukT"] = np.ascontiguousarray(a["w_uk_2"][0].transpose(1, 2, 0).reshape(D, CKV))
    out["w_uv"] = a["w_uv_2"][0].reshape(CKV, -1)
    return {k: np.ascontiguousarray(x) for k, x in out.items()}


def build(nc, d, out):
    es = ExitStack()
    with es:
        def sb(name, shape, dt=F32):
            return es.enter_context(nc.sbuf_tensor(name, shape, dt))

        def sem(name):
            return es.enter_context(nc.semaphore(name))

        ring = sb("ring", [P, SLOTS, SLOT])
        work = sb("work", [P, WORK])
        xres = sb("xres", [P, TT, D])
        cst = sb("cst", [P, NCST])
        tab = sb("tab", [P, 4, L])
        tokt = sb("tokt", [P, TT, 2, 64])
        masks = sb("masks", [P, 2, 3 * P])
        pcol = sb("pcol", [P, NPCOL])
        heads = sb("heads", [P, 128 + 4 * HD])
        router = sb("router", [P, KT, NE])
        bfc = sb("bfc", [P, 3, P], BF16)
        mod = sb("mod", [P, 48])
        modc = sb("modc", [P, 16])
        mul1 = sb("mul1", [P, 2, KT])
        mul2 = sb("mul2", [P, KT])
        gain = sb("gain", [P, 2, KT])
        grow = sb("grow", [P, D])
        lam = sb("lam", [P, 8])
        small = sb("small", [P, 64])
        epsc = sb("epsc", [P, 1])
        bank = [es.enter_context(nc.psum_tensor(f"bank{i}", [P, 512], F32)) for i in range(8)]

        def cm(name):
            i = CST.index(name) * P
            return cst[:, i:i + P]

        def tb(name):
            return tab[:, TAB.index(name) % 4, :]

        def pc(name, i, n=1):
            return pcol[:, PCOL[name] + i:PCOL[name] + i + n]

        ident, ones = cm("ident"), cm("ones")
        numbers = cst[:, len(CST) * P:NCST]

        class Region:

            def __init__(self, at=0):
                self.at = at

            def take(self, *dims):
                n = int(np.prod(dims))
                v = work[:, self.at:self.at + n]
                self.at += n
                assert self.at <= WORK, self.at
                if len(dims) == 1:
                    return v
                names = "abcde"[:len(dims)]
                return v.rearrange(f"p ({' '.join(names)}) -> p {' '.join(names)}", **dict(zip(names, dims)))

        consts_in = sem("consts_in")
        x_in = sem("x_in")
        slot_full = [sem(f"slot_full{i}") for i in range(SLOTS)]
        chunk_used = sem("chunk_used")
        stage_end = sem("stage_end")
        bfc_ready = sem("bfc_ready")
        eps_ready = sem("eps_ready")
        gemm_ready, gemm_freed = sem("gemm_ready"), sem("gemm_freed")
        rows_ready = sem("rows_ready")
        dve_step, act_step, pool_step = sem("dve_step"), sem("act_step"), sem("pool_step")
        grow_in, grow_loaded = sem("grow_in"), sem("grow_loaded")
        sT_ready, ada_ready, ada_copied, ada_cols, ada_done = (sem(n) for n in (
            "sT_ready", "ada_ready", "ada_copied", "ada_cols", "ada_done"))
        pads_ready = sem("pads_ready")
        gdiag_ready, grow_ready = sem("gdiag_ready"), sem("grow_ready")
        sq_done, std_done, xn_done, tr_ready, tr_freed = (sem(n) for n in (
            "sq_done", "std_done", "xn_done", "tr_ready", "tr_freed"))
        post_sq, post_sum, post_std, post_done = (sem(n) for n in ("post_sq", "post_sum", "post_std", "post_done"))
        raw_ready, swap_ready, swap_freed, rope_done = (sem(n) for n in (
            "raw_ready", "swap_ready", "swap_freed", "rope_done"))
        bias_in = [sem(f"bias_in{i}") for i in range(3)]
        att_scores, att_biased, att_exp, att_probs, att_turned, att_copied, att_out, att_stored = (sem(n) for n in (
            "att_scores", "att_biased", "att_exp", "att_probs", "att_turned", "att_copied", "att_out", "att_stored"))

        ql_ready, uv_ready = sem("ql_ready"), sem("uv_ready")
        counts = {}

        def stepper(eng, s):
            def link(ins):
                counts[id(s)] = counts.get(id(s), 0) + 1
                ins.then_inc(s, 1)
                eng.wait_ge(s, counts[id(s)])
            return link

        barriers = {}

        def end_stage(eng, who):
            barriers[who] = barriers.get(who, 0) + 1
            eng.drain().then_inc(stage_end, 1)
            eng.wait_ge(stage_end, 4 * barriers[who])

        GROUP, groups = {}, 0
        for name, n in ([(f"{t}{h}", 4) for h in (0, 1) for t in "qkv"] + [("dt", 1)]
                        + [(f"{t}{g}", n) for g in range(SSD_G) for t, n in (("z", 4), ("xs", 4), ("bc", 2))]
                        + [("gates", 16), ("na", 8), ("ssd", 8)]
                        + [("aq", 4), ("ak", 4), ("av", 2), ("bq", 4), ("bk", 4), ("bv", 2), ("up0", 32), ("ple0", 8)]
                        + [("cin", 4), ("uqr", 4), ("qi", 4), ("uqn", 8), ("up1", 32), ("ple1", 8)]):
            GROUP[name] = groups
            groups += n

        CHUNK, chunks = {}, []
        used = [0]

        def chunk(name, src, kt, n, released=None):
            if released is None:
                used[0] += 1
                released = (chunk_used, used[0])
            CHUNK[name] = len(chunks)
            chunks.append((src, kt, n, released))

        def rows_of(w, k0, k1, c0, c1):
            return w[k0:k1, c0:c1].rearrange("(t p) n -> p t n", p=P)

        for i in range(12):
            chunk(f"ada{i}", rows_of(d["w_ada"], 0, D, 512 * i, 512 * i + 512), KT, 512, (ada_ready, i + 1))

        def win(name, c0, n, group_end):
            chunk(name, rows_of(d["w_in"], 0, D, c0, c0 + n), KT, n, (gemm_ready, group_end))

        for h in (0, 1):
            for i, t in enumerate("qkv"):
                win(f"{t}{h}", i * D + 512 * h, 512, GROUP[f"{t}{h}"] + 4)
        Z0, X0, DT0, G0 = 3 * D, 3 * D + SSD_W, 3 * D + SSD_W + SSD_W + 2 * SSD_G * SSD_N, None
        G0 = DT0 + 2 * SSD_HEADS
        win("dt", DT0, 2 * SSD_HEADS, GROUP["dt"] + 1)
        for g in range(SSD_G):
            win(f"z{g}", Z0 + 512 * g, 512, GROUP[f"z{g}"] + 4)
            win(f"xs{g}", X0 + 512 * g, 512, GROUP[f"xs{g}"] + 4)
            b0 = X0 + SSD_W + SSD_N * g
            win(f"b{g}", b0, SSD_N, GROUP[f"bc{g}"] + 1)
            win(f"c{g}", b0 + SSD_G * SSD_N, SSD_N, GROUP[f"bc{g}"] + 2)
        for i in range(4):
            win(f"gates{i}", G0 + 512 * i, 512, GROUP["gates"] + 4 * i + 4)
        for i in range(2):
            chunk(f"na{i}", rows_of(d["w_na"], 0, D, 512 * i, 512 * i + 512), KT, 512, (gemm_ready, GROUP["na"] + 4 * i + 4))
        for i in range(2):
            for k in range(2):
                chunk(f"ssd{i}{k}", rows_of(d["w_ssd"], D * k, D * k + D, 512 * i, 512 * i + 512), KT, 512,
                      (gemm_ready, GROUP["ssd"] + 4 * i + 4) if k else None)
        ROWS = {}
        nrows = [0]

        def rows_chunks(name, w, k):
            ROWS[name] = nrows[0]
            nrows[0] += 4
            for i in range(k):
                for h in range(2):
                    chunk(f"{name}{i}{h}", rows_of(w, D * i, D * i + D, 512 * h, 512 * h + 512), KT, 512,
                          (rows_ready, ROWS[name] + 2 * h + 2) if i == k - 1 else None)

        rows_chunks("out", d["w_out"], 1)
        FIRST_EXPERT = len(chunks)
        chunks_before = list(chunks)
        chunks.extend([None] * (12 * NE))

        def second_layer_chunks(l, w_o):
            rows_chunks(f"o{l}", w_o, 1)
            for i in range(8):
                chunk(f"up{l}{i}", rows_of(d["w_mlp_in"][l], 0, D, 512 * i, 512 * i + 512), KT, 512,
                      (gemm_ready, GROUP[f"up{l}"] + 4 * i + 4))
            rows_chunks(f"dn{l}", d["w_mlp_out"][l], 4)
            for i in range(2):
                chunk(f"pg{l}{i}", rows_of(d["w_ple_gate"][l], 0, D, 512 * i, 512 * i + 512), KT, 512,
                      (gemm_ready, GROUP[f"ple{l}"] + 2 * i + 2))
            chunk(f"pp{l}", rows_of(d["w_ple_proj"][l], 0, 256, 0, D), 2, D, (gemm_ready, GROUP[f"ple{l}"] + 8))

        for i, (n, c) in enumerate((("aq", 4), ("ak", 4), ("av", 2), ("bq", 4), ("bk", 4), ("bv", 2))):
            chunk(n, rows_of(d["w_ab"], 0, D, 512 * i, 512 * i + 512), KT, 512, (gemm_ready, GROUP[n] + c))
        second_layer_chunks(0, d["w_oab"])
        chunk("cin0", rows_of(d["w_c"], 0, D, 0, 512), KT, 512, (gemm_ready, GROUP["cin"] + 2))
        chunk("cin1", rows_of(d["w_c"], 0, D, 512, 744), KT, 232, (gemm_ready, GROUP["cin"] + 4))
        chunk("uqr", rows_of(d["w_uqr"], 0, CQ, 0, 512), 3, 512, (gemm_ready, GROUP["uqr"] + 4))
        chunk("qi", rows_of(d["w_qi"], 0, CQ, 0, 512), 3, 512, (gemm_ready, GROUP["qi"] + 4))
        chunk("uqn", rows_of(d["w_uqn"], 0, CQ, 0, D), 3, D, (gemm_ready, GROUP["uqn"] + 8))
        chunk("ukT", rows_of(d["w_ukT"], 0, D, 0, CKV), KT, CKV, (ql_ready, C_HEADS))
        chunk("uv", rows_of(d["w_uv"], 0, CKV, 0, D), 2, D, (uv_ready, C_HEADS))
        second_layer_chunks(1, d["w_oc"])

        def slot(name):
            c = CHUNK[name]
            _, kt, n, _ = chunks[c]
            return ring[:, c % SLOTS, 0:kt * n].rearrange("p (t n) -> p t n", t=kt)

        EXPERT_USES = 12 // SLOTS
        assert 12 % SLOTS == 0

        def wait_chunk(pe, name):
            c = CHUNK[name]
            pe.wait_ge(slot_full[c % SLOTS], 16 * (c // SLOTS + 1))


        def feat_groups(pe, name, blocks, act, t0, t1, first, n_groups):
            w = slot(name)
            wait_chunk(pe, name)
            kt = chunks[CHUNK[name]][1]
            for i in range(n_groups):
                n = first + i
                if n >= 4:
                    pe.wait_ge(gemm_freed, n - 3)
                for k in range(kt):
                    last = pe.matmul(bank[n % 4][:, 0:t1 - t0], w[:, k, (blocks + i) * P:(blocks + i + 1) * P],
                                     act[:, k, t0:t1], start=k == 0, stop=k == kt - 1)
                last.then_inc(gemm_ready, 1)

        def token_groups(pe, name, act, tiles, width, first):
            w = slot(name)
            wait_chunk(pe, name)
            kt = chunks[CHUNK[name]][1]
            for i in range(tiles):
                n = first + i
                if n >= 4:
                    pe.wait_ge(gemm_freed, n - 3)
                for k in range(kt):
                    last = pe.matmul(bank[n % 4][:, 0:width], act[:, k, i * P:(i + 1) * P], w[:, k, 0:width],
                                     start=k == 0, stop=k == kt - 1)
                last.then_inc(gemm_ready, 1)

        def rows_product(pe, name, act, k):
            for i in range(k):
                for h in range(2):
                    w = slot(f"{name}{i}{h}")
                    wait_chunk(pe, f"{name}{i}{h}")
                    for t in range(TT):
                        for kk in range(KT):
                            last = pe.matmul(bank[4 + 2 * h + t][:, :], act[:, KT * i + kk, t * P:(t + 1) * P], w[:, kk, :],
                                             start=i == 0 and kk == 0, stop=i == k - 1 and kk == KT - 1)
                        if i == k - 1:
                            last.then_inc(rows_ready, 1)
                    if i < k - 1:
                        last.then_inc(chunk_used, 1)

        nrm = {"act": [0, 0], "dve": [0, 0, 0], "pe": [0, 0, 0]}

        def norm_act(act, src, junk):
            link = stepper(act, act_step)
            n = len(src)
            for i, s in enumerate(src):
                act.activation(junk[i], s, ACT.Square, accum_out=small[:, i:i + 1]).then_inc(sq_done, 1)
            nrm["act"][0] += n
            act.wait_ge(sq_done, nrm["act"][0])
            act.activation(small[:, 8:8 + n], small[:, 0:n], ACT.Sqrt, bias=epsc[:, :], scale=1.0 / D).then_inc(std_done, 1)

        def norm_dve(dve, src, xn):
            link = stepper(dve, dve_step)
            n = len(src)
            nrm["dve"][0] += 1
            dve.wait_ge(std_done, nrm["dve"][0])
            link(dve.reciprocal(small[:, 16:16 + n], small[:, 8:8 + n]))
            for i, s in enumerate(src):
                dve.tensor_scalar(xn[i], s, small[:, 16 + i:17 + i], None, ALU.mult).then_inc(xn_done, 1)

        def turn_pe(pe, xn, normed=True):
            n = len(xn)
            if normed:
                nrm["pe"][0] += n
                pe.wait_ge(xn_done, nrm["pe"][0])
            for k in range(KT):
                g = nrm["pe"][1]
                nrm["pe"][1] += 1
                if g >= 2:
                    pe.wait_ge(tr_freed, g - 1)
                for i in range(n):
                    last = pe.transpose(bank[g % 2][:, i * P:(i + 1) * P], xn[i][:, k * P:(k + 1) * P], ident)
                last.then_inc(tr_ready, 1)

        def turned_dve(dve, dst, mul=None, add=None, tokens=L):
            for k in range(KT):
                g = nrm["dve"][1]
                nrm["dve"][1] += 1
                dve.wait_ge(tr_ready, g + 1)
                if mul is None:
                    ins = dve.tensor_copy(dst[:, k, :], bank[g % 2][:, 0:tokens])
                elif add is None:
                    ins = dve.tensor_scalar(dst[:, k, :], bank[g % 2][:, 0:tokens], mul[:, k:k + 1], None, ALU.mult)
                else:
                    ins = dve.tensor_scalar(dst[:, k, :], bank[g % 2][:, 0:tokens], mul[:, k:k + 1], add[:, k:k + 1],
                                            ALU.mult, ALU.add)
                ins.then_inc(tr_freed, 1)

        posts = {"act": 0, "dve": 0, "pool": 0}

        def post_act(act, ready, counts_of, junk):
            link = stepper(act, act_step)
            u = posts["act"]
            posts["act"] += 1
            for j in range(4):
                act.wait_ge(ready, counts_of[j])
                act.activation(junk[:, j, :], bank[4 + j][:, :], ACT.Square, accum_out=small[:, 32 + j:33 + j]).then_inc(post_sq, 1)
            act.wait_ge(post_sum, u + 1)
            act.activation(small[:, 40:42], small[:, 36:38], ACT.Sqrt, bias=epsc[:, :], scale=1.0 / D).then_inc(post_std, 1)

        def post_dve(dve, tmp):
            link = stepper(dve, dve_step)
            u = posts["dve"]
            posts["dve"] += 1
            dve.wait_ge(post_sq, 4 * u + 4)
            dve.tensor_tensor(small[:, 36:38], small[:, 32:34], small[:, 34:36], ALU.add).then_inc(post_sum, 1)
            dve.wait_ge(post_std, u + 1)
            link(dve.reciprocal(small[:, 44:46], small[:, 40:42]))
            for j in range(4):
                h, t = j // 2, j % 2
                link(dve.scalar_tensor_tensor(tmp[:, j, :], bank[4 + j][:, :], small[:, 44 + t:45 + t],
                                              grow[:, 512 * h:512 * h + 512], ALU.mult, ALU.mult))
                x = xres[:, t, 512 * h:512 * h + 512]
                dve.tensor_tensor(x, x, tmp[:, j, :], ALU.add).then_inc(post_done, 1)
            dve.wait_ge(post_done, posts["dve"] * 4)

        r1 = Region()
        hT = r1.take(KT, 2 * L)
        xn1 = r1.take(4, D)
        ctx_in = r1.take(TT, D)
        sT = r1.take(KT, 32)
        cc = r1.take(KT, 2)
        ada_rows = r1.take(12, 512)
        AFTER_H = KT * 2 * L
        x_tiles = [xres[:, t, :] for t in range(TT)] + [ctx_in[:, t, :] for t in range(TT)]

        def ada_act(act):
            act.dma_start(xres[:, :, :], d["x"].rearrange("(t p) n -> p t n", p=P)).then_inc(x_in, 16)
            act.dma_start(ctx_in, d["ctx"].rearrange("(t p) n -> p t n", p=P)).then_inc(x_in, 16)
            act.wait_ge(consts_in, 16 * N_CONSTS)
            act.wait_ge(pads_ready, 1)
            act.activation(sT[:, :, 0:2], cc, ACT.Silu).then_inc(sT_ready, 1)
            act.wait_ge(x_in, 32)
            act.wait_ge(eps_ready, 1)
            norm_act(act, x_tiles, [xn1[:, i, :] for i in range(4)])

        def ada_pe(pe):
            pe.wait_ge(sT_ready, 1)
            for i in range(12):
                wait_chunk(pe, f"ada{i}")
                if i >= 4:
                    pe.wait_ge(ada_copied, i - 3)
                w = slot(f"ada{i}")
                for k in range(KT):
                    j = k % 4
                    last = pe.matmul(bank[i % 4][32 * j:32 * j + 32, :], sT[:, k, :], w[:, k, :], start=k < 4, stop=k >= 4,
                                     tile_position=(0, 32 * j))
                last.then_inc(ada_ready, 1)
            pe.wait_ge(ada_copied, 12)
            for b in range(48):
                last = pe.matmul(bank[4][:, 2 * b:2 * b + 2], ada_rows[:, b // 4, (b % 4) * P:(b % 4 + 1) * P], pick[:, :],
                                 start=True, stop=True)
            last.then_inc(ada_cols, 1)
            turn_pe(pe, [xn1[:, i, :] for i in range(4)])

        def ada_dve(dve):
            link = stepper(dve, dve_step)
            link(dve.memset(epsc[:, :], EPS))
            dve.memset(sT, 0.0).then_inc(pads_ready, 1)
            dve.wait_ge(consts_in, 16 * N_CONSTS)
            dve.tensor_copy(bfc[:, 0, :], ident).then_inc(bfc_ready, 1)
            dve.tensor_copy(bfc[:, 1, :], cm("mask_f")).then_inc(bfc_ready, 1)
            dve.tensor_copy(bfc[:, 2, :], cm("mask_b")).then_inc(eps_ready, 1)
            p4 = ident.rearrange("p (j i) -> p i j", i=32)
            link(dve.tensor_reduce(pick[:, :], p4[:, 0:2, :], AX.X, ALU.add))
            dve.wait_ge(x_in, 32)
            norm_dve(dve, x_tiles, [xn1[:, i, :] for i in range(4)])
            for i in range(12):
                dve.wait_ge(ada_ready, i + 1)
                dve.tensor_copy(ada_rows[:, i, :], bank[i % 4][:, :]).then_inc(ada_copied, 1)
            dve.wait_ge(ada_cols, 1)
            cols = bank[4][:, 0:96].rearrange("p (b i) -> p i b", i=2)
            link(dve.tensor_tensor(mod[:, :], cols[:, 0, :], pc("b_ada", 0, 48), ALU.add))
            link(dve.tensor_tensor(modc[:, :], cols[:, 1, 0:16], pc("b_ada", 0, 16), ALU.add))
            link(dve.scalar_tensor_tensor(mul1[:, 0, :], mod[:, 8:16], 1.0, pc("pre_mix", 0, 8), ALU.add, ALU.mult))
            link(dve.scalar_tensor_tensor(mul1[:, 1, :], modc[:, 8:16], 1.0, pc("pre_mix", 0, 8), ALU.add, ALU.mult))
            link(dve.scalar_tensor_tensor(mul2[:, :], mod[:, 32:40], 1.0, pc("pre_ffn", 0, 8), ALU.add, ALU.mult))
            link(dve.tensor_tensor(gain[:, 0, :], mod[:, 16:24], pc("post_mix", 0, 8), ALU.mult))
            link(dve.tensor_tensor(gain[:, 1, :], mod[:, 40:48], pc("post_ffn", 0, 8), ALU.mult))
            for k in range(KT):
                g = nrm["dve"][1]
                nrm["dve"][1] += 1
                dve.wait_ge(tr_ready, g + 1)
                link(dve.tensor_scalar(hT[:, k, 0:L], bank[g % 2][:, 0:L], mul1[:, 0, k:k + 1], mod[:, k:k + 1], ALU.mult, ALU.add))
                dve.tensor_scalar(hT[:, k, L:2 * L], bank[g % 2][:, L:2 * L], mul1[:, 1, k:k + 1], modc[:, k:k + 1],
                                  ALU.mult, ALU.add).then_inc(tr_freed, 1)

        pick = sb("pick", [P, 2])

        def grow_dve_in(dve, i, gdiag):
            for k in range(KT):
                dve.tensor_scalar(gdiag[:, k, :], ident, gain[:, i, k:k + 1], None, ALU.mult).then_inc(gdiag_ready, 1)

        def grow_pe(pe, i, gdiag):
            pe.wait_ge(gdiag_ready, KT * (i + 1))
            for h in range(2):
                pe.matmul(bank[4 + h][:, :], ones, gdiag[:, 4 * h:4 * h + 4, :], start=True, stop=True).then_inc(grow_ready, 1)

        def grow_dve_out(dve, i):
            for h in range(2):
                dve.wait_ge(grow_ready, 2 * i + h + 1)
                dve.tensor_copy(grow[:, 512 * h:512 * h + 512], bank[4 + h][:, :]).then_inc(grow_in, 1)

        rope_n = {"act": 0, "pe": 0, "dve": 0}
        raw = sb("raw", [P, 2, L])
        rp = sb("rp", [P, 2, L])

        def rope_act(act, group, extra=None):
            n = rope_n["act"]
            rope_n["act"] += 1
            act.wait_ge(gemm_ready, group + 1)
            if n >= 2:
                act.wait_ge(rope_done, n - 1)
            if extra is not None:
                dst, src = extra
                link = stepper(act, act_step)
                link(act.copy(dst, src))
            act.copy(raw[:, n % 2, :], bank[group % 4][:, 0:L]).then_inc(gemm_freed, 1)

        def rope_pe(pe, group, swap):
            n = rope_n["pe"]
            rope_n["pe"] += 1
            pe.wait_ge(gemm_freed, group + 1)
            if n >= 2:
                pe.wait_ge(swap_freed, n - 1)
            pe.matmul(bank[4 + n % 2][:, 0:L], cm(swap), raw[:, n % 2, :], start=True, stop=True).then_inc(swap_ready, 1)

        def rope_dve(dve, cos, sin, outs):
            link = stepper(dve, dve_step)
            n = rope_n["dve"]
            rope_n["dve"] += 1
            dve.wait_ge(swap_ready, n + 1)
            if n:
                dve.wait_ge(rope_done, n)
            link(dve.tensor_tensor(rp[:, 0, :], raw[:, n % 2, :], cos, ALU.mult))
            dve.tensor_tensor(rp[:, 1, :], bank[4 + n % 2][:, 0:L], sin, ALU.mult).then_inc(swap_freed, 1)
            dve.wait_ge(swap_freed, n + 1)
            for i, (dst, p0, p1) in enumerate(outs):
                ins = dve.tensor_tensor(dst, rp[p0:p1, 0, :], rp[p0:p1, 1, :], ALU.add)
                if i < len(outs) - 1:
                    link(ins)
            ins.then_inc(rope_done, 1)

        stat = sb("stat", [P, 2, 4])
        counted = {"sets": 0, "units": 0, "values": 0}

        class Attention:

            def __init__(self, units, parts, width, bias, scale, s, pr, turned):
                self.units, self.parts, self.width, self.bias = units, parts, width, bias
                self.scale, self.s, self.pr, self.turned = scale, s, pr, turned
                self.sets, self.first = counted["sets"], counted["units"]
                counted["sets"] += units * parts
                counted["units"] += units

            before_bias = staticmethod(lambda dve, i: None)

        def att_pe(pe, A, scores, value):
            n = A.units * A.parts
            for step in range(n + 4):
                if step < n:
                    if step >= 2:
                        pe.wait_ge(att_biased, A.sets + step - 1)
                    scores(pe, step, bank[step % 2]).then_inc(att_scores, 1)
                i = step - 2
                if 0 <= i < n and i % A.parts == A.parts - 1:
                    u = i // A.parts
                    pe.wait_ge(att_probs, A.first + u + 1)
                    if u >= 2:
                        pe.wait_ge(att_copied, A.first + u - 1)
                    for k in range(A.width(u) // P):
                        last = pe.transpose(bank[2 + u % 2][:, k * P:(k + 1) * P], A.pr[:, u % 2, k * P:(k + 1) * P], ident)
                    last.then_inc(att_turned, 1)
                i = step - 4
                if 0 <= i < n and i % A.parts == A.parts - 1:
                    value(pe, i // A.parts)

        def att_dve(dve, A, after, lam_of=None):
            link = stepper(dve, dve_step)
            n = A.units * A.parts
            for step in range(n + 7):
                i = step
                if i < n:
                    A.before_bias(dve, i)
                    u, w = i // A.parts, A.width(i // A.parts)
                    dve.wait_ge(att_scores, A.sets + i + 1)
                    if u >= 2 // A.parts:
                        dve.wait_ge(att_probs, A.first + (i - 2) // A.parts + (i - 2) % A.parts)
                        if A.parts == 1:
                            dve.wait_ge(att_probs, A.first + i - 1)
                    st = stat[:, i % 2, :]
                    link(dve.tensor_tensor_reduce(out=A.s[:, i % 2, 0:w], in0=bank[i % 2][:, 0:w], in1=A.bias(u), scale=1.0,
                                                  scalar=-3e38, op0=ALU.add, op1=ALU.max, accum_out=st[:, 0:1]))
                    dve.tensor_scalar(st[:, 1:2], st[:, 0:1], -A.scale, None, ALU.mult).then_inc(att_biased, 1)
                i = step - 1
                if 0 <= i < n:
                    u, w = i // A.parts, A.width(i // A.parts)
                    st = stat[:, i % 2, :]
                    dve.wait_ge(att_exp, A.sets + i + 1)
                    link(dve.reciprocal(st[:, 3:4], st[:, 2:3]))
                    if i % A.parts == A.parts - 1 and u >= 2:
                        dve.wait_ge(att_turned, A.first + u - 1)
                    e, pr = A.s[:, i % 2, 0:w], A.pr[:, u % 2, 0:w]
                    if A.parts == 1:
                        dve.tensor_scalar(pr, e, st[:, 3:4], None, ALU.mult).then_inc(att_probs, 1)
                    elif i % 2 == 0:
                        link(dve.tensor_scalar(lam_of[1][:, 0:w], e, st[:, 3:4], None, ALU.mult))
                    else:
                        link(dve.tensor_tensor(st[:, 3:4], st[:, 3:4], lam_of[0], ALU.mult))
                        dve.scalar_tensor_tensor(pr, e, st[:, 3:4], lam_of[1][:, 0:w], ALU.mult, ALU.add).then_inc(att_probs, 1)
                i = step - 6
                if 0 <= i < n and i % A.parts == A.parts - 1:
                    after(dve, i // A.parts)

        def att_act(act, A, turned_free):
            n = A.units * A.parts
            for step in range(n + 3):
                i = step
                if i < n:
                    u, w = i // A.parts, A.width(i // A.parts)
                    st = stat[:, i % 2, :]
                    act.wait_ge(att_biased, A.sets + i + 1)
                    s = A.s[:, i % 2, 0:w]
                    act.activation(s, s, ACT.Exp, bias=st[:, 1:2], scale=A.scale, accum_out=st[:, 2:3]).then_inc(att_exp, 1)
                i = step - 3
                if 0 <= i < n and i % A.parts == A.parts - 1:
                    u = i // A.parts
                    act.wait_ge(att_turned, A.first + u + 1)
                    turned_free(act, u)
                    k = A.width(u) // P
                    act.copy(A.turned(u), bank[2 + u % 2][:, 0:k * P].rearrange("p (k q) -> p k q", q=P)).then_inc(att_copied, 1)

        def head_values(A, v, PT, heads, causal, first, store):
            def value(pe, u):
                h, qt = u // 2, u % 2
                if qt == 0:
                    return
                blk, side = h // 2, h % 2
                pe.wait_ge(att_copied, A.first + u + 1)
                if side == 0 and blk >= 2:
                    pe.wait_ge(att_stored, first // 2 + blk - 1)
                n = A.width(1) // P
                o = bank[4 + blk % 2][64 * side:64 * side + 64, :]
                for k in range(n):
                    q0 = P if causal and k == 1 else 0
                    last = pe.matmul(o[:, q0:L], v[:, k, HD * h:HD * h + HD], PT[:, h % 2, k, q0:L], start=k == 0, stop=k == n - 1)
                last.then_inc(att_out, 1)

            def after(dve, u):
                h, qt = u // 2, u % 2
                if qt == 0 or h % 2 == 0:
                    return
                dve.wait_ge(att_out, first + h + 1)
                dve.tensor_copy(store(h // 2), bank[4 + (h // 2) % 2][:, 0:L]).then_inc(att_stored, 1)

            def turned_free(act, u):
                h = u // 2
                if h >= 2:
                    act.wait_ge(att_out, first + h - 1)
            counted["values"] += heads
            return value, after, turned_free

        r2 = Region(AFTER_H)
        oT = r2.take(KT, L)
        AFTER_O = r2.at
        qz = r2.take(4, 2, L)
        kT = r2.take(4, 2 * L)
        v_na = r2.take(4, 512)
        na_bias = r2.take(3, TT, 2 * L)
        s_na, pr_na, PT_na = r2.take(2, 512), r2.take(2, 512), r2.take(2, 4, L)
        zero_ready = sem("zero_ready")

        NA = []
        for hf in (0, 1):
            A = Attention(16, 1, lambda u: 2 * L, lambda u, hf=hf: na_bias[:, (8 * hf + u // 2) % 3, u % 2, :], 1.0, s_na, pr_na,
                          lambda u: PT_na[:, (u // 2) % 2, :, (u % 2) * P:(u % 2 + 1) * P])

            def before(dve, i, hf=hf):
                h = 8 * hf + i // 2
                if i % 2 == 0:
                    dve.wait_ge(bias_in[h % 3], 16 * (h // 3 + 1))
            A.before_bias = before
            A.hooks = head_values(A, v_na, PT_na, 8, False, counted["values"], lambda blk, hf=hf: oT[:, 4 * hf + blk, :])
            NA.append(A)

        def na_proj_pe(pe, hf):
            feat_groups(pe, f"q{hf}", 0, hT, 0, L, GROUP[f"q{hf}"], 4)
            for b in range(4):
                rope_pe(pe, GROUP[f"q{hf}"] + b, "swap16")
            feat_groups(pe, f"k{hf}", 0, hT, 0, 2 * L, GROUP[f"k{hf}"], 4)
            for b in range(4):
                rope_pe(pe, GROUP[f"k{hf}"] + b, "swap16")
            token_groups(pe, f"v{hf}", hT, 4, 512, GROUP[f"v{hf}"])

        def na_proj_act(act, hf):
            for b in range(4):
                rope_act(act, GROUP[f"q{hf}"] + b)
            for b in range(4):
                g = GROUP[f"k{hf}"] + b
                rope_act(act, g, (kT[:, b, L:2 * L], bank[g % 4][:, L:2 * L]))
            for i in range(4):
                g = GROUP[f"v{hf}"] + i
                act.wait_ge(gemm_ready, g + 1)
                act.copy(v_na[:, i, :], bank[g % 4][:, :]).then_inc(gemm_freed, 1)

        def na_proj_dve(dve, hf):
            link = stepper(dve, dve_step)
            if hf == 0:
                link(dve.memset(qz, 0.0))
            for b in range(4):
                rope_dve(dve, tb("na_qc"), tb("na_qs"), [(qz[0:64, b, 0, :], 0, 64), (qz[64:128, b, 1, :], 64, 128)])
            for b in range(4):
                rope_dve(dve, tb("na_kc"), tb("na_ks"), [(kT[:, b, 0:L], 0, 128)])

        def na_bias_pool(pool, hf, first, last):
            if hf == 0 and first == 0:
                pool.memset(na_bias, 0.0).then_inc(zero_ready, 1)
                pool.wait_ge(zero_ready, 1)
            for h in range(8 * hf + first, 8 * hf + last):
                if h >= 3:
                    pool.wait_ge(att_biased, 2 * (h - 2))
                pool.dma_start(na_bias[:, h % 3, :, 0:L], d["na_bias"][h]).then_inc(bias_in[h % 3], 16)

        def na_scores_of(hf):
            def scores(pe, u, b):
                h, qt = u // 2, u % 2
                return pe.matmul(b[:, :], qz[:, h // 2, h % 2, qt * P:(qt + 1) * P], kT[:, h // 2, :], start=True, stop=True)
            return scores

        r3 = Region(AFTER_O)
        yT = r3.take(16, L)
        AFTER_Y = r3.at
        dtv = r3.take(4, 64)
        av = r3.take(4, 64)
        nega = r3.take(64)
        acs = r3.take(TT, P)
        nacs = r3.take(TT, 64)
        eacs = r3.take(TT, 64)
        wctx = r3.take(TT, 64)
        AT = r3.take(L)
        zs = r3.take(GB, L)
        cin = r3.take(2, 2, L + 4)
        cacc = r3.take(2, 2, L)
        conv = r3.take(6, 2, L)
        sp = conv.rearrange("p b s l -> p (b s l)")[:, 0:6 * 256].rearrange("p (i t h) -> p i t h", i=6, t=4)
        xst = r3.take(4, GB * P)
        bst = r3.take(TT, P)
        xw = r3.take(2, GB * P)
        h0 = r3.take(2, GB * P)
        yoff = r3.take(TT, GB * P)
        yo2 = r3.take(GB * P)
        cbT = r3.take(TT, L)
        Em = r3.take(2, 2, 3 * P)
        ysum, ysq, rstd = r3.take(2, L), r3.take(2, L), r3.take(2, L)
        (dt_abs, dt_exp, dt_one, dt_ln, dt_ready, acs_ready, acs_done, at_ready, wct_done, at_done, negA_done, ctxw_done) = (sem(n) for n in (
            "dt_abs", "dt_exp", "dt_one", "dt_ln", "dt_ready", "acs_ready", "acs_done", "at_ready", "wct_done", "at_done",
            "negA_done", "ctxw_done"))
        (pad_zero, cin_ready, conv_done, conv_silu, xt_ready, xt_done, xw_done, h0_ready, h0_done, yoff_ready, yoff_done, cb_ready,
         cb_done, seg_ready, seg_exp, seg_done, y_ready, y_out, y_gated, y_sq, y_tot, y_std, y_norm, st_used) = (sem(n) for n in (
             "pad_zero", "cin_ready", "conv_done", "conv_silu", "xt_ready", "xt_done", "xw_done", "h0_ready", "h0_done", "yoff_ready",
             "yoff_done", "cb_ready", "cb_done", "seg_ready", "seg_exp", "seg_done", "y_ready", "y_out", "y_gated", "y_sq",
             "y_tot", "y_std", "y_norm", "st_used"))

        def dt_pe(pe):
            w, n = slot("dt"), GROUP["dt"]
            wait_chunk(pe, "dt")
            if n >= 4:
                pe.wait_ge(gemm_freed, n - 3)
            for i in range(4):
                for k in range(KT):
                    last = pe.matmul(bank[n % 4][:, 64 * i:64 * i + 64], hT[:, k, i * P:(i + 1) * P], w[:, k, :],
                                     start=k == 0, stop=k == KT - 1)
            last.then_inc(gemm_ready, 1)
            pe.wait_ge(dt_ready, 1)
            F, B = slice(0, 32), slice(32, 64)

            def total(col, terms):
                for i, (m, tile, cols) in enumerate(terms):
                    r = pe.matmul(bank[4][:, col:col + 32], m, av[:, tile, cols], start=i == 0, stop=i == len(terms) - 1)
                return r
            le, ge, gt, lt = cm("le"), cm("ge"), cm("gt"), cm("lt")
            total(0, [(le, 0, F)])
            total(32, [(ge, 0, B), (ones, 1, B)])
            total(64, [(le, 1, F), (ones, 0, F)])
            total(96, [(ge, 1, B)])
            total(128, [(gt, 2, F), (ones, 3, F)])
            total(160, [(lt, 2, B)])
            total(192, [(gt, 3, F)])
            total(224, [(lt, 3, B), (ones, 2, B)]).then_inc(acs_ready, 1)
            pe.wait_ge(acs_done, 1)
            for t in range(TT):
                last = pe.transpose(bank[5][:, t * P:(t + 1) * P], acs[:, t, :], ident)
            last.then_inc(at_ready, 1)

        def dt_act(act):
            act.wait_ge(consts_in, 16 * N_CONSTS)
            act.activation(nega, heads[:, 0:64], ACT.Exp).then_inc(negA_done, 1)
            act.wait_ge(dt_abs, 1)
            act.activation(sp[:, 2], sp[:, 1], ACT.Exp).then_inc(dt_exp, 1)
            act.wait_ge(dt_one, 1)
            act.activation(sp[:, 4], sp[:, 3], ACT.Ln).then_inc(dt_ln, 1)
            act.wait_ge(acs_ready, 1)
            act.wait_ge(acs_done, 1)
            link = stepper(act, act_step)
            b = bank[4]
            act.activation(eacs, b[:, 0:128].rearrange("p (t h) -> p t h", t=TT), ACT.Exp).then_inc(ctxw_done, 1)
            act.activation(wctx, b[:, 128:256].rearrange("p (t h) -> p t h", t=TT), ACT.Exp).then_inc(ctxw_done, 1)

        def dt_dve(dve):
            link = stepper(dve, dve_step)
            n = GROUP["dt"]
            x, na, e, u, ln, t = (sp[:, i] for i in range(6))
            link(dve.memset(acs, 0.0))
            dve.wait_ge(gemm_ready, n + 1)
            ps = bank[n % 4][:, 0:256].rearrange("p (t h) -> p t h", t=4)
            dve.tensor_tensor(x, ps, heads[:, 64:128].unsqueeze(1).broadcast_to([P, 4, 64]), ALU.add).then_inc(gemm_freed, 1)
            dve.wait_ge(gemm_freed, n + 1)
            dve.scalar_tensor_tensor(na, x, -1.0, x, ALU.mult, ALU.min).then_inc(dt_abs, 1)
            dve.wait_ge(dt_exp, 1)
            dve.tensor_scalar(u, e, 1.0, None, ALU.add).then_inc(dt_one, 1)
            dve.wait_ge(dt_one, 1)
            link(dve.tensor_scalar(t, u, 1.0, None, ALU.is_equal))
            link(dve.scalar_tensor_tensor(na, u, -1.0, t, ALU.add, ALU.add))
            link(dve.reciprocal(na, na))
            link(dve.tensor_tensor(na, na, e, ALU.mult))
            dve.wait_ge(dt_ln, 1)
            link(dve.tensor_tensor(na, na, ln, ALU.mult))
            link(dve.tensor_tensor(t, t, e, ALU.mult))
            link(dve.tensor_tensor(na, na, t, ALU.add))
            link(dve.scalar_tensor_tensor(dtv, x, 0.0, na, ALU.max, ALU.add))
            dve.wait_ge(negA_done, 1)
            dve.scalar_tensor_tensor(av, dtv, -1.0, nega.unsqueeze(1).broadcast_to([P, 4, 64]), ALU.mult, ALU.mult).then_inc(dt_ready, 1)
            dve.wait_ge(acs_ready, 1)
            ps = bank[4][:, 0:128].rearrange("p (t h) -> p t h", t=TT)
            link(dve.tensor_scalar(nacs, ps, -1.0, None, ALU.mult))
            dve.tensor_copy(acs[:, :, 0:64], ps).then_inc(acs_done, 1)
            dve.wait_ge(ctxw_done, 2)
            dve.tensor_tensor(wctx, wctx, dtv[:, 2:4, :], ALU.mult).then_inc(wct_done, 1)
            dve.wait_ge(at_ready, 1)
            dve.tensor_copy(AT, bank[5][:, 0:L]).then_inc(at_done, 1)

        def ssd_pe(pe, g):
            bt, ct = conv[:, 4], conv[:, 5]
            if g:
                pe.wait_ge(seg_exp, 4 * GH * g)
            feat_groups(pe, f"z{g}", 0, hT, 0, L, GROUP[f"z{g}"], 4)
            feat_groups(pe, f"xs{g}", 0, hT, 0, 2 * L, GROUP[f"xs{g}"], 4)
            feat_groups(pe, f"b{g}", 0, hT, 0, 2 * L, GROUP[f"bc{g}"], 1)
            feat_groups(pe, f"c{g}", 0, hT, 0, 2 * L, GROUP[f"bc{g}"] + 1, 1)
            for i in range(5):
                n = 5 * g + i
                pe.wait_ge(conv_silu, 6 * g + (5 if i == 4 else 4))
                if n >= 2:
                    pe.wait_ge(xt_done, n - 1)
                for b in range(GB if i < 4 else TT):
                    src = conv[:, b, i // 2, (i % 2) * P:(i % 2 + 1) * P] if i < 4 else bt[:, 1, b * P:(b + 1) * P]
                    last = pe.transpose(bank[4 + n % 2][:, b * P:(b + 1) * P], src, ident)
                last.then_inc(xt_ready, 1)
            pe.wait_ge(conv_silu, 6 * g + 6)
            if g:
                pe.wait_ge(y_std, g)
            for s in range(TT):
                last = pe.matmul(bank[6][:, s * L:(s + 1) * L], bt[:, 0, s * P:(s + 1) * P], ct[:, 0, :], start=True, stop=True)
            last.then_inc(cb_ready, 1)
            pe.wait_ge(xt_done, 5 * g + 5)
            for dr in range(2):
                n = 2 * g + dr
                if n >= 1:
                    pe.wait_ge(h0_done, n)
                for t in range(TT):
                    pe.wait_ge(xw_done, 2 * n + t + 1)
                    last = pe.matmul(bank[7][:, :], bst[:, t, :], xw[:, t, :], start=t == 0, stop=t == TT - 1)
                last.then_inc(h0_ready, 1)
            pe.wait_ge(h0_done, 2 * g + 2)
            for t in range(TT):
                n = 2 * g + t
                if n >= 1:
                    pe.wait_ge(yoff_done, n)
                for dr in range(2):
                    last = pe.matmul(bank[4 + dr][:, :], ct[:, 0, t * P:(t + 1) * P], h0[:, dr, :], start=True, stop=True)
                last.then_inc(yoff_ready, 1)
            pe.wait_ge(gemm_freed, GROUP[f"bc{g}"] + 2)
            pe.wait_ge(at_done, 1)
            pe.wait_ge(yoff_done, 2 * g + 2)

            def segs(r):
                n = GH * g + r
                if n >= 2:
                    pe.wait_ge(seg_exp, 4 * (n - 1))
                for dr in range(2):
                    b = bank[2 * (r % 2) + dr]
                    pick_head = ident[:, 32 * dr + n:32 * dr + n + 1].broadcast_to([P, P])
                    cols = ((0, L, 0, 0), (L, 3 * P, P, L)) if dr == 0 else ((0, P, 0, 0), (P, 3 * P, 0, 2 * P))
                    for c0, c1, l0, dg in cols:
                        pe.matmul(b[:, c0:c1], pick_head, AT[:, l0:l0 + c1 - c0], start=True, stop=False, skip_group_check=True)
                        last = pe.matmul(b[:, dg:dg + P], bfc[:, 0, :], bfc[:, 1 + dr, :], start=False, stop=True, skip_group_check=True)
                last.then_inc(seg_ready, 1)

            def product(r):
                n = GH * g + r
                blk, side = r // 2, r % 2
                nb = GB * g + blk
                o = bank[4 + blk % 2]
                if side == 0:
                    if blk >= 2:
                        pe.wait_ge(y_out, nb - 1)
                    for t in range(TT):
                        pe.matmul(o[:, t * P:(t + 1) * P], yoff[:, t, blk * P:(blk + 1) * P], ident, start=t == 0, stop=False,
                                  skip_group_check=True)
                pe.wait_ge(seg_done, 4 * n + 4)
                e = Em[:, r % 2]
                oh = o[64 * side:64 * side + 64, :]
                for c0, c1, l0, s, dr in ((0, L, 0, 0, 0), (L, 3 * P, P, 1, 0), (0, P, 0, 0, 1), (P, 3 * P, 0, 1, 1)):
                    last = pe.matmul(oh[:, l0:l0 + c1 - c0], xst[:, s, r * HD:(r + 1) * HD], e[:, dr, c0:c1], start=False, stop=True,
                                     skip_group_check=True)
                last.then_inc(y_ready, 1)

            for r in range(GH + 1):
                if r < GH:
                    segs(r)
                if r >= 1:
                    product(r - 1)
            for blk in range(GB):
                pe.wait_ge(y_sq, GB * g + blk + 1)
                if blk == 0:
                    pe.wait_ge(cb_done, g + 1)
                last = pe.matmul(bank[6][:, 0:L], ones, ysq[:, blk % 2, :], start=blk == 0, stop=blk == GB - 1)
                last.then_inc(y_tot, 1)

        def ssd_act(act, g):
            for b in range(4):
                n = GROUP[f"z{g}"] + b
                act.wait_ge(gemm_ready, n + 1)
                if b == 0 and g:
                    act.wait_ge(y_gated, GB * g)
                act.activation(zs[:, b, :], bank[n % 4][:, 0:L], ACT.Silu).then_inc(gemm_freed, 1)

            def silu(b):
                m = 6 * g + b
                act.wait_ge(conv_done, m + 1)
                act.activation(conv[:, b], cacc[:, m % 2], ACT.Silu).then_inc(conv_silu, 1)

            for b in range(6):
                m = 6 * g + b
                n = GROUP[f"xs{g}"] + b
                act.wait_ge(gemm_ready, n + 1)
                act.wait_ge(pad_zero, 1)
                if m >= 2:
                    act.wait_ge(conv_done, m - 1)
                act.copy(cin[:, m % 2, :, 2:L + 2], bank[n % 4][:, :].rearrange("p (s l) -> p s l", s=2)).then_inc(gemm_freed, 1)
                if b == 1 and g:
                    act.wait_ge(y_out, GB * g)
                if b >= 1:
                    silu(b - 1)
            silu(5)
            for i in range(5):
                n = 5 * g + i
                act.wait_ge(xt_ready, n + 1)
                if i < 4:
                    act.copy(xst[:, i, :], bank[4 + n % 2][:, :]).then_inc(xt_done, 1)
                else:
                    act.copy(bst, bank[4 + n % 2][:, 0:2 * P].rearrange("p (t n) -> p t n", t=TT)).then_inc(xt_done, 1)
            act.wait_ge(cb_ready, g + 1)
            act.copy(cbT, bank[6][:, :].rearrange("p (s l) -> p s l", s=TT)).then_inc(cb_done, 1)
            for dr in range(2):
                n = 2 * g + dr
                act.wait_ge(h0_ready, n + 1)
                act.copy(h0[:, dr, :], bank[7][:, :]).then_inc(h0_done, 1)
            for r in range(GH):
                n = GH * g + r
                act.wait_ge(seg_ready, n + 1)
                if n >= 2:
                    act.wait_ge(y_ready, n - 1)
                for dr in range(2):
                    for s, (c0, c1) in enumerate(((0, L), (L, 3 * P)) if dr == 0 else ((0, P), (P, 3 * P))):
                        c = 32 * dr + n
                        act.activation(Em[:, r % 2, dr, c0:c1], bank[2 * (r % 2) + dr][:, c0:c1], ACT.Exp,
                                       bias=nacs[:, s, c:c + 1]).then_inc(seg_exp, 1)
            for blk in range(GB):
                nb = GB * g + blk
                act.wait_ge(y_gated, nb + 1)
                if nb >= 2:
                    act.wait_ge(y_tot, nb - 1)
                act.activation(ysq[:, blk % 2, :], yT[:, nb, :], ACT.Square).then_inc(y_sq, 1)
            act.wait_ge(y_tot, GB * g + GB)
            if g:
                act.wait_ge(y_norm, GB * g)
            act.activation(rstd[:, 0, :], bank[6][:, 0:L], ACT.Sqrt, bias=epsc[:, :], scale=1.0 / (GB * P)).then_inc(y_std, 1)

        def ssd_dve(dve, g):
            link = stepper(dve, dve_step)
            if g == 0:
                dve.memset(cin, 0.0).then_inc(pad_zero, 1)
            for b in range(6):
                m = 6 * g + b
                blk = 6 * g + b
                n = GROUP[f"xs{g}"] + b
                dve.wait_ge(gemm_freed, n + 1)
                if m >= 2:
                    dve.wait_ge(conv_silu, m - 1)
                c, x = cacc[:, m % 2], cin[:, m % 2]
                link(dve.tensor_scalar(c, x[:, :, 0:L], pc("conv_w", blk * CONV), pc("conv_b", blk), ALU.mult, ALU.add))
                for k in range(1, CONV):
                    ins = dve.scalar_tensor_tensor(c, x[:, :, k:k + L], pc("conv_w", blk * CONV + k), c, ALU.mult, ALU.add)
                    if k < CONV - 1:
                        link(ins)
                ins.then_inc(conv_done, 1)
            for t in range(TT):
                dve.wait_ge(yoff_ready, 2 * g + t + 1)
                if t == 0 and g:
                    dve.wait_ge(y_ready, GH * g)
                for dr in range(2):
                    dst = (yoff[:, t, :] if dr == 0 else yo2).rearrange("p (r d) -> p r d", r=GH)
                    w = eacs[:, t, 32 * dr + GH * g:32 * dr + GH * g + GH].unsqueeze(2).broadcast_to([P, GH, HD])
                    link(dve.tensor_tensor(dst, bank[4 + dr][:, :].rearrange("p (r d) -> p r d", r=GH), w, ALU.mult))
                dve.tensor_tensor(yoff[:, t, :], yoff[:, t, :], yo2, ALU.add).then_inc(yoff_done, 1)
                dve.wait_ge(yoff_done, 2 * g + t + 1)
            dve.wait_ge(cb_done, g + 1)

            def out(blk):
                nb = GB * g + blk
                dve.wait_ge(y_ready, GH * g + 2 * blk + 2)
                dve.scalar_tensor_tensor(ysum[:, blk % 2, :], conv[:, blk, 0, :], pc("d_skip", nb), bank[4 + blk % 2][:, 0:L],
                                         ALU.mult, ALU.add).then_inc(y_out, 1)
                dve.wait_ge(y_out, nb + 1)
                dve.tensor_tensor(yT[:, nb, :], ysum[:, blk % 2, :], zs[:, blk, :], ALU.mult).then_inc(y_gated, 1)
                dve.wait_ge(y_gated, nb + 1)

            for r in range(GH):
                n = GH * g + r
                for dr in range(2):
                    for s, (c0, c1, l0) in enumerate(((0, L, 0), (L, 3 * P, P)) if dr == 0 else ((0, P, 0), (P, 3 * P, 0))):
                        c = 32 * dr + n
                        e = Em[:, r % 2, dr, c0:c1]
                        dve.wait_ge(seg_exp, 4 * n + 2 * dr + s + 1)
                        dve.scalar_tensor_tensor(e, e, dtv[:, s, c:c + 1], cbT[:, s, l0:l0 + c1 - c0], ALU.mult, ALU.mult).then_inc(seg_done, 1)
                if r >= 3 and r % 2 == 1:
                    out((r - 3) // 2)
            out(GB - 1)
            dve.wait_ge(y_std, g + 1)
            link(dve.reciprocal(rstd[:, 1, :], rstd[:, 0, :]))
            for blk in range(GB):
                nb = GB * g + blk
                dve.scalar_tensor_tensor(yT[:, nb, :], yT[:, nb, :], pc("ssd_norm", nb), rstd[:, 1, :], ALU.mult, ALU.mult).then_inc(y_norm, 1)

        def ssd_pool(pool, g):
            pool.wait_ge(wct_done, 1)
            for dr in range(2):
                for t in range(TT):
                    m = 2 * (2 * g + dr) + t
                    pool.wait_ge(xt_done, 5 * g + 4)
                    if m >= 2:
                        pool.wait_ge(h0_ready, m // 2)
                    w = wctx[:, t, 32 * dr + GH * g:32 * dr + GH * g + GH].unsqueeze(2).broadcast_to([P, GH, HD])
                    pool.tensor_tensor(xw[:, t, :].rearrange("p (r d) -> p r d", r=GH),
                                       xst[:, 2 + t, :].rearrange("p (r d) -> p r d", r=GH), w, ALU.mult).then_inc(xw_done, 1)

        r4 = Region(AFTER_Y)
        gT = r4.take(16, L)
        uT = r4.take(KT, L)
        ut = r4.take(2, L)
        tmp4 = r4.take(4, 512)
        gdiag4 = r4.take(KT, P)
        merged = sem("merged")

        def merge_pe(pe):
            for i in range(4):
                feat_groups(pe, f"gates{i}", 0, hT, 0, L, GROUP["gates"] + 4 * i, 4)
            grow_pe(pe, 0, gdiag4)
            for i in range(2):
                feat_groups(pe, f"na{i}", 0, oT, 0, L, GROUP["na"] + 4 * i, 4)
            for i in range(2):
                for k in range(2):
                    w = slot(f"ssd{i}{k}")
                    wait_chunk(pe, f"ssd{i}{k}")
                    for b in range(4):
                        n = GROUP["ssd"] + 4 * i + b
                        if k == 0:
                            pe.wait_ge(gemm_freed, n - 3)
                        for kk in range(KT):
                            last = pe.matmul(bank[n % 4][:, 0:L], w[:, kk, b * P:(b + 1) * P], yT[:, KT * k + kk, :],
                                             start=k == 0 and kk == 0, stop=k == 1 and kk == KT - 1)
                        if k == 1:
                            last.then_inc(gemm_ready, 1)
                    if k == 0:
                        last.then_inc(chunk_used, 1)
            pe.wait_ge(grow_in, 2)
            pe.wait_ge(merged, 8)
            rows_product(pe, "out", uT, 1)

        def merge_act(act):
            for i in range(16):
                n = GROUP["gates"] + i
                act.wait_ge(gemm_ready, n + 1)
                act.activation(gT[:, i, :], bank[n % 4][:, 0:L], ACT.Sigmoid).then_inc(gemm_freed, 1)
            post_act(act, rows_ready, [ROWS["out"] + j + 1 for j in range(4)], tmp4)

        def merge_dve(dve):
            link = stepper(dve, dve_step)
            grow_dve_in(dve, 0, gdiag4)
            grow_dve_out(dve, 0)
            dve.wait_ge(gemm_freed, GROUP["na"])
            for i in range(8):
                n = GROUP["na"] + i
                dve.wait_ge(gemm_ready, n + 1)
                dve.tensor_tensor(uT[:, i, :], bank[n % 4][:, 0:L], gT[:, i, :], ALU.mult).then_inc(gemm_freed, 1)
            for i in range(8):
                n = GROUP["ssd"] + i
                dve.wait_ge(gemm_ready, n + 1)
                dve.tensor_tensor(ut[:, i % 2, :], bank[n % 4][:, 0:L], gT[:, 8 + i, :], ALU.mult).then_inc(gemm_freed, 1)
                dve.wait_ge(gemm_freed, n + 1)
                dve.tensor_tensor(uT[:, i, :], uT[:, i, :], ut[:, i % 2, :], ALU.add).then_inc(merged, 1)
            dve.wait_ge(merged, 8)
            post_dve(dve, tmp4)

        r5 = Region()
        hm = r5.take(KT, L)
        xn5 = r5.take(TT, D)
        junk5 = r5.take(TT, D)
        aff = r5.take(TT, NE)
        affT = r5.take(L)
        left = r5.take(L)
        top = r5.take(4, 8)
        place = r5.take(3, L)
        code = r5.take(TT, NE)
        pick5 = r5.take(TT, NE, CAP)
        pick_g = r5.take(NE, 4, CAP)
        xgT = r5.take(KT, NE * CAP)
        PgT = r5.take(NE, L)
        gdiag5 = r5.take(KT, P)
        xg = r5.take(2, KT, CAP)
        pg = r5.take(2, 2, L)
        sg = r5.take(2, 512)
        hid = r5.take(2, 512)
        hidT = r5.take(2, 512)
        yo = r5.take(2, 512)
        tmp5 = junk5.rearrange("p t (h n) -> p (t h) n", h=2)
        (logits_ready, aff_max, aff_exp, aff_done, affT_ready, place_ready, code_ready, pick_ready, gather_ready, gather_read,
         pgt_ready, pgt_done, pgate_done, zero_pg) = (sem(n) for n in (
             "logits_ready", "aff_max", "aff_exp", "aff_done", "affT_ready", "place_ready", "code_ready", "pick_ready",
             "gather_ready", "gather_read", "pgt_ready", "pgt_done", "pgate_done", "zero_pg"))
        (expert_used, gate_ready, up_ready, down_ready, xg_staged, pg_staged, gate_acted, hid_done, hid_turned, hid_copied,
         yo_done, scattered) = (sem(n) for n in (
             "expert_used", "gate_ready", "up_ready", "down_ready", "xg_staged", "pg_staged", "gate_acted", "hid_done",
             "hid_turned", "hid_copied", "yo_done", "scattered"))
        xn5_t = [xn5[:, t, :] for t in range(TT)]
        x_t = [xres[:, t, :] for t in range(TT)]

        def route_act(act):
            norm_act(act, x_t, [junk5[:, t, :] for t in range(TT)])
            act.wait_ge(aff_max, 2)
            for t in range(TT):
                act.activation(aff[:, t, :], bank[2][:, NE * t:NE * t + NE], ACT.Exp, bias=small[:, 26 + t:27 + t],
                               accum_out=small[:, 28 + t:29 + t]).then_inc(aff_exp, 1)
            for g in range(8):
                act.wait_ge(pgt_ready, g + 1)
                act.copy(PgT.rearrange("p e l -> p (e l)")[:, 512 * g:512 * g + 512], bank[4 + g % 2][:, :]).then_inc(pgt_done, 1)

        def route_pe(pe):
            turn_pe(pe, xn5_t)
            pe.wait_ge(tr_freed, nrm["pe"][1])
            for t in range(TT):
                for k in range(KT):
                    last = pe.matmul(bank[2][:, NE * t:NE * t + NE], hm[:, k, t * P:(t + 1) * P], router[:, k, :],
                                     start=k == 0, stop=k == KT - 1)
            last.then_inc(logits_ready, 1)
            pe.wait_ge(aff_done, 2)
            for t in range(TT):
                last = pe.transpose(bank[3][0:NE, t * P:(t + 1) * P], aff[:, t, :], ident)
            last.then_inc(affT_ready, 1)
            pe.wait_ge(place_ready, 1)
            for t in range(TT):
                last = pe.transpose(bank[2][:, NE * t:NE * t + NE], place[0:NE, 2, t * P:(t + 1) * P], ident[0:NE, 0:NE])
            last.then_inc(code_ready, 1)
            pe.wait_ge(pick_ready, 2)
            for k in range(KT):
                if k >= 2:
                    pe.wait_ge(gather_read, k - 1)
                for t in range(TT):
                    last = pe.matmul(bank[k % 2][:, :], xn5[:, t, k * P:(k + 1) * P], pick5[:, t], start=t == 0, stop=t == TT - 1)
                last.then_inc(gather_ready, 1)
            grow_pe(pe, 1, gdiag5)
            pe.wait_ge(grow_in, 4)
            for g in range(8):
                if g >= 2:
                    pe.wait_ge(pgt_done, g - 1)
                for i in range(4):
                    e, t = 2 * g + i // 2, i % 2
                    pe.wait_ge(pgate_done, 2 * e + t + 1)
                    last = pe.transpose(bank[4 + g % 2][:, i * P:(i + 1) * P], pick_g[:, (2 * e + t) % NE], ident)
                last.then_inc(pgt_ready, 1)

        def route_dve(dve):
            link = stepper(dve, dve_step)
            norm_dve(dve, x_t, xn5_t)
            turned_dve(dve, hm, mul2, mod[:, 24:32])
            link(dve.memset(pg, 0.0))
            dve.wait_ge(logits_ready, 1)
            for t in range(TT):
                link(dve.tensor_reduce(small[:, 24 + t:25 + t], bank[2][:, NE * t:NE * t + NE], AX.X, ALU.max))
                dve.tensor_scalar(small[:, 26 + t:27 + t], small[:, 24 + t:25 + t], -1.0, None, ALU.mult).then_inc(aff_max, 1)
            for t in range(TT):
                dve.wait_ge(aff_exp, t + 1)
                link(dve.reciprocal(small[:, 30 + t:31 + t], small[:, 28 + t:29 + t]))
                dve.tensor_scalar(aff[:, t, :], aff[:, t, :], small[:, 30 + t:31 + t], None, ALU.mult).then_inc(aff_done, 1)
            dve.wait_ge(affT_ready, 1)
            link(dve.tensor_copy(affT[0:NE, :], bank[3][0:NE, 0:L]))
            src = affT
            for r in range(CAP // 8):
                link(dve.max(top[0:NE, r, :], src[0:NE, :]))
                link(dve.match_replace(left[0:NE, :], top[0:NE, r, :], src[0:NE, :], -1.0))
                src = left
            link(dve.tensor_scalar(place[0:NE, 0, :], left[0:NE, :], -1.0, None, ALU.is_equal))
            link(dve.memset(place[0:NE, 1, :], 1.0))
            link(dve.tensor_tensor_scan(place[0:NE, 2, :], place[0:NE, 1, :], place[0:NE, 0, :], 0.0, ALU.mult, ALU.add))
            dve.tensor_tensor(place[0:NE, 2, :], place[0:NE, 2, :], place[0:NE, 0, :], ALU.mult).then_inc(place_ready, 1)
            dve.wait_ge(code_ready, 1)
            link(dve.tensor_copy(code, bank[2][:, 0:2 * NE].rearrange("p (t e) -> p t e", t=TT)))
            for t in range(TT):
                dve.tensor_tensor(pick5[:, t], code[:, t, :].unsqueeze(2).broadcast_to([P, NE, CAP]),
                                  numbers.unsqueeze(1).broadcast_to([P, NE, CAP]), ALU.is_equal).then_inc(pick_ready, 1)
            dve.wait_ge(pick_ready, 2)
            dve.wait_ge(aff_done, 2)
            grow_dve_in(dve, 1, gdiag5)
            for k in range(KT):
                dve.wait_ge(gather_ready, k + 1)
                dve.tensor_scalar(xgT[:, k, :], bank[k % 2][:, :], mul2[:, k:k + 1], mod[:, 24 + k:25 + k],
                                  ALU.mult, ALU.add).then_inc(gather_read, 1)
            grow_dve_out(dve, 1)
            for i in range(2 * NE):
                e, t = i // 2, i % 2
                if i >= NE:
                    dve.wait_ge(pgt_ready, (i - NE) // 4 + 1)
                dve.tensor_tensor(pick_g[:, i % NE], pick5[:, t, e, :].unsqueeze(1).broadcast_to([P, 4, CAP]),
                                  aff[:, t, e:e + 1].unsqueeze(2).broadcast_to([P, 4, CAP]), ALU.mult).then_inc(pgate_done, 1)

        FE = FIRST_EXPERT

        def expert_wait(pe, e, k):
            c = FE + k
            pe.wait_ge(slot_full[c % SLOTS], e * (16 * EXPERT_USES) + 16 * (c // SLOTS + 1))

        def expert_slot(k, kt):
            return ring[:, (FE + k) % SLOTS, :].rearrange("p (t n) -> p t n", t=kt)

        def experts_pe(pe):
            pe.wait_ge(hid_done, 1)
            for j in range(4):
                last = pe.matmul(bank[4 + j][:, :], yo_zero[:, 0:P], yo_zero, start=True, stop=False, skip_group_check=True)
            last.then_inc(zero_pg, 1)
            with pe.Fori(0, NE // 2) as i:
                for e2 in range(2):
                    e = 2 * i + e2
                    pe.wait_ge(xg_staged, e + 1)
                    for which, ready in ((0, gate_ready), (1, up_ready)):
                        if which == 0:
                            pe.wait_ge(gate_acted, e + 1)
                        else:
                            pe.wait_ge(hid_done, e + 1)
                        for c in range(4):
                            k = 4 * which + c
                            expert_wait(pe, e, k)
                            w = expert_slot(k, 2)
                            for k2 in range(2):
                                for n in range(4):
                                    last = pe.matmul(bank[which][32 * n:32 * n + 32, :], xg[:, e2, 2 * c + k2, :],
                                                     w[:, k2, 512 * n:512 * n + 512], start=c == 0 and k2 == 0,
                                                     stop=c == 3 and k2 == 1, tile_position=(0, 32 * n))
                            last.then_inc(expert_used if c < 3 else ready, 1)
                    pe.wait_ge(hid_done, e + 2)
                    for b in range(4):
                        last = pe.transpose(bank[2][:, b * P:(b + 1) * P], hid[:, e2, b * P:(b + 1) * P], ident)
                    last.then_inc(hid_turned, 1)
                    pe.wait_ge(hid_copied, e + 1)
                    pe.wait_ge(yo_done, e + 1)
                    for n in range(4):
                        k = 8 + n
                        expert_wait(pe, e, k)
                        w = expert_slot(k, 4)
                        for b in range(4):
                            for half in range(2):
                                q = 2 * half + b % 2
                                last = pe.matmul(bank[3][32 * q:32 * q + 32, :], hidT[:, e2, b * P + 32 * n:b * P + 32 * n + 32],
                                                 w[:, b, 512 * half:512 * half + 512], start=n == 0 and b < 2,
                                                 stop=n == 3 and b >= 2, tile_position=(0, 32 * q))
                        last.then_inc(expert_used if n < 3 else down_ready, 1)
                    pe.wait_ge(yo_done, e + 2)
                    pe.wait_ge(pg_staged, 2 * e + 2)
                    for t in range(TT):
                        for half in range(2):
                            last = pe.matmul(bank[4 + 2 * half + t][:, :], pg[:, e2, half, t * P:(t + 1) * P], yo[:, e2, :],
                                             start=False, stop=False, skip_group_check=True)
                    last.then_inc(scattered, 1)

        yo_zero = tmp5[:, 0, :]

        def experts_act(act):
            act.sem_inc(gate_acted, 1)
            act.sem_inc(yo_done, 1)
            with act.Fori(0, NE // 2) as i:
                for e2 in range(2):
                    e = 2 * i + e2
                    act.wait_ge(gate_ready, e + 1)
                    act.activation(sg[:, e2, :], bank[0][:, :], ACT.Silu).then_inc(gate_acted, 1)
                    act.wait_ge(hid_turned, e + 1)
                    act.copy(hidT[:, e2, :], bank[2][:, :]).then_inc(hid_copied, 1)
                    act.wait_ge(down_ready, e + 1)
                    act.copy(yo[:, e2, :], bank[3][:, :]).then_inc(yo_done, 1)

        def experts_dve(dve):
            link = stepper(dve, dve_step)
            dve.memset(yo_zero, 0.0).then_inc(hid_done, 1)
            dve.wait_ge(hid_done, 1)
            dve.sem_inc(scattered, 2)
            with dve.Fori(0, NE // 2) as i:
                for e2 in range(2):
                    e = 2 * i + e2
                    dve.wait_ge(scattered, e + 1)
                    dve.tensor_scalar(xg[:, e2], xgT[:, :, bass.ds(e * CAP, CAP)], 1.0, None, ALU.mult).then_inc(xg_staged, 1)
                    for half in range(2):
                        p0 = 64 * half
                        dve.tensor_scalar(pg[p0:p0 + 64, e2, half, :], PgT[p0:p0 + 64, bass.ds(e, 1), :].rearrange("p e l -> p (e l)"),
                                          1.0, None, ALU.mult).then_inc(pg_staged, 1)
                    dve.wait_ge(gate_acted, e + 2)
                    dve.wait_ge(up_ready, e + 1)
                    dve.tensor_tensor(hid[:, e2, :], bank[1][:, :], sg[:, e2, :], ALU.mult).then_inc(hid_done, 1)

        tab_in, pT_in = sem("tab_in"), sem("pT_in")
        relu_done, hid2_done, ple_gate, ple_term, ple_done = (sem(n) for n in (
            "relu_done", "hid2_done", "ple_gate", "ple_term", "ple_done"))
        rm = Region()
        hn = rm.take(KT, L)
        xnm = rm.take(TT, D)
        AFTER_N = rm.at
        hid2 = rm.take(DFF // P, L)
        tmpm = rm.take(4, 512)
        gs = rm.take(TT, D)
        gterm = rm.take(2, 512)
        pT = rm.take(2, L)
        xnm_t = [xnm[:, t, :] for t in range(TT)]

        def mlp_pe(pe, l):
            turn_pe(pe, xnm_t)
            pe.wait_ge(tr_freed, nrm["pe"][1])
            for i in range(8):
                feat_groups(pe, f"up{l}{i}", 0, hn, 0, L, GROUP[f"up{l}"] + 4 * i, 4)
            pe.wait_ge(hid2_done, 32 * (l + 1))
            rows_product(pe, f"dn{l}", hid2, 4)

        def mlp_act(act, l):
            norm_act(act, x_t, [tmpm.rearrange("p (t h) n -> p t (h n)", t=2)[:, t, :] for t in range(TT)])
            for i in range(32):
                n = GROUP[f"up{l}"] + i
                act.wait_ge(gemm_ready, n + 1)
                act.activation(hid2[:, i, :], bank[n % 4][:, 0:L], ACT.Relu).then_inc(gemm_freed, 1)
            post_act(act, rows_ready, [ROWS[f"dn{l}"] + j + 1 for j in range(4)], tmpm)

        def mlp_dve(dve, l):
            norm_dve(dve, x_t, xnm_t)
            turned_dve(dve, hn, pc("mlp_pre2", 8 * l, 8))
            dve.wait_ge(grow_loaded, 16 * (2 * l + 2))
            post_dve(dve, tmpm)

        def mlp_pool(pool, l):
            for i in range(32):
                pool.wait_ge(gemm_freed, GROUP[f"up{l}"] + i + 1)
                pool.tensor_tensor(hid2[:, i, :], hid2[:, i, :], hid2[:, i, :], ALU.mult).then_inc(hid2_done, 1)

        def load_grow(pool, i):
            pool.dma_start(grow[:, :], d["g_post"][i:i + 1, :].partition_broadcast(P).rearrange("q o n -> q (o n)")).then_inc(grow_loaded, 16)

        def ple_pe(pe, l):
            turn_pe(pe, x_t, normed=False)
            pe.wait_ge(tr_freed, nrm["pe"][1])
            for i in range(2):
                token_groups(pe, f"pg{l}{i}", hn, TT, 512, GROUP[f"ple{l}"] + 2 * i)
            wait_chunk(pe, f"pp{l}")
            pe.wait_ge(pT_in, 16 * (l + 1))
            w = slot(f"pp{l}")
            for i in range(4):
                h, t = i // 2, i % 2
                n = GROUP[f"ple{l}"] + 4 + i
                pe.wait_ge(gemm_freed, n - 3)
                for k in range(2):
                    last = pe.matmul(bank[n % 4][:, :], pT[:, k, t * P:(t + 1) * P], w[:, k, 512 * h:512 * h + 512], start=k == 0, stop=k == 1)
                last.then_inc(gemm_ready, 1)

        def ple_act(act, l):
            for i in range(4):
                h, t = i // 2, i % 2
                n = GROUP[f"ple{l}"] + i
                act.wait_ge(gemm_ready, n + 1)
                act.activation(gs[:, t, 512 * h:512 * h + 512], bank[n % 4][:, :], ACT.Sigmoid).then_inc(gemm_freed, 1)

        def ple_dve(dve, l):
            link = stepper(dve, dve_step)
            turned_dve(dve, hn)
            for i in range(4):
                h, t = i // 2, i % 2
                n = GROUP[f"ple{l}"] + 4 + i
                dve.wait_ge(gemm_ready, n + 1)
                dve.wait_ge(gemm_freed, n)
                dve.tensor_tensor(gterm[:, i % 2, :], bank[n % 4][:, :], gs[:, t, 512 * h:512 * h + 512], ALU.mult).then_inc(gemm_freed, 1)
                dve.wait_ge(gemm_freed, n + 1)
                x = xres[:, t, 512 * h:512 * h + 512]
                dve.tensor_tensor(x, x, gterm[:, i % 2, :], ALU.add).then_inc(ple_done, 1)
            dve.wait_ge(ple_done, 4 * (l + 1))

        def ple_pool(pool, l):
            pool.dma_start(pT, d["pT"][l].rearrange("(k p) n -> p k n", p=P)).then_inc(pT_in, 16)

        r6 = Region(AFTER_N)
        qz_ab = {t: r6.take(4, 2, L) for t in "ab"}
        k_ab = {t: r6.take(4, L) for t in "ab"}
        v_ab = {t: r6.take(TT, 512) for t in "ab"}
        s_ab, pr_ab = r6.take(2, L), r6.take(2, L)
        PT_a, PT_b = r6.take(2, TT, P), r6.take(2, TT, L)
        first_map = r6.take(L)
        oA, oA2 = r6.take(8, P), r6.take(8, P)
        obT = r6.take(KT, L)
        sub = r6.take(4, 8)
        lam_sum, lam_exp, av_ready, av_stored, sub_sum, sub_std, sub_done, sub_ready, sub_out = (sem(n) for n in (
            "lam_sum", "lam_exp", "av_ready", "av_stored", "sub_sum", "sub_std", "sub_done", "sub_ready", "sub_out"))
        causal_w = lambda u: P * (u % 2 + 1)

        def mask_of(m, qt):
            return masks[:, m, 0:P] if qt == 0 else masks[:, m, P:3 * P]

        AA = Attention(8, 2, causal_w, lambda u: mask_of(0, u % 2), 1.0, s_ab, pr_ab, lambda u: PT_a[:, u % 2, 0:u % 2 + 1, :])
        AB = Attention(16, 1, causal_w, lambda u: mask_of(1, u % 2), 1.0, s_ab, pr_ab,
                       lambda u: PT_b[:, (u // 2) % 2, 0:u % 2 + 1, (u % 2) * P:(u % 2 + 1) * P])
        AB.hooks = head_values(AB, v_ab["b"], PT_b, 8, True, counted["values"], lambda blk: obT[:, 4 + blk, :])

        def ab_proj_pe(pe):
            turn_pe(pe, xnm_t)
            pe.wait_ge(tr_freed, nrm["pe"][1])
            for t in "ab":
                for m in "qk":
                    feat_groups(pe, t + m, 0, hn, 0, L, GROUP[t + m], 4)
                    if t + m == "aq":
                        pe.wait_ge(tab_in, 16)
                    for b in range(4):
                        rope_pe(pe, GROUP[t + m] + b, "swap32")
                token_groups(pe, t + "v", hn, TT, 512, GROUP[t + "v"])

        def ab_proj_act(act):
            norm_act(act, x_t, [oA.rearrange("p u n -> p (u n)"), oA2.rearrange("p u n -> p (u n)")])
            for t in "ab":
                for m in "qk":
                    for b in range(4):
                        rope_act(act, GROUP[t + m] + b)
                for i in range(TT):
                    n = GROUP[t + "v"] + i
                    act.wait_ge(gemm_ready, n + 1)
                    act.copy(v_ab[t][:, i, :], bank[n % 4][:, :]).then_inc(gemm_freed, 1)
            act.wait_ge(lam_sum, 2)
            act.activation(lam[:, 2:4], lam[:, 0:2], ACT.Exp).then_inc(lam_exp, 1)

        def ab_proj_dve(dve):
            link = stepper(dve, dve_step)
            norm_dve(dve, x_t, xnm_t)
            link(dve.memset(qz_ab["a"], 0.0))
            link(dve.memset(qz_ab["b"], 0.0))
            turned_dve(dve, hn, pc("mix_pre2", 0, 8))
            dve.wait_ge(tab_in, 16)
            for t in "ab":
                for b in range(4):
                    q = qz_ab[t]
                    rope_dve(dve, tb("ab_qc"), tb("ab_qs"), [(q[0:64, b, 0, :], 0, 64), (q[64:128, b, 1, :], 64, 128)])
                for b in range(4):
                    rope_dve(dve, tb("ab_kc"), tb("ab_ks"), [(k_ab[t][:, b, :], 0, 128)])
            hv = heads[:, 128:].rearrange("p (i d) -> p i d", i=4)
            for i in range(2):
                dve.tensor_tensor_reduce(out=oA[:, i, 0:HD], in0=hv[:, 2 * i, :], in1=hv[:, 2 * i + 1, :], scale=1.0, scalar=0.0,
                                         op0=ALU.mult, op1=ALU.add, accum_out=lam[:, i:i + 1]).then_inc(lam_sum, 1)
            dve.wait_ge(lam_exp, 1)
            link(dve.tensor_tensor(lam[:, 4:5], lam[:, 2:3], lam[:, 3:4], ALU.subtract))
            link(dve.tensor_scalar(lam[:, 5:6], lam[:, 4:5], -1.0, -LAM_INIT, ALU.mult, ALU.add))

        def ab_att_pe(pe):
            def scores_a(pe, i, b):
                u, m = i // 2, i % 2
                h, qt = u // 2, u % 2
                return pe.matmul(b[:, 0:causal_w(u)], qz_ab["a"][:, h, m, qt * P:(qt + 1) * P], k_ab["a"][:, h, 0:causal_w(u)],
                                 start=True, stop=True)

            def value_a(pe, u):
                h, qt = u // 2, u % 2
                pe.wait_ge(att_copied, AA.first + u + 1)
                if u >= 2:
                    pe.wait_ge(av_stored, u - 1)
                for k in range(qt + 1):
                    last = pe.matmul(bank[4 + u % 2][:, 0:P], PT_a[:, u % 2, k, :], v_ab["a"][:, k, h * P:(h + 1) * P],
                                     start=k == 0, stop=k == qt)
                last.then_inc(av_ready, 1)
            att_pe(pe, AA, scores_a, value_a)
            pe.wait_ge(sub_done, 1)
            for h in range(A_HEADS):
                for qt in range(TT):
                    last = pe.transpose(bank[6 + h % 2][:, (h // 2 * TT + qt) * P:(h // 2 * TT + qt + 1) * P], oA[:, 2 * h + qt, :], ident)
            last.then_inc(sub_ready, 1)
            pe.wait_ge(sub_out, 4)
            pe.wait_ge(av_stored, 8)

            def scores_b(pe, u, b):
                h, qt = u // 2, u % 2
                return pe.matmul(b[:, 0:causal_w(u)], qz_ab["b"][:, h // 2, h % 2, qt * P:(qt + 1) * P], k_ab["b"][:, h // 2, 0:causal_w(u)],
                                 start=True, stop=True)
            att_pe(pe, AB, scores_b, AB.hooks[0])
            pe.wait_ge(att_stored, (AB.values_first + 8) // 2)
            rows_product(pe, "o0", obT, 1)

        AB.values_first = counted["values"] - 8

        def ab_att_act(act):
            def free_a(act, u):
                if u >= 2:
                    act.wait_ge(av_ready, u - 1)
            att_act(act, AA, free_a)
            act.wait_ge(sub_sum, 1)
            act.activation(sub[:, 1, :], sub[:, 0, :], ACT.Sqrt, bias=epsc[:, :], scale=1.0 / P).then_inc(sub_std, 1)
            att_act(act, AB, AB.hooks[2])
            post_act(act, rows_ready, [ROWS["o0"] + j + 1 for j in range(4)], tmp_o)

        def ab_att_dve(dve):
            link = stepper(dve, dve_step)

            def after_a(dve, u):
                dve.wait_ge(av_ready, u + 1)
                dve.tensor_copy(oA[:, u, :], bank[4 + u % 2][:, 0:P]).then_inc(av_stored, 1)
            att_dve(dve, AA, after_a, lam_of=(lam[:, 5:6], first_map))
            dve.wait_ge(av_stored, 8)
            link(dve.tensor_tensor(oA2, oA, oA, ALU.mult))
            dve.tensor_reduce(sub[:, 0, :], oA2, AX.X, ALU.add).then_inc(sub_sum, 1)
            dve.wait_ge(sub_std, 1)
            link(dve.reciprocal(sub[:, 2, :], sub[:, 1, :]))
            link(dve.tensor_scalar(sub[:, 3, :], sub[:, 2, :], 1.0 - LAM_INIT, None, ALU.mult))
            dve.tensor_tensor(oA, oA, sub[:, 3, :].unsqueeze(2).broadcast_to([P, 8, P]), ALU.mult).then_inc(sub_done, 1)
            dve.wait_ge(sub_ready, 1)
            for h in range(A_HEADS):
                dve.tensor_scalar(obT[:, h, :], bank[6 + h % 2][:, h // 2 * L:h // 2 * L + L], pc("sub", 0), None, ALU.mult).then_inc(sub_out, 1)
            att_dve(dve, AB, AB.hooks[1])
            dve.wait_ge(grow_loaded, 16)
            post_dve(dve, tmp_o)

        ro = Region(r6.at)
        tmp_o = ro.take(4, 512)

        r9 = Region(AFTER_N)
        CW = CQ + CKV + CROPE + 64 + IDX_HEADS
        cct = r9.take(TT, CW)
        cqT = r9.take(3, L)
        ckvT = r9.take(2, L)
        krep = r9.take(TT, P)
        kirep = r9.take(TT, P)
        rot = r9.take(2, TT, 64)
        kz = r9.take(4, L)
        kiz = r9.take(2, L)
        wi = r9.take(TT, IDX_HEADS)
        qnz = r9.take(4, 2, L)
        qrT = r9.take(4, L)
        qiT = r9.take(4, L)
        qlat = r9.take(C_HEADS, 2, L)
        acc = r9.take(TT, L)
        bsel = r9.take(TT, L)
        top9 = r9.take(8)
        relu = r9.take(2, L)
        s_c, pr_c, PT_c = r9.take(2, L), r9.take(2, L), r9.take(2, TT, L)
        olat = r9.take(2, 2, L)
        oTc = hn
        stc = r9.take(12)
        (c_copied, c_sq, c_std, c_norm, c_rot, ct_ready, ct_out, qn_stored, ql_freed, ix_ready, ix_relu, ix_added, olat_ready,
         olat_done, uv_stored) = (sem(n) for n in (
             "c_copied", "c_sq", "c_std", "c_norm", "c_rot", "ct_ready", "ct_out", "qn_stored", "ql_freed", "ix_ready", "ix_relu",
             "ix_added", "olat_ready", "olat_done", "uv_stored"))
        AC = Attention(2 * C_HEADS, 1, causal_w, lambda u: bsel[:, u % 2, 0:causal_w(u)], C_SCALE, s_c, pr_c,
                       lambda u: PT_c[:, (u // 2) % 2, 0:u % 2 + 1, (u % 2) * P:(u % 2 + 1) * P])
        N_TURNED = 7

        def c_pe(pe):
            turn_pe(pe, xnm_t)
            pe.wait_ge(tr_freed, nrm["pe"][1])
            token_groups(pe, "cin0", hn, TT, 512, GROUP["cin"])
            token_groups(pe, "cin1", hn, TT, 232, GROUP["cin"] + 2)
            srcs = [cct[:, :, i * P:(i + 1) * P] for i in range(5)] + [krep, kirep]
            for i, s in enumerate(srcs):
                if i == 0:
                    pe.wait_ge(c_norm, 4)
                if i == 5:
                    pe.wait_ge(c_rot, 2)
                if i >= 2:
                    pe.wait_ge(ct_out, i - 1)
                for t in range(TT):
                    last = pe.transpose(bank[6 + i % 2][:, t * P:(t + 1) * P], s[:, t, :], ident)
                last.then_inc(ct_ready, 1)
            pe.wait_ge(ct_out, N_TURNED)
            for m in ("uqr", "qi"):
                feat_groups(pe, m, 0, cqT, 0, L, GROUP[m], 4)
                for b in range(4):
                    rope_pe(pe, GROUP[m] + b, "swap16")
            pe.wait_ge(rope_done, rope_n["pe"])
            for n in range(2 * IDX_HEADS):
                qt, h = n // IDX_HEADS, n % IDX_HEADS
                if n >= 2:
                    pe.wait_ge(ix_relu, n - 1)
                pe.matmul(bank[n % 2][:, 0:causal_w(qt)], qiT[:, h // 2, qt * P:(qt + 1) * P], kiz[:, h % 2, 0:causal_w(qt)],
                          start=True, stop=True).then_inc(ix_ready, 1)
            pe.wait_ge(ix_relu, 2 * IDX_HEADS)
            for half in range(2):
                feat_groups(pe, "uqn", 4 * half, cqT, 0, L, GROUP["uqn"] + 4 * half, 4)
                wait_chunk(pe, "ukT")
                w = slot("ukT")
                for h in range(8 * half, 8 * half + 8):
                    pe.wait_ge(gemm_freed, GROUP["uqn"] + h // 2 + 1)
                    if h >= 2:
                        pe.wait_ge(ql_freed, h - 1)
                    for c in range(2):
                        last = pe.matmul(bank[6 + h % 2][:, c * L:(c + 1) * L], w[:, h // 2, c * P:(c + 1) * P],
                                         qnz[:, (h // 2) % 4, h % 2, :], start=True, stop=True)
                    last.then_inc(ql_ready, 1)
            pe.wait_ge(ql_freed, C_HEADS)
            wait_chunk(pe, "uv")
            uv = slot("uv")

            def scores(pe, u, b):
                h, qt = u // 2, u % 2
                o, q = b[:, 0:causal_w(u)], slice(qt * P, (qt + 1) * P)
                for c in range(2):
                    pe.matmul(o, qlat[:, h, c, q], ckvT[:, c, 0:causal_w(u)], start=c == 0, stop=False)
                return pe.matmul(o, qrT[:, h // 4, q], kz[:, h % 4, 0:causal_w(u)], start=False, stop=True)

            def up(h):
                blk, side = h // 2, h % 2
                pe.wait_ge(olat_done, h + 1)
                if side == 0 and blk >= 2:
                    pe.wait_ge(uv_stored, blk - 1)
                for c in range(2):
                    last = pe.matmul(bank[6 + blk % 2][64 * side:64 * side + 64, 0:L], uv[:, c, HD * h:HD * h + HD],
                                     olat[:, h % 2, c, :], start=c == 0, stop=c == 1)
                last.then_inc(uv_ready, 1)

            def value(pe, u):
                h, qt = u // 2, u % 2
                if qt == 0:
                    return
                pe.wait_ge(att_copied, AC.first + u + 1)
                if h >= 2:
                    pe.wait_ge(olat_done, h - 1)
                for c in range(2):
                    o = bank[4 + h % 2][:, c * L:(c + 1) * L]
                    w = cct[:, :, CQ + c * P:CQ + (c + 1) * P]
                    pe.matmul(o, w[:, 0, :], PT_c[:, h % 2, 0, :], start=True, stop=False)
                    last = pe.matmul(o[:, P:L], w[:, 1, :], PT_c[:, h % 2, 1, P:L], start=False, stop=True)
                last.then_inc(olat_ready, 1)
                if h >= 1:
                    up(h - 1)
            att_pe(pe, AC, scores, value)
            up(C_HEADS - 1)
            pe.wait_ge(uv_stored, C_HEADS // 2)
            rows_product(pe, "o1", oTc, 1)

        def c_act(act):
            link = stepper(act, act_step)
            norm_act(act, x_t, [qlat.rearrange("p h c l -> p (h c l)")[:, D * t:D * t + D] for t in range(TT)])
            for i in range(4):
                c, t = i // 2, i % 2
                n = GROUP["cin"] + i
                act.wait_ge(gemm_ready, n + 1)
                w = (512, CW - 512)[c]
                act.copy(cct[:, t, 512 * c:512 * c + w], bank[n % 4][:, 0:w]).then_inc(gemm_freed, 1)
            act.wait_ge(gemm_freed, GROUP["cin"] + 4)
            junk = acc.rearrange("p t l -> p (t l)")
            for t in range(TT):
                link(act.activation(junk[:, 0:CQ], cct[:, t, 0:CQ], ACT.Square, accum_out=stc[:, t:t + 1]))
                link(act.activation(junk[:, 0:CKV], cct[:, t, CQ:CQ + CKV], ACT.Square, accum_out=stc[:, 2 + t:3 + t]))
            act.activation(stc[:, 4:6], stc[:, 0:2], ACT.Sqrt, bias=epsc[:, :], scale=1.0 / CQ).then_inc(c_std, 1)
            act.activation(stc[:, 6:8], stc[:, 2:4], ACT.Sqrt, bias=epsc[:, :], scale=1.0 / CKV).then_inc(c_std, 1)
            for m in ("uqr", "qi"):
                for b in range(4):
                    rope_act(act, GROUP[m] + b)
            for n in range(2 * IDX_HEADS):
                w = causal_w(n // IDX_HEADS)
                act.wait_ge(ix_ready, n + 1)
                if n >= 2:
                    act.wait_ge(ix_added, n - 1)
                act.activation(relu[:, n % 2, 0:w], bank[n % 2][:, 0:w], ACT.Relu).then_inc(ix_relu, 1)
            act.wait_ge(qn_stored, 1)
            for half in range(2):
                for b in range(4):
                    n = GROUP["uqn"] + 4 * half + b
                    act.wait_ge(gemm_ready, n + 1)
                    if half:
                        act.wait_ge(ql_ready, 2 * b + 2)
                    link(act.copy(qnz[0:64, b, 0, :], bank[n % 4][0:64, 0:L]))
                    act.copy(qnz[64:128, b, 1, :], bank[n % 4][64:128, 0:L]).then_inc(gemm_freed, 1)
                for h in range(8 * half, 8 * half + 8):
                    act.wait_ge(ql_ready, h + 1)
                    act.copy(qlat[:, h], bank[6 + h % 2][:, :].rearrange("p (c l) -> p c l", c=2)).then_inc(ql_freed, 1)

            def free_c(act, u):
                if u // 2 >= 2:
                    act.wait_ge(olat_ready, u // 2 - 1)
            att_act(act, AC, free_c)
            post_act(act, rows_ready, [ROWS["o1"] + j + 1 for j in range(4)], tmp_c)

        def c_dve(dve):
            link = stepper(dve, dve_step)
            norm_dve(dve, x_t, xnm_t)
            link(dve.memset(kz, 0.0))
            link(dve.memset(kiz, 0.0))
            dve.memset(qnz, 0.0).then_inc(qn_stored, 1)
            turned_dve(dve, hn, pc("mix_pre2", 8, 8))
            dve.wait_ge(c_std, 2)
            link(dve.reciprocal(stc[:, 8:12], stc[:, 4:8]))
            for t in range(TT):
                q, kv = cct[:, t, 0:CQ], cct[:, t, CQ:CQ + CKV]
                dve.tensor_scalar(q, q, stc[:, 8 + t:9 + t], None, ALU.mult).then_inc(c_norm, 1)
                dve.tensor_scalar(kv, kv, stc[:, 10 + t:11 + t], None, ALU.mult).then_inc(c_norm, 1)
            r0 = CQ + CKV
            for t in range(TT):
                x = cct[:, t, r0:r0 + 64]
                xs = x.rearrange("p (g h j) -> p g h j", g=2, h=2)
                ys = rot[:, 1, t, :].rearrange("p (g h j) -> p g h j", g=2, h=2)
                ss = tokt[:, t, 1, :].rearrange("p (g h j) -> p g h j", g=2, h=2)
                link(dve.tensor_tensor(rot[:, 0, t, :], x, tokt[:, t, 0, :], ALU.mult))
                for h in range(2):
                    link(dve.tensor_tensor(ys[:, :, h, :], xs[:, :, 1 - h, :], ss[:, :, h, :], ALU.mult))
                link(dve.tensor_tensor(rot[:, 0, t, :], rot[:, 0, t, :], rot[:, 1, t, :], ALU.add))
                link(dve.tensor_copy(krep[:, t, :].rearrange("p (r j) -> p r j", r=4), rot[:, 0, t, 0:32].unsqueeze(1).broadcast_to([P, 4, 32])))
                kr = kirep[:, t, :].rearrange("p (r j) -> p r j", r=2)
                link(dve.tensor_copy(kr[:, :, 0:32], rot[:, 0, t, 32:64].unsqueeze(1).broadcast_to([P, 2, 32])))
                dve.tensor_copy(kr[:, :, 32:64], cct[:, t, r0 + 64:r0 + 96].unsqueeze(1).broadcast_to([P, 2, 32])).then_inc(c_rot, 1)
            link(dve.tensor_scalar(wi, cct[:, :, CW - IDX_HEADS:CW], IDX_HEADS ** -0.5 * HD ** -0.5, None, ALU.mult))
            for i in range(N_TURNED):
                b = bank[6 + i % 2]
                dve.wait_ge(ct_ready, i + 1)
                if i < 3:
                    ins = dve.tensor_scalar(cqT[:, i, :], b[:, 0:L], pc("cq", i), None, ALU.mult)
                elif i < 5:
                    ins = dve.tensor_scalar(ckvT[:, i - 3, :], b[:, 0:L], pc("ckv", i - 3), None, ALU.mult)
                else:
                    k, n = (kz, 4) if i == 5 else (kiz, 2)
                    for j in range(n):
                        p0, p1 = j * P // n, (j + 1) * P // n
                        ins = dve.tensor_copy(k[p0:p1, j, :], b[p0:p1, 0:L])
                        if j < n - 1:
                            link(ins)
                ins.then_inc(ct_out, 1)
            dve.wait_ge(tab_in, 32)
            for b in range(4):
                rope_dve(dve, tb("cr_c"), tb("cr_s"), [(qrT[:, b, :], 0, P)])
            for b in range(4):
                rope_dve(dve, tb("ci_c"), tb("ci_s"), [(qiT[:, b, :], 0, P)])
            for qt in range(TT):
                w = causal_w(qt)
                a, m = acc[:, qt, 0:w], mask_of(0, qt)
                for h in range(IDX_HEADS):
                    n = IDX_HEADS * qt + h
                    dve.wait_ge(ix_relu, n + 1)
                    dve.scalar_tensor_tensor(a, relu[:, n % 2, 0:w], wi[:, qt, h:h + 1], m if h == 0 else a, ALU.mult, ALU.add).then_inc(ix_added, 1)
                    dve.wait_ge(ix_added, n + 1)
            for qt in range(TT):
                w = causal_w(qt)
                a, m = acc[:, qt, 0:w], mask_of(0, qt)
                for r in range(TOPK // 8):
                    link(dve.max(top9, a))
                    link(dve.match_replace(a, top9, a, -3e38))
                link(dve.tensor_scalar(a, a, -2e38, NEG, ALU.is_gt, ALU.mult))
                link(dve.tensor_tensor(bsel[:, qt, 0:w], a, m, ALU.add))

            def store(blk):
                dve.wait_ge(uv_ready, 2 * blk + 2)
                dve.tensor_copy(oTc[:, blk, :], bank[6 + blk % 2][:, 0:L]).then_inc(uv_stored, 1)

            def after(dve, u):
                h, qt = u // 2, u % 2
                if qt == 0:
                    return
                dve.wait_ge(olat_ready, h + 1)
                if h >= 2:
                    dve.wait_ge(uv_ready, h - 1)
                link(dve.tensor_scalar(olat[:, h % 2, 0, :], bank[4 + h % 2][:, 0:L], pc("ckv", 0), None, ALU.mult))
                dve.tensor_scalar(olat[:, h % 2, 1, :], bank[4 + h % 2][:, L:2 * L], pc("ckv", 1), None, ALU.mult).then_inc(olat_done, 1)
                if h % 2 == 1 and h >= 3:
                    store((h - 3) // 2)
            att_dve(dve, AC, after)
            store(C_HEADS // 2 - 1)
            dve.wait_ge(grow_loaded, 48)
            post_dve(dve, tmp_c)

        tmp_c = qlat.rearrange("p h c l -> p (h c l)")[:, 0:2 * D].rearrange("p (j n) -> p j n", j=4)

        out_in = sem("out_in")
        N_CONSTS = 8
        block = es.enter_context(nc.Block())

        @block.sync
        def _(sp):
            sp.dma_start(cc, d["cc"]).then_inc(consts_in, 16)
            sp.dma_start(cst[:, :], d["cst"]).then_inc(consts_in, 16)
            sp.dma_start(pcol[:, :], d["pcol"]).then_inc(consts_in, 16)
            sp.dma_start(heads[:, :], d["heads"].partition_broadcast(P).rearrange("q o n -> q (o n)")).then_inc(consts_in, 16)
            sp.dma_start(tab[:, :, :], d["tab"][:, 0:4, :]).then_inc(consts_in, 16)
            sp.dma_start(tokt[:, :, :, :], d["tokt"]).then_inc(consts_in, 16)
            sp.dma_start(masks[:, :, :], d["masks"]).then_inc(consts_in, 16)
            sp.dma_start(router[:, :, :], d["w_router"].rearrange("(t p) n -> p t n", p=P)).then_inc(consts_in, 16)

            def load(c):
                src, kt, n, _ = chunks[c]
                if c >= SLOTS and chunks[c - SLOTS] is not None:
                    sp.wait_ge(*chunks[c - SLOTS][3])
                dst = ring[:, c % SLOTS, 0:kt * n].rearrange("p (t n) -> p t n", t=kt)
                sp.dma_start(dst, src).then_inc(slot_full[c % SLOTS], 16)

            for c in range(FE):
                load(c)

            def expert_sources(e):
                for w, rows, n in (("w_egate", 2 * P, FF), ("w_eup", 2 * P, FF), ("w_edown", 4 * P, D)):
                    for c in range(4):
                        s = d[w][bass.ds(e, 1), rows * c:rows * c + rows, :].rearrange("e (t p) n -> p (e t) n", p=P)
                        yield s, rows // P

            def expert_left(k, e):
                which, c = k // 4, k % 4
                if c == 3:
                    return (gate_ready, up_ready, down_ready)[which], e + 1
                return expert_used, e * 9 + (3 * which + c + 1)

            def load_expert(e, first):
                for k, (src, kt) in enumerate(expert_sources(e)):
                    if k < 4:
                        sp.wait_ge(*(chunks[FE - SLOTS + k][3] if first else expert_left(8 + k, e - 1)))
                    else:
                        sp.wait_ge(*expert_left(k - 4, e))
                    s = (FE + k) % SLOTS
                    sp.dma_start(ring[:, s, :].rearrange("p (t n) -> p t n", t=kt), src).then_inc(slot_full[s], 16)

            load_expert(0, True)
            with sp.Fori(1, NE) as e:
                load_expert(e, False)
            for c in range(FE + 12 * NE, len(chunks)):
                if c < FE + 12 * NE + SLOTS:
                    sp.wait_ge(*expert_left(8 + c - FE - 12 * NE, NE - 1))
                load(c)
            sp.wait_ge(ple_done, 8)
            sp.dma_start(out.rearrange("b (t p) n -> p (b t) n", p=P), xres[:, :, :]).then_inc(out_in, 16)
            sp.wait_ge(out_in, 16)

        @block.tensor
        def _(pe):
            ada_pe(pe)
            end_stage(pe, "pe")
            for hf in range(2):
                na_proj_pe(pe, hf)
                end_stage(pe, "pe")
                att_pe(pe, NA[hf], na_scores_of(hf), NA[hf].hooks[0])
                end_stage(pe, "pe")
            dt_pe(pe)
            end_stage(pe, "pe")
            for g in range(SSD_G):
                ssd_pe(pe, g)
            end_stage(pe, "pe")
            merge_pe(pe)
            end_stage(pe, "pe")
            route_pe(pe)
            end_stage(pe, "pe")
            experts_pe(pe)
            end_stage(pe, "pe")
            for l in range(2):
                if l == 0:
                    end_stage(pe, "pe")
                    ab_proj_pe(pe)
                    end_stage(pe, "pe")
                    ab_att_pe(pe)
                else:
                    c_pe(pe)
                end_stage(pe, "pe")
                mlp_pe(pe, l)
                end_stage(pe, "pe")
                ple_pe(pe, l)
                end_stage(pe, "pe")

        @block.scalar
        def _(act):
            ada_act(act)
            end_stage(act, "act")
            for hf in range(2):
                na_proj_act(act, hf)
                end_stage(act, "act")
                att_act(act, NA[hf], NA[hf].hooks[2])
                end_stage(act, "act")
            dt_act(act)
            end_stage(act, "act")
            for g in range(SSD_G):
                ssd_act(act, g)
            end_stage(act, "act")
            merge_act(act)
            end_stage(act, "act")
            route_act(act)
            end_stage(act, "act")
            experts_act(act)
            end_stage(act, "act")
            for l in range(2):
                if l == 0:
                    post_act(act, scattered, [2 + NE] * 4, tmp5)
                    end_stage(act, "act")
                    ab_proj_act(act)
                    end_stage(act, "act")
                    ab_att_act(act)
                else:
                    c_act(act)
                end_stage(act, "act")
                mlp_act(act, l)
                end_stage(act, "act")
                ple_act(act, l)
                end_stage(act, "act")

        @block.vector
        def _(dve):
            ada_dve(dve)
            end_stage(dve, "dve")
            for hf in range(2):
                na_proj_dve(dve, hf)
                end_stage(dve, "dve")
                att_dve(dve, NA[hf], NA[hf].hooks[1])
                end_stage(dve, "dve")
            dt_dve(dve)
            end_stage(dve, "dve")
            for g in range(SSD_G):
                ssd_dve(dve, g)
            end_stage(dve, "dve")
            merge_dve(dve)
            end_stage(dve, "dve")
            route_dve(dve)
            end_stage(dve, "dve")
            experts_dve(dve)
            end_stage(dve, "dve")
            for l in range(2):
                if l == 0:
                    post_dve(dve, tmp5)
                    end_stage(dve, "dve")
                    ab_proj_dve(dve)
                    end_stage(dve, "dve")
                    ab_att_dve(dve)
                else:
                    c_dve(dve)
                end_stage(dve, "dve")
                mlp_dve(dve, l)
                end_stage(dve, "dve")
                ple_dve(dve, l)
                end_stage(dve, "dve")

        @block.gpsimd
        def _(pool):
            end_stage(pool, "pool")
            for hf in range(2):
                na_bias_pool(pool, hf, 0, 3)
                end_stage(pool, "pool")
                na_bias_pool(pool, hf, 3, 8)
                end_stage(pool, "pool")
            pool.dma_start(tab[:, :, :], d["tab"][:, 4:8, :]).then_inc(tab_in, 16)
            end_stage(pool, "pool")
            for g in range(SSD_G):
                ssd_pool(pool, g)
            for _ in range(4):
                end_stage(pool, "pool")
            for l in range(2):
                if l == 0:
                    end_stage(pool, "pool")
                    load_grow(pool, 0)
                    end_stage(pool, "pool")
                    end_stage(pool, "pool")
                    pool.dma_start(tab[:, :, :], d["tab"][:, 8:12, :]).then_inc(tab_in, 16)
                else:
                    load_grow(pool, 2)
                    end_stage(pool, "pool")
                load_grow(pool, 2 * l + 1)
                mlp_pool(pool, l)
                end_stage(pool, "pool")
                ple_pool(pool, l)
                end_stage(pool, "pool")


def kernel(**inputs):
    import concourse.bacc as bacc
    from concourse.bass_utils import run_bass_kernel_spmd

    nc = bacc.Bacc("TRN2", target_bir_lowering=False, num_devices=1)
    arrays = layouts(inputs)
    d = {n: nc.dram_tensor(f"in_{n}", a.shape, mybir.dt.from_np(a.dtype), kind="ExternalInput").ap() for n, a in arrays.items()}
    out = nc.dram_tensor("out", (1, L, D), F32, kind="ExternalOutput").ap()
    build(nc, d, out)
    r = run_bass_kernel_spmd(nc, [{f"in_{n}": a for n, a in arrays.items()}], core_ids=[0])
    return r.results[0]["out"]
```

```python
from contextlib import ExitStack

import numpy as np
import concourse.bass as bass
from concourse import mybir

F32 = mybir.dt.float32
ALU = mybir.AluOpType
ACT = mybir.ActivationFunctionType
AX = mybir.AxisListType

P = 128
L = 256
TT = L // P
D = 1024
KT = D // P
EPS = 1e-6
NEG = -1e30
HD = 64
SLOTS = 4
SLOT = 4096
WORK = 29120

NA_HEADS, GRID_W, NA_KH, NA_KW = 16, 64, 8, 16
SSD_W, SSD_HEADS, SSD_G, SSD_N, CONV = 2048, 32, 4, 128, 5
GB = SSD_W // SSD_G // P
GH = SSD_HEADS // SSD_G
NE, FF, CAP = 16, 2048, 32
A_HEADS, B_HEADS = 4, 8
C_HEADS, CQ, CKV, CROPE, CNOPE = 16, 384, 256, 32, 64
IDX_HEADS, TOPK = 8, 64
C_SCALE = (CNOPE + CROPE) ** -0.5
DFF = 4096
SKIP0 = 4 * SSD_HEADS + 4 * HD
ADA_FIRST = 4
LAM_INIT = 0.2

PCOL = {}
_at = 0
for _name, _n in (("b_ada", 48), ("pre_mix", 8), ("post_mix", 8), ("pre_ffn", 8), ("post_ffn", 8),
                  ("conv_w", 24 * CONV), ("conv_b", 24), ("ssd_norm", 16),
                  ("mix_pre2", 16), ("mlp_pre2", 16), ("cq", 3), ("ckv", 2), ("sub", 1)):
    PCOL[_name] = _at
    _at += _n
NPCOL = _at

CST = ["ident", "ones", "le", "ge", "gt", "lt", "swap16", "swap32"]
NCST = len(CST) * P + CAP
TAB = ["na_qc", "na_qs", "na_kc", "na_ks", "ab_qc", "ab_qs", "ab_kc", "ab_ks",
       "cq_even", "cq_odd", "ci"]


def constants():
    f = np.float32
    i = np.arange(P)
    r, c = i[:, None], i[None, :]
    one = lambda m: m.astype(f)
    mats = {
        "ident": one(r == c), "ones": np.ones((P, P), f), "le": one(r <= c), "ge": one(r >= c),
        "gt": one(r > c), "lt": one(r < c), "swap16": one(r == (c ^ 16)), "swap32": one(r == (c ^ 32)),
    }
    cst = np.concatenate([mats[m] for m in CST] + [np.tile(np.arange(1, CAP + 1, dtype=f), (P, 1))], 1)
    tok = np.arange(L)

    def angles(pos, half):
        inv = (f(10000.0) ** (-np.arange(half, dtype=f) / f(half))).astype(f)
        a = pos.astype(f)[:, None] * inv[None, :]
        return np.cos(a).astype(f), np.sin(a).astype(f)

    def table(pos_of, half, width, rope_width):
        cs, sn = np.ones((P, L), f), np.zeros((P, L), f)
        for p in range(P):
            d = p % width
            if d < rope_width:
                cc, ss = angles(pos_of(d), half)
                j = d % (2 * half)
                cs[p] = cc[:, j % half]
                sn[p] = ss[:, j % half] * (-1 if j < half else 1)
        return cs, sn

    na = table(lambda d: tok // GRID_W if d < 32 else tok % GRID_W, 16, 64, 64)
    ab = table(lambda d: tok, 32, 64, 64)
    cr = table(lambda d: tok, 16, 32, 32)
    plain = np.ones((64, L), f)
    turned = np.concatenate([cr[0][:32], cr[1][:32]])
    cq_even, cq_odd = np.concatenate([plain, turned]), np.concatenate([turned, plain])
    ci = np.concatenate([turned, plain[:32], 0 * plain[:32]])
    s = f(HD ** -0.5)
    tab = np.stack([na[0] * s, na[1] * s, na[0], na[1], ab[0] * s, ab[1] * s, ab[0], ab[1],
                    cq_even, cq_odd, ci], 1)
    cc, ss = angles(tok, 16)
    tokt = np.stack([np.concatenate([cc] * 4, 1), np.concatenate([-ss, ss] * 2, 1)], 1)
    tokt = tokt.reshape(TT, P, 2, 64).transpose(1, 0, 2, 3)
    q, k = tok[:, None], tok[None, :]
    causal = q >= k
    count = ((causal & (q - k <= 128)).astype(int) + (causal & ((q - k) % 4 == 0))
             + (causal & ((q - k) % 16 == 0)))
    cmask = np.where(causal, 0, NEG)
    wmask = np.where(count > 0, np.log(np.maximum(count, 1)), NEG)
    masks = np.stack([np.concatenate([m[:P, :P], m[P:, :]], 1) for m in (cmask, wmask)], 1).astype(f)
    return {"cst": cst, "tab": np.ascontiguousarray(tab.astype(f)), "tokt": np.ascontiguousarray(tokt),
            "masks": np.ascontiguousarray(masks)}


def layouts(v):
    a = {k: np.asarray(x) for k, x in v.items()}
    f = np.float32
    out = constants()
    col = lambda x: np.ascontiguousarray(x.reshape(-1, P).T)
    out["x"], out["ctx"] = a["x"][0], a["ctx"][0]
    out["cc"] = np.stack([col(a["c"][0]), col(a["c_ctx"])], 2)
    gb = SSD_W // SSD_G
    order = np.concatenate([np.concatenate([np.arange(g * gb, (g + 1) * gb),
                                            SSD_W + np.arange(g * SSD_N, (g + 1) * SSD_N),
                                            SSD_W + SSD_G * SSD_N + np.arange(g * SSD_N, (g + 1) * SSD_N)])
                            for g in range(SSD_G)])
    cw = a["ssd_conv_w"][0][:, order]
    pc = [col(a["b_ada"][0])] + [col(a["norm_" + n][0]) for n in ("pre_mix", "post_mix", "pre_ffn", "post_ffn")]
    pc += [cw.reshape(CONV, -1, P).transpose(2, 1, 0).reshape(P, -1), col(a["ssd_conv_b"][0][order])]
    pc += [col(a["ssd_norm"][0])]
    pc += [col(a["g_mix_pre_2"].ravel()), col(a["g_mlp_pre_2"].ravel()), col(a["g_cq_2"][0]),
           col(a["g_ckv_2"][0]), col(a["g_diff_sub_2"][0])]
    out["pcol"] = np.ascontiguousarray(np.concatenate(pc, 1))
    out["heads"] = np.concatenate([a[n][0] for n in ("ssd_a_log_fwd", "ssd_a_log_bwd", "ssd_dt_bias_fwd",
                                                     "ssd_dt_bias_bwd", "diff_lq1_2", "diff_lk1_2",
                                                     "diff_lq2_2", "diff_lk2_2", "ssd_d_skip")])[None, :]
    out["g_post"] = np.stack([a["g_mix_post_2"][0], a["g_mlp_post_2"][0],
                              a["g_mix_post_2"][1], a["g_mlp_post_2"][1]])
    tok = np.arange(L)
    r, w = tok // GRID_W, tok % GRID_W
    start = np.clip(w - NA_KW // 2, 0, GRID_W - NA_KW)
    ok = (w[None, :] >= start[:, None]) & (w[None, :] < start[:, None] + NA_KW)
    dr = r[None, :] - r[:, None] + NA_KH - 1
    dc = np.clip(w[None, :] - w[:, None] + NA_KW - 1, 0, 2 * NA_KW - 2)
    bias = np.where(ok[None], a["na_rpb"][0][:, dr, dc], f(NEG)).astype(f)
    out["na_bias"] = np.ascontiguousarray(bias.reshape(NA_HEADS, TT, P, L).transpose(0, 2, 1, 3))
    out["w_ada"], out["w_in"] = a["w_ada"][0], a["w_in"][0]
    out["w_na"], out["w_ssd"], out["w_out"] = a["w_branch_na"][0], a["w_branch_ssd"][0], a["w_out"][0]
    out["w_router"] = a["w_router"][0]
    for n in ("gate", "up", "down"):
        out["w_e" + n] = a["w_exp_" + n][0]
    out["pT"] = np.ascontiguousarray(a["p_2"][:, 0].transpose(0, 2, 1))
    for n in ("mlp_in", "mlp_out", "ple_proj", "ple_gate"):
        out["w_" + n] = a["w_" + n + "_2"]
    out["w_ab"], out["w_oab"] = a["w_in_ab_2"][0], a["w_out_ab_2"][0]
    out["w_c"], out["w_oc"] = a["w_in_c_2"][0], a["w_out_c_2"][0]
    uq = a["w_uq_2"][0].reshape(CQ, C_HEADS // 2, 2, CNOPE + CROPE)
    plain, rotated = np.arange(CNOPE), np.arange(CROPE)
    even = np.concatenate([plain, CNOPE + rotated, CNOPE + (rotated ^ 16)])
    odd = np.concatenate([CNOPE + rotated, CNOPE + (rotated ^ 16), plain])
    out["w_uq"] = np.stack([uq[:, :, 0][:, :, even], uq[:, :, 1][:, :, odd]], 2).reshape(CQ, -1)
    qi = a["w_qi_2"][0].reshape(CQ, IDX_HEADS, 64)
    out["w_qi"] = qi[:, :, np.concatenate([rotated, rotated ^ 16, 32 + rotated, 32 + rotated])].reshape(CQ, -1)
    out["w_uk"] = a["w_uk_2"][0].reshape(CKV, -1)
    out["w_uv"] = a["w_uv_2"][0].reshape(CKV, -1)
    return {k: np.ascontiguousarray(x) for k, x in out.items()}


def build(nc, d, out):
    es = ExitStack()
    with es:
        def sb(name, shape, dt=F32):
            return es.enter_context(nc.sbuf_tensor(name, shape, dt))

        def sem(name):
            return es.enter_context(nc.semaphore(name))

        ring = sb("ring", [P, SLOTS, SLOT])
        work = sb("work", [P, WORK])
        xres = sb("xres", [P, TT, D])
        cst = sb("cst", [P, NCST])
        tab = sb("tab", [P, 4, L])
        tokt = sb("tokt", [P, TT, 2, 64])
        masks = sb("masks", [P, 2, 3 * P])
        pcol = sb("pcol", [P, NPCOL])
        heads = sb("heads", [P, SKIP0 + SSD_HEADS])
        router = sb("router", [P, KT, NE])
        mod = sb("mod", [P, 48])
        modc = sb("modc", [P, 16])
        mul1 = sb("mul1", [P, 2, KT])
        mul2 = sb("mul2", [P, KT])
        gain = sb("gain", [P, 2, KT])
        grow = sb("grow", [P, D])
        lam = sb("lam", [P, 8])
        sT = sb("sT", [P, KT, 32])
        small = sb("small", [P, 64])
        epsc = sb("epsc", [P, 1])
        bank = [es.enter_context(nc.psum_tensor(f"bank{i}", [P, 512], F32)) for i in range(8)]

        def cm(name):
            i = CST.index(name) * P
            return cst[:, i:i + P]

        def tb(name):
            return tab[:, TAB.index(name) % 4, :]

        def pc(name, i, n=1):
            return pcol[:, PCOL[name] + i:PCOL[name] + i + n]

        ident, ones = cm("ident"), cm("ones")
        numbers = cst[:, len(CST) * P:NCST]

        class Region:

            def __init__(self, at=0, end=WORK):
                self.at, self.end = at, end

            def take(self, *dims):
                n = int(np.prod(dims))
                v = work[:, self.at:self.at + n]
                self.at += n
                assert self.at <= self.end, self.at
                if len(dims) == 1:
                    return v
                names = "abcde"[:len(dims)]
                return v.rearrange(f"p ({' '.join(names)}) -> p {' '.join(names)}", **dict(zip(names, dims)))

        consts_in = sem("consts_in")
        tables_in = sem("tables_in")
        x_in = sem("x_in")
        slot_full = [sem(f"slot_full{i}") for i in range(SLOTS)]
        chunk_used = sem("chunk_used")
        stage_end = sem("stage_end")
        eps_ready = sem("eps_ready")
        gemm_ready, gemm_freed = sem("gemm_ready"), sem("gemm_freed")
        rows_ready = sem("rows_ready")
        dve_step, act_step, pool_step = sem("dve_step"), sem("act_step"), sem("pool_step")
        grow_in, grow_loaded = sem("grow_in"), sem("grow_loaded")
        sT_ready, ada_ready, ada_copied, ada_cols, ada_done = (sem(n) for n in (
            "sT_ready", "ada_ready", "ada_copied", "ada_cols", "ada_done"))
        pads_ready = sem("pads_ready")
        gdiag_ready, grow_ready = sem("gdiag_ready"), sem("grow_ready")
        sq_done, std_done, xn_done, tr_ready, tr_freed = (sem(n) for n in (
            "sq_done", "std_done", "xn_done", "tr_ready", "tr_freed"))
        post_sq, post_sum, post_std, post_done = (sem(n) for n in ("post_sq", "post_sum", "post_std", "post_done"))
        raw_ready, swap_ready, swap_freed, rope_done = (sem(n) for n in (
            "raw_ready", "swap_ready", "swap_freed", "rope_done"))
        bias_in = [sem(f"bias_in{i}") for i in range(3)]
        att_scores, att_biased, att_exp, att_probs, att_turned, att_copied, att_out, att_stored = (sem(n) for n in (
            "att_scores", "att_biased", "att_exp", "att_probs", "att_turned", "att_copied", "att_out", "att_stored"))

        counts = {}

        def stepper(eng, s):
            def link(ins):
                counts[id(s)] = counts.get(id(s), 0) + 1
                ins.then_inc(s, 1)
                eng.wait_ge(s, counts[id(s)])
            return link

        barriers = {}

        def end_stage(eng, who):
            barriers[who] = barriers.get(who, 0) + 1
            eng.drain().then_inc(stage_end, 1)
            eng.wait_ge(stage_end, 4 * barriers[who])

        ADA_AFTER = {"q0": (("ada4", 1),), "k0": (("ada5", 1),), "v0": (("ada6", 1), ("ada7", 1)),
                     "q1": (("ada8", 1),), "k1": (("ada9", 1),), "v1": (("ada10", 1), ("ada11", 1))}
        GROUP, groups = {}, 0
        for name, n in ([(n, c) for h in (0, 1) for t in "qkv" for n, c in ((f"{t}{h}", 4),) + ADA_AFTER[f"{t}{h}"]] + [("dt", 1)]
                        + [(f"{t}{g}", n) for g in range(SSD_G) for t, n in (("xs", 4), ("bc", 2), ("z", 4))]
                        + [("gates", 16), ("na", 8), ("ssd", 8)]
                        + [("aq", 4), ("ak", 4), ("av", 2), ("bq", 4), ("bk", 4), ("bv", 2), ("up0", 32), ("ple0", 8)]
                        + [("cin", 4), ("qi", 8), ("uk", 8), ("uv", 4), ("uq", 16), ("up1", 32), ("ple1", 8)]):
            GROUP[name] = groups
            groups += n

        CHUNK, chunks = {}, []
        used = [0]

        def chunk(name, src, kt, n, released=None):
            if released is None:
                used[0] += 1
                released = (chunk_used, used[0])
            CHUNK[name] = len(chunks)
            chunks.append((src, kt, n, released))

        def rows_of(w, k0, k1, c0, c1):
            return w[k0:k1, c0:c1].rearrange("(t p) n -> p t n", p=P)

        def ada_chunk(i, released):
            chunk(f"ada{i}", rows_of(d["w_ada"], 0, D, 512 * i, 512 * i + 512), KT, 512, released)

        for i in range(ADA_FIRST):
            ada_chunk(i, (ada_ready, i + 1))

        def win(name, c0, n, group_end):
            chunk(name, rows_of(d["w_in"], 0, D, c0, c0 + n), KT, n, (gemm_ready, group_end))

        for h in (0, 1):
            for i, t in enumerate("qkv"):
                win(f"{t}{h}", i * D + 512 * h, 512, GROUP[f"{t}{h}"] + 4)
                for n, _ in ADA_AFTER[f"{t}{h}"]:
                    ada_chunk(int(n[3:]), (gemm_ready, GROUP[n] + 1))
        Z0, X0, DT0 = 3 * D, 3 * D + SSD_W, 3 * D + SSD_W + SSD_W + 2 * SSD_G * SSD_N
        G0 = DT0 + 2 * SSD_HEADS
        win("dt", DT0, 2 * SSD_HEADS, GROUP["dt"] + 1)
        for g in range(SSD_G):
            win(f"xs{g}", X0 + 512 * g, 512, GROUP[f"xs{g}"] + 4)
            b0 = X0 + SSD_W + SSD_N * g
            win(f"b{g}", b0, SSD_N, GROUP[f"bc{g}"] + 1)
            win(f"c{g}", b0 + SSD_G * SSD_N, SSD_N, GROUP[f"bc{g}"] + 2)
            win(f"z{g}", Z0 + 512 * g, 512, GROUP[f"z{g}"] + 4)
        for i in range(4):
            win(f"gates{i}", G0 + 512 * i, 512, GROUP["gates"] + 4 * i + 4)
        for i in range(2):
            chunk(f"na{i}", rows_of(d["w_na"], 0, D, 512 * i, 512 * i + 512), KT, 512, (gemm_ready, GROUP["na"] + 4 * i + 4))
        for i in range(2):
            for k in range(2):
                chunk(f"ssd{i}{k}", rows_of(d["w_ssd"], D * k, D * k + D, 512 * i, 512 * i + 512), KT, 512,
                      (gemm_ready, GROUP["ssd"] + 4 * i + 4) if k else None)
        ROWS = {}
        nrows = [0]

        def rows_chunks(name, w, k):
            ROWS[name] = nrows[0]
            nrows[0] += 4
            for i in range(k):
                for h in range(2):
                    chunk(f"{name}{i}{h}", rows_of(w, D * i, D * i + D, 512 * h, 512 * h + 512), KT, 512,
                          (rows_ready, ROWS[name] + 2 * h + 2) if i == k - 1 else None)

        rows_chunks("out", d["w_out"], 1)
        FIRST_EXPERT = len(chunks)
        chunks_before = list(chunks)
        chunks.extend([None] * (12 * NE))

        def second_layer_chunks(l, w_o):
            rows_chunks(f"o{l}", w_o, 1)
            for i in range(8):
                chunk(f"up{l}{i}", rows_of(d["w_mlp_in"][l], 0, D, 512 * i, 512 * i + 512), KT, 512,
                      (gemm_ready, GROUP[f"up{l}"] + 4 * i + 4))
            rows_chunks(f"dn{l}", d["w_mlp_out"][l], 4)
            for i in range(2):
                chunk(f"pg{l}{i}", rows_of(d["w_ple_gate"][l], 0, D, 512 * i, 512 * i + 512), KT, 512,
                      (gemm_ready, GROUP[f"ple{l}"] + 2 * i + 2))
            chunk(f"pp{l}", rows_of(d["w_ple_proj"][l], 0, 256, 0, D), 2, D, (gemm_ready, GROUP[f"ple{l}"] + 8))

        for i, (n, c) in enumerate((("aq", 4), ("ak", 4), ("av", 2), ("bq", 4), ("bk", 4), ("bv", 2))):
            chunk(n, rows_of(d["w_ab"], 0, D, 512 * i, 512 * i + 512), KT, 512, (gemm_ready, GROUP[n] + c))
        second_layer_chunks(0, d["w_oab"])
        chunk("cin0", rows_of(d["w_c"], 0, D, 0, 512), KT, 512, (gemm_ready, GROUP["cin"] + 2))
        chunk("cin1", rows_of(d["w_c"], 0, D, 512, 744), KT, 232, (gemm_ready, GROUP["cin"] + 4))
        chunk("qi", rows_of(d["w_qi"], 0, CQ, 0, D), 3, D, (gemm_ready, GROUP["qi"] + IDX_HEADS))
        chunk("uk", rows_of(d["w_uk"], 0, CKV, 0, D), 2, D, (gemm_ready, GROUP["uk"] + C_HEADS // 2))
        chunk("uv", rows_of(d["w_uv"], 0, CKV, 0, D), 2, D, (gemm_ready, GROUP["uv"] + 4))
        for i in range(2):
            chunk(f"uq{i}", rows_of(d["w_uq"], 0, CQ, D * i, D * i + D), 3, D, (gemm_ready, GROUP["uq"] + 8 * i + 8))
        second_layer_chunks(1, d["w_oc"])

        def slot(name):
            c = CHUNK[name]
            _, kt, n, _ = chunks[c]
            return ring[:, c % SLOTS, 0:kt * n].rearrange("p (t n) -> p t n", t=kt)

        EXPERT_USES = 12 // SLOTS
        assert 12 % SLOTS == 0

        def wait_chunk(pe, name):
            c = CHUNK[name]
            pe.wait_ge(slot_full[c % SLOTS], 16 * (c // SLOTS + 1))


        def feat_groups(pe, name, blocks, act, t0, t1, first, n_groups):
            w = slot(name)
            wait_chunk(pe, name)
            kt = chunks[CHUNK[name]][1]
            for i in range(n_groups):
                n = first + i
                if n >= 4:
                    pe.wait_ge(gemm_freed, n - 3)
                for k in range(kt):
                    last = pe.matmul(bank[n % 4][:, 0:t1 - t0], w[:, k, (blocks + i) * P:(blocks + i + 1) * P],
                                     act[:, k, t0:t1], start=k == 0, stop=k == kt - 1)
                last.then_inc(gemm_ready, 1)

        def token_groups(pe, name, act, tiles, width, first):
            w = slot(name)
            wait_chunk(pe, name)
            kt = chunks[CHUNK[name]][1]
            for i in range(tiles):
                n = first + i
                if n >= 4:
                    pe.wait_ge(gemm_freed, n - 3)
                for k in range(kt):
                    last = pe.matmul(bank[n % 4][:, 0:width], act[:, k, i * P:(i + 1) * P], w[:, k, 0:width],
                                     start=k == 0, stop=k == kt - 1)
                last.then_inc(gemm_ready, 1)

        def rows_product(pe, name, act, k):
            for i in range(k):
                for h in range(2):
                    w = slot(f"{name}{i}{h}")
                    wait_chunk(pe, f"{name}{i}{h}")
                    for t in range(TT):
                        for kk in range(KT):
                            last = pe.matmul(bank[4 + 2 * h + t][:, :], act[:, KT * i + kk, t * P:(t + 1) * P], w[:, kk, :],
                                             start=i == 0 and kk == 0, stop=i == k - 1 and kk == KT - 1)
                        if i == k - 1:
                            last.then_inc(rows_ready, 1)
                    if i < k - 1:
                        last.then_inc(chunk_used, 1)

        nrm = {"act": [0, 0], "dve": [0, 0, 0], "pe": [0, 0, 0]}

        def norm_act(act, src, junk):
            link = stepper(act, act_step)
            n = len(src)
            for i, s in enumerate(src):
                act.activation(junk[i], s, ACT.Square, accum_out=small[:, i:i + 1]).then_inc(sq_done, 1)
            nrm["act"][0] += n
            act.wait_ge(sq_done, nrm["act"][0])
            act.activation(small[:, 8:8 + n], small[:, 0:n], ACT.Sqrt, bias=epsc[:, :], scale=1.0 / D).then_inc(std_done, 1)

        def norm_dve(dve, src, xn):
            link = stepper(dve, dve_step)
            n = len(src)
            nrm["dve"][0] += 1
            dve.wait_ge(std_done, nrm["dve"][0])
            link(dve.reciprocal(small[:, 16:16 + n], small[:, 8:8 + n]))
            for i, s in enumerate(src):
                dve.tensor_scalar(xn[i], s, small[:, 16 + i:17 + i], None, ALU.mult).then_inc(xn_done, 1)

        def turn_pe(pe, xn, normed=True):
            n = len(xn)
            if normed:
                nrm["pe"][0] += n
                pe.wait_ge(xn_done, nrm["pe"][0])
            for k in range(KT):
                g = nrm["pe"][1]
                nrm["pe"][1] += 1
                if g >= 2:
                    pe.wait_ge(tr_freed, g - 1)
                for i in range(n):
                    last = pe.transpose(bank[g % 2][:, i * P:(i + 1) * P], xn[i][:, k * P:(k + 1) * P], ident)
                last.then_inc(tr_ready, 1)

        def turned_dve(dve, dst, mul=None, add=None, tokens=L):
            for k in range(KT):
                g = nrm["dve"][1]
                nrm["dve"][1] += 1
                dve.wait_ge(tr_ready, g + 1)
                if mul is None:
                    ins = dve.tensor_copy(dst[:, k, :], bank[g % 2][:, 0:tokens])
                elif add is None:
                    ins = dve.tensor_scalar(dst[:, k, :], bank[g % 2][:, 0:tokens], mul[:, k:k + 1], None, ALU.mult)
                else:
                    ins = dve.tensor_scalar(dst[:, k, :], bank[g % 2][:, 0:tokens], mul[:, k:k + 1], add[:, k:k + 1],
                                            ALU.mult, ALU.add)
                ins.then_inc(tr_freed, 1)

        posts = {"act": 0, "dve": 0, "pool": 0}

        def post_act(act, ready, counts_of, junk):
            link = stepper(act, act_step)
            u = posts["act"]
            posts["act"] += 1
            for j in range(4):
                act.wait_ge(ready, counts_of[j])
                act.activation(junk[:, j, :], bank[4 + j][:, :], ACT.Square, accum_out=small[:, 32 + j:33 + j]).then_inc(post_sq, 1)
            act.wait_ge(post_sum, u + 1)
            act.activation(small[:, 40:42], small[:, 36:38], ACT.Sqrt, bias=epsc[:, :], scale=1.0 / D).then_inc(post_std, 1)

        def post_dve(dve, tmp):
            link = stepper(dve, dve_step)
            u = posts["dve"]
            posts["dve"] += 1
            dve.wait_ge(post_sq, 4 * u + 4)
            dve.tensor_tensor(small[:, 36:38], small[:, 32:34], small[:, 34:36], ALU.add).then_inc(post_sum, 1)
            dve.wait_ge(post_std, u + 1)
            link(dve.reciprocal(small[:, 44:46], small[:, 40:42]))
            for j in range(4):
                h, t = j // 2, j % 2
                link(dve.scalar_tensor_tensor(tmp[:, j, :], bank[4 + j][:, :], small[:, 44 + t:45 + t],
                                              grow[:, 512 * h:512 * h + 512], ALU.mult, ALU.mult))
                x = xres[:, t, 512 * h:512 * h + 512]
                dve.tensor_tensor(x, x, tmp[:, j, :], ALU.add).then_inc(post_done, 1)
            dve.wait_ge(post_done, posts["dve"] * 4)

        r1 = Region()
        hT = r1.take(KT, 2 * L)
        xn1 = r1.take(4, D)
        ctx_in = r1.take(TT, D)
        cc = r1.take(KT, 2)
        ada_rows = r1.take(ADA_FIRST, 512)
        AFTER_H = KT * 2 * L
        x_tiles = [xres[:, t, :] for t in range(TT)] + [ctx_in[:, t, :] for t in range(TT)]

        def ada_act(act):
            act.dma_start(xres[:, :, :], d["x"].rearrange("(t p) n -> p t n", p=P)).then_inc(x_in, 16)
            act.dma_start(ctx_in, d["ctx"].rearrange("(t p) n -> p t n", p=P)).then_inc(x_in, 16)
            act.wait_ge(consts_in, 16 * N_CONSTS)
            act.wait_ge(pads_ready, 1)
            act.activation(sT[:, :, 0:2], cc, ACT.Silu).then_inc(sT_ready, 1)
            act.wait_ge(x_in, 32)
            act.wait_ge(eps_ready, 1)
            norm_act(act, x_tiles, [xn1[:, i, :] for i in range(4)])

        def ada_set(pe, i, b):
            wait_chunk(pe, f"ada{i}")
            w = slot(f"ada{i}")
            for k in range(KT):
                j = k % 4
                last = pe.matmul(b[32 * j:32 * j + 32, :], sT[:, k, :], w[:, k, :], start=k < 4, stop=k >= 4, tile_position=(0, 32 * j))
            return last

        def ada_turn(pe, first, n, rows, b):
            for i in range(4 * n):
                last = pe.matmul(b[:, 2 * i:2 * i + 2], rows[:, i // 4, (i % 4) * P:(i % 4 + 1) * P], pick[:, :], start=True, stop=True)
            last.then_inc(ada_cols, 1)

        def ada_pe(pe):
            pe.wait_ge(sT_ready, 1)
            for i in range(ADA_FIRST):
                ada_set(pe, i, bank[i]).then_inc(ada_ready, 1)
            pe.wait_ge(ada_copied, ADA_FIRST)
            ada_turn(pe, 0, ADA_FIRST, ada_rows, bank[4])
            turn_pe(pe, [xn1[:, i, :] for i in range(4)])

        def ada_dve(dve):
            link = stepper(dve, dve_step)
            dve.memset(epsc[:, :], EPS).then_inc(eps_ready, 1)
            dve.memset(sT[:, :, :], 0.0).then_inc(pads_ready, 1)
            dve.wait_ge(consts_in, 16 * N_CONSTS)
            p4 = ident.rearrange("p (j i) -> p i j", i=32)
            link(dve.tensor_reduce(pick[:, :], p4[:, 0:2, :], AX.X, ALU.add))
            dve.wait_ge(x_in, 32)
            norm_dve(dve, x_tiles, [xn1[:, i, :] for i in range(4)])
            for i in range(ADA_FIRST):
                dve.wait_ge(ada_ready, i + 1)
                dve.tensor_copy(ada_rows[:, i, :], bank[i][:, :]).then_inc(ada_copied, 1)
            dve.wait_ge(ada_cols, 1)
            n = 4 * ADA_FIRST
            cols = bank[4][:, 0:2 * n].rearrange("p (b i) -> p i b", i=2)
            link(dve.tensor_tensor(mod[:, 0:n], cols[:, 0, :], pc("b_ada", 0, n), ALU.add))
            link(dve.tensor_tensor(modc[:, :], cols[:, 1, :], pc("b_ada", 0, n), ALU.add))
            link(dve.scalar_tensor_tensor(mul1[:, 0, :], mod[:, 8:16], 1.0, pc("pre_mix", 0, 8), ALU.add, ALU.mult))
            link(dve.scalar_tensor_tensor(mul1[:, 1, :], modc[:, 8:16], 1.0, pc("pre_mix", 0, 8), ALU.add, ALU.mult))
            for k in range(KT):
                g = nrm["dve"][1]
                nrm["dve"][1] += 1
                dve.wait_ge(tr_ready, g + 1)
                link(dve.tensor_scalar(hT[:, k, 0:L], bank[g % 2][:, 0:L], mul1[:, 0, k:k + 1], mod[:, k:k + 1], ALU.mult, ALU.add))
                dve.tensor_scalar(hT[:, k, L:2 * L], bank[g % 2][:, L:2 * L], mul1[:, 1, k:k + 1], modc[:, k:k + 1],
                                  ALU.mult, ALU.add).then_inc(tr_freed, 1)

        def ada_rest_pe(pe):
            pe.wait_ge(gemm_freed, GROUP["ada11"] + 1)
            ada_turn(pe, ADA_FIRST, 12 - ADA_FIRST, ada_more, bank[7])

        def ada_rest_dve(dve):
            link = stepper(dve, dve_step)
            dve.wait_ge(ada_cols, 2)
            n0 = 4 * ADA_FIRST
            cols = bank[7][:, 0:2 * (48 - n0)].rearrange("p (b i) -> p i b", i=2)
            link(dve.tensor_tensor(mod[:, n0:48], cols[:, 0, :], pc("b_ada", n0, 48 - n0), ALU.add))
            link(dve.scalar_tensor_tensor(mul2[:, :], mod[:, 32:40], 1.0, pc("pre_ffn", 0, 8), ALU.add, ALU.mult))
            link(dve.tensor_tensor(gain[:, 0, :], mod[:, 16:24], pc("post_mix", 0, 8), ALU.mult))
            link(dve.tensor_tensor(gain[:, 1, :], mod[:, 40:48], pc("post_ffn", 0, 8), ALU.mult))

        pick = sb("pick", [P, 2])

        def grow_dve_in(dve, i, gdiag):
            for k in range(KT):
                dve.tensor_scalar(gdiag[:, k, :], ident, gain[:, i, k:k + 1], None, ALU.mult).then_inc(gdiag_ready, 1)

        def grow_pe(pe, i, gdiag):
            pe.wait_ge(gdiag_ready, KT * (i + 1))
            for h in range(2):
                pe.matmul(bank[4 + h][:, :], ones, gdiag[:, 4 * h:4 * h + 4, :], start=True, stop=True).then_inc(grow_ready, 1)

        def grow_dve_out(dve, i):
            for h in range(2):
                dve.wait_ge(grow_ready, 2 * i + h + 1)
                dve.tensor_copy(grow[:, 512 * h:512 * h + 512], bank[4 + h][:, :]).then_inc(grow_in, 1)

        rope_n = {"act": 0, "pe": 0, "dve": 0}
        ROPE0 = WORK - 4 * L
        raw = work[:, ROPE0:ROPE0 + 2 * L].rearrange("p (i l) -> p i l", i=2)
        rp = work[:, ROPE0 + 2 * L:WORK].rearrange("p (i l) -> p i l", i=2)

        def rope_act(act, group, extra=None):
            n = rope_n["act"]
            rope_n["act"] += 1
            act.wait_ge(gemm_ready, group + 1)
            if n >= 2:
                act.wait_ge(rope_done, n - 1)
            if extra is not None:
                dst, src = extra
                link = stepper(act, act_step)
                link(act.copy(dst, src))
            act.copy(raw[:, n % 2, :], bank[group % 4][:, 0:L]).then_inc(gemm_freed, 1)

        def rope_pe(pe, group, swap):
            n = rope_n["pe"]
            rope_n["pe"] += 1
            pe.wait_ge(gemm_freed, group + 1)
            if n >= 2:
                pe.wait_ge(swap_freed, n - 1)
            pe.matmul(bank[4 + n % 2][:, 0:L], cm(swap), raw[:, n % 2, :], start=True, stop=True).then_inc(swap_ready, 1)

        def rope_dve(dve, cos, sin, outs):
            link = stepper(dve, dve_step)
            n = rope_n["dve"]
            rope_n["dve"] += 1
            dve.wait_ge(swap_ready, n + 1)
            if n:
                dve.wait_ge(rope_done, n)
            link(dve.tensor_tensor(rp[:, 0, :], raw[:, n % 2, :], cos, ALU.mult))
            dve.tensor_tensor(rp[:, 1, :], bank[4 + n % 2][:, 0:L], sin, ALU.mult).then_inc(swap_freed, 1)
            dve.wait_ge(swap_freed, n + 1)
            for i, (dst, p0, p1) in enumerate(outs):
                ins = dve.tensor_tensor(dst, rp[p0:p1, 0, :], rp[p0:p1, 1, :], ALU.add)
                if i < len(outs) - 1:
                    link(ins)
            ins.then_inc(rope_done, 1)

        AHEAD = 3
        stat = sb("stat", [P, AHEAD, 4])
        counted = {"sets": 0, "units": 0, "values": 0}

        class Attention:

            def __init__(self, units, parts, width, bias, scale, s, pr, turned, turned_banks):
                self.units, self.parts, self.width, self.bias = units, parts, width, bias
                self.scale, self.s, self.pr, self.turned, self.turned_banks = scale, s, pr, turned, turned_banks
                self.sets, self.first = counted["sets"], counted["units"]
                counted["sets"] += units * parts
                counted["units"] += units

            def turned_bank(self, u):
                return bank[self.turned_banks[u % len(self.turned_banks)]]

            before_bias = staticmethod(lambda dve, i: None)

        def att_pe(pe, A, scores, value, between={}):
            n = A.units * A.parts
            for step in range(n + AHEAD + 2):
                if step in between:
                    between[step](pe)
                if step < n:
                    if step >= AHEAD:
                        pe.wait_ge(att_biased, A.sets + step - AHEAD + 1)
                    scores(pe, step, bank[step % AHEAD]).then_inc(att_scores, 1)
                i = step - AHEAD
                if 0 <= i < n and i % A.parts == A.parts - 1:
                    u = i // A.parts
                    pe.wait_ge(att_probs, A.first + u + 1)
                    back = len(A.turned_banks)
                    if u >= back:
                        pe.wait_ge(att_copied, A.first + u - back + 1)
                    for k in range(A.width(u) // P):
                        last = pe.transpose(A.turned_bank(u)[:, k * P:(k + 1) * P], A.pr[:, u % AHEAD, k * P:(k + 1) * P], ident)
                    last.then_inc(att_turned, 1)
                i = step - AHEAD - 2
                if 0 <= i < n and i % A.parts == A.parts - 1:
                    value(pe, i // A.parts)

        def att_dve(dve, A, after, lam_of=None):
            link = stepper(dve, dve_step)
            n = A.units * A.parts
            for step in range(n + AHEAD + 4):
                i = step
                if i < n:
                    A.before_bias(dve, i)
                    u, w = i // A.parts, A.width(i // A.parts)
                    dve.wait_ge(att_scores, A.sets + i + 1)
                    j = i - AHEAD
                    if j >= 0 and j % A.parts == A.parts - 1:
                        dve.wait_ge(att_probs, A.first + j // A.parts + 1)
                    st = stat[:, i % AHEAD, :]
                    link(dve.tensor_tensor_reduce(out=A.s[:, i % AHEAD, 0:w], in0=bank[i % AHEAD][:, 0:w], in1=A.bias(u), scale=1.0,
                                                  scalar=-3e38, op0=ALU.add, op1=ALU.max, accum_out=st[:, 0:1]))
                    dve.tensor_scalar(st[:, 1:2], st[:, 0:1], -A.scale, None, ALU.mult).then_inc(att_biased, 1)
                i = step - 1
                if 0 <= i < n:
                    u, w = i // A.parts, A.width(i // A.parts)
                    st = stat[:, i % AHEAD, :]
                    dve.wait_ge(att_exp, A.sets + i + 1)
                    link(dve.reciprocal(st[:, 3:4], st[:, 2:3]))
                    if i % A.parts == A.parts - 1 and u >= AHEAD:
                        dve.wait_ge(att_turned, A.first + u - AHEAD + 1)
                    e, pr = A.s[:, i % AHEAD, 0:w], A.pr[:, u % AHEAD, 0:w]
                    if A.parts == 1:
                        dve.tensor_scalar(pr, e, st[:, 3:4], None, ALU.mult).then_inc(att_probs, 1)
                    elif i % 2 == 0:
                        link(dve.tensor_scalar(lam_of[1][:, 0:w], e, st[:, 3:4], None, ALU.mult))
                    else:
                        link(dve.tensor_tensor(st[:, 3:4], st[:, 3:4], lam_of[0], ALU.mult))
                        dve.scalar_tensor_tensor(pr, e, st[:, 3:4], lam_of[1][:, 0:w], ALU.mult, ALU.add).then_inc(att_probs, 1)
                i = step - AHEAD - 4
                if 0 <= i < n and i % A.parts == A.parts - 1:
                    after(dve, i // A.parts)

        def att_act(act, A, turned_free):
            n = A.units * A.parts
            for step in range(n + AHEAD):
                i = step
                if i < n:
                    u, w = i // A.parts, A.width(i // A.parts)
                    st = stat[:, i % AHEAD, :]
                    act.wait_ge(att_biased, A.sets + i + 1)
                    s = A.s[:, i % AHEAD, 0:w]
                    act.activation(s, s, ACT.Exp, bias=st[:, 1:2], scale=A.scale, accum_out=st[:, 2:3]).then_inc(att_exp, 1)
                i = step - AHEAD
                if 0 <= i < n and i % A.parts == A.parts - 1:
                    u = i // A.parts
                    act.wait_ge(att_turned, A.first + u + 1)
                    turned_free(act, u)
                    k = A.width(u) // P
                    act.copy(A.turned(u), A.turned_bank(u)[:, 0:k * P].rearrange("p (k q) -> p k q", q=P)).then_inc(att_copied, 1)

        def head_values(A, v, PT, heads, causal, first, store):
            def value(pe, u):
                h, qt = u // 2, u % 2
                if qt == 0:
                    return
                blk, side = h // 2, h % 2
                pe.wait_ge(att_copied, A.first + u + 1)
                if side == 0 and blk >= 2:
                    pe.wait_ge(att_stored, first // 2 + blk - 1)
                n = A.width(1) // P
                o = bank[4 + blk % 2][64 * side:64 * side + 64, :]
                for k in range(n):
                    q0 = P if causal and k == 1 else 0
                    last = pe.matmul(o[:, q0:L], v[:, k, HD * h:HD * h + HD], PT[:, h % 2, k, q0:L], start=k == 0, stop=k == n - 1)
                last.then_inc(att_out, 1)

            def after(dve, u):
                h, qt = u // 2, u % 2
                if qt == 0 or h % 2 == 0:
                    return
                dve.wait_ge(att_out, first + h + 1)
                dve.tensor_copy(store(h // 2), bank[4 + (h // 2) % 2][:, 0:L]).then_inc(att_stored, 1)

            def turned_free(act, u):
                h = u // 2
                if h >= 2:
                    act.wait_ge(att_out, first + h - 1)
            counted["values"] += heads
            return value, after, turned_free

        r2 = Region(AFTER_H, ROPE0)
        oT = r2.take(KT, L)
        AFTER_O = r2.at
        qz = r2.take(4, 2, L)
        kT = r2.take(4, 2 * L)
        v_na = r2.take(4, 512)
        na_bias = r2.take(3, TT, 2 * L)
        s_na, pr_na, PT_na = r2.take(AHEAD, 512), r2.take(AHEAD, 512), r2.take(2, 4, L)
        ada_more = r2.take(12 - ADA_FIRST, 512)
        zero_ready = sem("zero_ready")

        NA = []
        for hf in (0, 1):
            A = Attention(16, 1, lambda u: 2 * L, lambda u, hf=hf: na_bias[:, (8 * hf + u // 2) % 3, u % 2, :], 1.0, s_na, pr_na,
                          lambda u: PT_na[:, (u // 2) % 2, :, (u % 2) * P:(u % 2 + 1) * P], (3, 6))

            def before(dve, i, hf=hf):
                h = 8 * hf + i // 2
                if i % 2 == 0:
                    dve.wait_ge(bias_in[h % 3], 16 * (h // 3 + 1))
            A.before_bias = before
            A.hooks = head_values(A, v_na, PT_na, 8, False, counted["values"], lambda blk, hf=hf: oT[:, 4 * hf + blk, :])
            NA.append(A)

        def na_proj_pe(pe, hf):
            def ada_sets(t):
                for name, _ in ADA_AFTER[f"{t}{hf}"]:
                    n = GROUP[name]
                    pe.wait_ge(gemm_freed, n - 3)
                    ada_set(pe, int(name[3:]), bank[n % 4]).then_inc(gemm_ready, 1)

            feat_groups(pe, f"q{hf}", 0, hT, 0, L, GROUP[f"q{hf}"], 4)
            ada_sets("q")
            for b in range(4):
                rope_pe(pe, GROUP[f"q{hf}"] + b, "swap16")
            feat_groups(pe, f"k{hf}", 0, hT, 0, 2 * L, GROUP[f"k{hf}"], 4)
            ada_sets("k")
            for b in range(4):
                rope_pe(pe, GROUP[f"k{hf}"] + b, "swap16")
            token_groups(pe, f"v{hf}", hT, 4, 512, GROUP[f"v{hf}"])
            ada_sets("v")

        def na_proj_act(act, hf):
            def ada_sets(t):
                for name, _ in ADA_AFTER[f"{t}{hf}"]:
                    n = GROUP[name]
                    act.wait_ge(gemm_ready, n + 1)
                    act.copy(ada_more[:, int(name[3:]) - ADA_FIRST, :], bank[n % 4][:, :]).then_inc(gemm_freed, 1)

            for b in range(4):
                rope_act(act, GROUP[f"q{hf}"] + b)
            ada_sets("q")
            for b in range(4):
                g = GROUP[f"k{hf}"] + b
                rope_act(act, g, (kT[:, b, L:2 * L], bank[g % 4][:, L:2 * L]))
            ada_sets("k")
            for i in range(4):
                g = GROUP[f"v{hf}"] + i
                act.wait_ge(gemm_ready, g + 1)
                act.copy(v_na[:, i, :], bank[g % 4][:, :]).then_inc(gemm_freed, 1)
            ada_sets("v")

        def na_proj_dve(dve, hf):
            link = stepper(dve, dve_step)
            if hf == 0:
                link(dve.memset(qz, 0.0))
            for b in range(4):
                rope_dve(dve, tb("na_qc"), tb("na_qs"), [(qz[0:64, b, 0, :], 0, 64), (qz[64:128, b, 1, :], 64, 128)])
            for b in range(4):
                rope_dve(dve, tb("na_kc"), tb("na_ks"), [(kT[:, b, 0:L], 0, 128)])

        def na_bias_pool(pool, hf, first, last):
            if hf == 0 and first == 0:
                pool.memset(na_bias, 0.0).then_inc(zero_ready, 1)
                pool.wait_ge(zero_ready, 1)
            for h in range(8 * hf + first, 8 * hf + last):
                if h >= 3:
                    pool.wait_ge(att_biased, 2 * (h - 2))
                pool.dma_start(na_bias[:, h % 3, :, 0:L], d["na_bias"][h]).then_inc(bias_in[h % 3], 16)

        def na_scores_of(hf):
            def scores(pe, u, b):
                h, qt = u // 2, u % 2
                return pe.matmul(b[:, :], qz[:, h // 2, h % 2, qt * P:(qt + 1) * P], kT[:, h // 2, :], start=True, stop=True)
            return scores

        r3 = Region(AFTER_O)
        yT = r3.take(16, L)
        AFTER_Y = r3.at
        dtv = r3.take(4, 64)
        nacs = r3.take(TT, 64)
        eacs = r3.take(TT, 64)
        wctx = r3.take(TT, 64)
        zs = r3.take(GB, L)
        cin = r3.take(2, 2, L + 4)
        cacc = r3.take(2, 2, L)
        conv = r3.take(5, 2, L)
        convC = r3.take(L)
        bst = r3.take(TT, P)
        xdt = r3.take(2, TT, GB * P)
        xw = r3.take(2, TT, GB * P)
        h0 = r3.take(2, GB * P)
        yoff = r3.take(TT, GB * P)
        yo2 = r3.take(GB * P)
        EMS = 3
        cbm = r3.take(6, P)
        Em = r3.take(EMS, 6, P)
        abc = r3.take(2, 2, L)
        ysq, rstd = r3.take(2, L), r3.take(L)
        sp = xdt.rearrange("p d t n -> p (d t n)")[:, 0:6 * 256].rearrange("p (i t h) -> p i t h", i=6, t=4)
        free = xw.rearrange("p d t n -> p (d t n)")
        av = free[:, 0:256].rearrange("p (t h) -> p t h", t=4)
        acs = free[:, 256:512].rearrange("p (t h) -> p t h", t=TT)
        AT = free[:, 512:768]
        nega = free[:, 768:832]
        sums = nc.dram_tensor("sums", (2, SSD_HEADS, L), F32).ap()
        TILES_OF = (((0, 0, 2, 0), (1, 2, 3, P)), ((0, 3, 4, 0), (1, 4, 6, 0)))
        (dt_abs, dt_exp, dt_one, dt_ln, dt_ready, acs_ready, acs_done, at_ready, wct_done, at_done, negA_done, ctxw_done,
         sums_out) = (sem(n) for n in (
            "dt_abs", "dt_exp", "dt_one", "dt_ln", "dt_ready", "acs_ready", "acs_done", "at_ready", "wct_done", "at_done",
            "negA_done", "ctxw_done", "sums_out"))
        (pad_zero, conv_done, conv_silu, xt_ready, xt_done, xw_done, h0_ready, h0_done, yoff_ready, yoff_done, cb_ready,
         cb_done, seg_added, seg_exp, seg_done, y_ready, y_gated, y_sq, y_tot, y_std, y_norm) = (sem(n) for n in (
             "pad_zero", "conv_done", "conv_silu", "xt_ready", "xt_done", "xw_done", "h0_ready", "h0_done", "yoff_ready",
             "yoff_done", "cb_ready", "cb_done", "seg_added", "seg_exp", "seg_done", "y_ready", "y_gated", "y_sq",
             "y_tot", "y_std", "y_norm"))
        seg_added_b = sem("seg_added_b")
        abc_in = [sem(f"abc_in{i}") for i in range(2)]
        XB = GB + 2

        def conv_of(b):
            return conv[:, b] if b < 5 else convC.unsqueeze(1)

        def x_block(pe, g, b):
            name, i, t1 = ((f"xs{g}", b, 2 * L), (f"b{g}", 0, 2 * L), (f"c{g}", 0, L))[max(0, b - GB + 1)]
            feat_groups(pe, name, i, hT, 0, t1, GROUP[f"xs{g}"] + b, 1)

        def dt_product(pe):
            w, n = slot("dt"), GROUP["dt"]
            wait_chunk(pe, "dt")
            if n >= 4:
                pe.wait_ge(gemm_freed, n - 3)
            for i in range(4):
                for k in range(KT):
                    last = pe.matmul(bank[n % 4][:, 64 * i:64 * i + 64], hT[:, k, i * P:(i + 1) * P], w[:, k, :],
                                     start=k == 0, stop=k == KT - 1)
            last.then_inc(gemm_ready, 1)

        def dt_sums(pe):
            pe.wait_ge(dt_ready, 1)
            F, B = slice(0, 32), slice(32, 64)

            def total(col, terms):
                for i, (m, tile, cols) in enumerate(terms):
                    r = pe.matmul(bank[4][:, col:col + 32], m, av[:, tile, cols], start=i == 0, stop=i == len(terms) - 1)
                return r
            le, ge, gt, lt = cm("le"), cm("ge"), cm("gt"), cm("lt")
            total(0, [(le, 0, F)])
            total(32, [(ge, 0, B), (ones, 1, B)])
            total(64, [(le, 1, F), (ones, 0, F)])
            total(96, [(ge, 1, B)])
            total(128, [(gt, 2, F), (ones, 3, F)])
            total(160, [(lt, 2, B)])
            total(192, [(gt, 3, F)])
            total(224, [(lt, 3, B), (ones, 2, B)]).then_inc(acs_ready, 1)

        def dt_turn(pe):
            pe.wait_ge(acs_done, 1)
            for t in range(TT):
                last = pe.transpose(bank[5][:, t * P:(t + 1) * P], acs[:, t, :], ident)
            last.then_inc(at_ready, 1)

        def dt_act(act):
            act.activation(nega, heads[:, 0:64], ACT.Exp).then_inc(negA_done, 1)
            act.wait_ge(dt_abs, 1)
            act.activation(sp[:, 2], sp[:, 1], ACT.Exp).then_inc(dt_exp, 1)
            act.wait_ge(dt_one, 1)
            act.activation(sp[:, 4], sp[:, 3], ACT.Ln).then_inc(dt_ln, 1)

        def sums_act(act):
            act.wait_ge(acs_ready, 1)
            act.wait_ge(acs_done, 1)
            b = bank[4]
            act.activation(eacs, b[:, 0:128].rearrange("p (t h) -> p t h", t=TT), ACT.Exp).then_inc(ctxw_done, 1)
            act.activation(wctx, b[:, 128:256].rearrange("p (t h) -> p t h", t=TT), ACT.Exp).then_inc(ctxw_done, 1)

        def dt_dve(dve):
            link = stepper(dve, dve_step)
            n = GROUP["dt"]
            x, na, e, u, ln, t = (sp[:, i] for i in range(6))
            link(dve.memset(acs, 0.0))
            dve.wait_ge(gemm_ready, n + 1)
            ps = bank[n % 4][:, 0:256].rearrange("p (t h) -> p t h", t=4)
            dve.tensor_tensor(x, ps, heads[:, 64:128].unsqueeze(1).broadcast_to([P, 4, 64]), ALU.add).then_inc(gemm_freed, 1)
            dve.wait_ge(gemm_freed, n + 1)
            dve.scalar_tensor_tensor(na, x, -1.0, x, ALU.mult, ALU.min).then_inc(dt_abs, 1)
            dve.wait_ge(dt_exp, 1)
            dve.tensor_scalar(u, e, 1.0, None, ALU.add).then_inc(dt_one, 1)
            dve.wait_ge(dt_one, 1)
            link(dve.tensor_scalar(t, u, 1.0, None, ALU.is_equal))
            link(dve.scalar_tensor_tensor(na, u, -1.0, t, ALU.add, ALU.add))
            link(dve.reciprocal(na, na))
            link(dve.tensor_tensor(na, na, e, ALU.mult))
            dve.wait_ge(dt_ln, 1)
            link(dve.tensor_tensor(na, na, ln, ALU.mult))
            link(dve.tensor_tensor(t, t, e, ALU.mult))
            link(dve.tensor_tensor(na, na, t, ALU.add))
            link(dve.scalar_tensor_tensor(dtv, x, 0.0, na, ALU.max, ALU.add))
            dve.wait_ge(negA_done, 1)
            dve.scalar_tensor_tensor(av, dtv, -1.0, nega.unsqueeze(1).broadcast_to([P, 4, 64]), ALU.mult, ALU.mult).then_inc(dt_ready, 1)

        def sums_dve(dve):
            link = stepper(dve, dve_step)
            dve.wait_ge(acs_ready, 1)
            ps = bank[4][:, 0:128].rearrange("p (t h) -> p t h", t=TT)
            link(dve.tensor_scalar(nacs, ps, -1.0, None, ALU.mult))
            dve.tensor_copy(acs[:, :, 0:64], ps).then_inc(acs_done, 1)
            dve.wait_ge(ctxw_done, 2)
            dve.tensor_tensor(wctx, wctx, dtv[:, 2:4, :], ALU.mult).then_inc(wct_done, 1)
            dve.wait_ge(at_ready, 1)
            dve.tensor_copy(AT, bank[5][:, 0:L]).then_inc(at_done, 1)

        def add_decays(eng, n, dr, done):
            eng.wait_ge(abc_in[n % 2], 16 * (n // 2 + 1))
            if n >= EMS:
                eng.wait_ge(y_ready, n - EMS + 1)
            for s, c0, c1, l0 in TILES_OF[dr]:
                c = 32 * dr + n
                eng.tensor_scalar(Em[:, n % EMS, c0:c1, :].rearrange("p c l -> p (c l)"), abc[:, n % 2, dr, l0:l0 + (c1 - c0) * P],
                                  nacs[:, s, c:c + 1], 0.0, ALU.add, ALU.min).then_inc(done, 1)

        def ssd_pool(pool):
            pool.wait_ge(at_done, 1)
            pool.dma_start(sums.rearrange("d h l -> (d h) l"), AT[0:64, :]).then_inc(sums_out, 16)
            pool.wait_ge(sums_out, 16)
            for n in range(SSD_HEADS + 2):
                if n >= 2:
                    add_decays(pool, n - 2, 1, seg_added_b)
                if n < SSD_HEADS:
                    if n >= 2:
                        pool.wait_ge(seg_added, 2 * n - 2)
                        pool.wait_ge(seg_added_b, 2 * n - 2)
                    pool.dma_start(abc[:, n % 2], sums[:, n, :].partition_broadcast(P)).then_inc(abc_in[n % 2], 16)

        def product(pe, g, r):
            n = GH * g + r
            blk, side = r // 2, r % 2
            nb = GB * g + blk
            o = bank[4 + blk % 2]
            if side == 0:
                pe.wait_ge(yoff_done, 2 * g + 2)
                if blk >= 2:
                    pe.wait_ge(y_gated, nb - 1)
                for t in range(TT):
                    pe.matmul(o[:, t * P:(t + 1) * P], yoff[:, t, blk * P:(blk + 1) * P], ident, start=t == 0, stop=False,
                              skip_group_check=True)
            pe.wait_ge(seg_done, n + 1)
            oh = o[64 * side:64 * side + 64, :]
            for dr in range(2):
                for s, c0, c1, l0 in TILES_OF[dr]:
                    last = pe.matmul(oh[:, l0:l0 + (c1 - c0) * P], xdt[:, dr, s, r * HD:(r + 1) * HD], Em[:, n % EMS, c0:c1, :],
                                     start=False, stop=True, skip_group_check=True)
            last.then_inc(y_ready, 1)

        def squares_sum(pe, g):
            for blk in range(GB):
                pe.wait_ge(y_sq, GB * g + blk + 1)
                pe.matmul(bank[6][:, 0:L], ones, ysq[:, blk % 2, :], start=blk == 0, stop=blk == GB - 1).then_inc(y_tot, 1)

        def ssd_pe(pe):
            dt_product(pe)
            for g in range(SSD_G + 1):
                for i in range(GH):
                    if g < SSD_G and i < XB:
                        x_block(pe, g, i)
                    if g:
                        product(pe, g - 1, i)
                    elif i == 1:
                        dt_sums(pe)
                    elif i == 2:
                        dt_turn(pe)
                if g == SSD_G:
                    squares_sum(pe, g - 1)
                    break

                def gate_block(b, g=g):
                    feat_groups(pe, f"z{g}", b, hT, 0, L, GROUP[f"z{g}"] + b, 1)

                def turn(i, g=g):
                    n = 5 * g + i
                    pe.wait_ge(conv_silu, XB * g + (GB + 1 if i == 4 else GB))
                    if i >= 2:
                        pe.wait_ge(xt_done, n - 1)
                    elif g:
                        pe.wait_ge(yoff_done, 2 * g)
                    for b in range(GB if i < 4 else TT):
                        src = conv[:, b, i // 2, (i % 2) * P:(i % 2 + 1) * P] if i < 4 else conv[:, 4, 1, b * P:(b + 1) * P]
                        last = pe.transpose(bank[6 + i % 2][:, b * P:(b + 1) * P], src, ident)
                    last.then_inc(xt_ready, 1)

                gate_block(0)
                turn(0)
                turn(1)
                gate_block(1)
                turn(2)
                turn(3)
                turn(4)
                gate_block(2)
                pe.wait_ge(conv_silu, XB * g + XB)
                pe.wait_ge(xt_done, 5 * g + 4)
                for s in range(TT):
                    last = pe.matmul(bank[7][:, s * L:(s + 1) * L], conv[:, 4, 0, s * P:(s + 1) * P], convC, start=True, stop=True)
                last.then_inc(cb_ready, 1)
                pe.wait_ge(xt_done, 5 * g + 5)
                for dr in range(2):
                    if dr == 1:
                        pe.wait_ge(cb_done, g + 1)
                    for t in range(TT):
                        pe.wait_ge(xw_done, 4 * g + 2 * t + dr + 1)
                        last = pe.matmul(bank[6 + dr][:, :], bst[:, t, :], xw[:, dr, t, :], start=t == 0, stop=t == TT - 1)
                    last.then_inc(h0_ready, 1)
                gate_block(3)
                pe.wait_ge(h0_done, 2 * g + 2)
                if g:
                    squares_sum(pe, g - 1)
                    pe.wait_ge(y_gated, GB * g)
                for t in range(TT):
                    if t and g:
                        pe.wait_ge(y_std, g)
                    for dr in range(2):
                        last = pe.matmul(bank[4 + 2 * t + dr][:, :], convC[:, t * P:(t + 1) * P], h0[:, dr, :], start=True, stop=True)
                    last.then_inc(yoff_ready, 1)

        def ssd_act(act):
            def head_exp(n):
                act.wait_ge(seg_added, 2 * n + 2)
                act.wait_ge(seg_added_b, 2 * n + 2)
                act.activation(Em[:, n % EMS], Em[:, n % EMS], ACT.Exp).then_inc(seg_exp, 1)

            def take_block(g, b):
                m = XB * g + b
                n = GROUP[f"xs{g}"] + b
                act.wait_ge(gemm_ready, n + 1)
                act.wait_ge(pad_zero, 1)
                if m >= 2:
                    act.wait_ge(conv_done, m - 1)
                s = 2 if b < 5 else 1
                act.copy(cin[:, m % 2, 0:s, 2:L + 2], bank[n % 4][:, 0:s * L].rearrange("p (s l) -> p s l", s=s)).then_inc(gemm_freed, 1)

            def silu(g, b):
                m = XB * g + b
                act.wait_ge(conv_done, m + 1)
                if g:
                    act.wait_ge(yoff_ready, 2 * g)
                s = 2 if b < 5 else 1
                act.activation(conv_of(b), cacc[:, m % 2, 0:s], ACT.Silu).then_inc(conv_silu, 1)

            def squares(g):
                for blk in range(GB):
                    nb = GB * g + blk
                    act.wait_ge(y_gated, nb + 1)
                    if nb >= 2:
                        act.wait_ge(y_tot, nb - 1)
                    act.activation(ysq[:, blk % 2, :], yT[:, nb, :], ACT.Square).then_inc(y_sq, 1)
                act.wait_ge(y_tot, GB * g + GB)
                if g:
                    act.wait_ge(y_norm, GB * g)
                act.activation(rstd, bank[6][:, 0:L], ACT.Sqrt, bias=epsc[:, :], scale=1.0 / (GB * P)).then_inc(y_std, 1)

            dt_act(act)
            for g in range(SSD_G + 1):
                for i in range(GH):
                    if g:
                        head_exp(GH * (g - 1) + i)
                    if g < SSD_G and i < XB:
                        take_block(g, i)
                        if i:
                            silu(g, i - 1)
                    if g == 0 and i == 1:
                        sums_act(act)
                if g == SSD_G:
                    squares(g - 1)
                    break
                silu(g, XB - 1)

                def gate(b, g=g):
                    n = GROUP[f"z{g}"] + b
                    act.wait_ge(gemm_ready, n + 1)
                    if b == 0 and g:
                        act.wait_ge(y_gated, GB * g)
                    act.activation(zs[:, b, :], bank[n % 4][:, 0:L], ACT.Silu).then_inc(gemm_freed, 1)
                gate(0)
                gate(1)
                act.wait_ge(xt_ready, 5 * g + 5)
                act.wait_ge(xt_done, 5 * g + 4)
                act.copy(bst, bank[6][:, 0:2 * P].rearrange("p (t n) -> p t n", t=TT)).then_inc(xt_done, 1)
                gate(2)
                for dr in range(2):
                    act.wait_ge(h0_ready, 2 * g + dr + 1)
                    act.copy(h0[:, dr, :], bank[6 + dr][:, :]).then_inc(h0_done, 1)
                gate(3)
                if g:
                    squares(g - 1)

        def ssd_dve(dve):
            link = stepper(dve, dve_step)


            def mask_head(n):
                dve.wait_ge(seg_exp, n + 1)
                dve.tensor_tensor(Em[:, n % EMS], Em[:, n % EMS], cbm, ALU.mult).then_inc(seg_done, 1)

            def convolve(g, b):
                m = XB * g + b
                dve.wait_ge(gemm_freed, GROUP[f"xs{g}"] + b + 1)
                if m >= 2:
                    dve.wait_ge(conv_silu, m - 1)
                s = 2 if b < 5 else 1
                c, x = cacc[:, m % 2, 0:s], cin[:, m % 2, 0:s]
                link(dve.tensor_scalar(c, x[:, :, 0:L], pc("conv_w", m * CONV), pc("conv_b", m), ALU.mult, ALU.add))
                for k in range(1, CONV):
                    ins = dve.scalar_tensor_tensor(c, x[:, :, k:k + L], pc("conv_w", m * CONV + k), c, ALU.mult, ALU.add)
                    if k < CONV - 1:
                        link(ins)
                ins.then_inc(conv_done, 1)

            def gate_heads(g, blk):
                nb = GB * g + blk
                dve.wait_ge(y_ready, GH * g + 2 * blk + 2)
                dve.tensor_tensor(yT[:, nb, :], bank[4 + blk % 2][:, 0:L], zs[:, blk, :], ALU.mult).then_inc(y_gated, 1)

            def per_head(v):
                return v.rearrange("p (r d) -> p r d", r=GH)

            def spread(v):
                return v.unsqueeze(2).broadcast_to([P, GH, HD])

            dve.memset(cin, 0.0).then_inc(pad_zero, 1)
            dt_dve(dve)
            for g in range(SSD_G + 1):
                if g:
                    add_decays(dve, GH * (g - 1), 0, seg_added)
                for i in range(GH):
                    if g:
                        if i + 1 < GH:
                            add_decays(dve, GH * (g - 1) + i + 1, 0, seg_added)
                        mask_head(GH * (g - 1) + i)
                        if i >= 3 and i % 2 == 1:
                            gate_heads(g - 1, (i - 3) // 2)
                    if g < SSD_G and i < XB:
                        convolve(g, i)
                    if g == 0 and i == 1:
                        sums_dve(dve)
                if g:
                    gate_heads(g - 1, GB - 1)
                if g < SSD_G:
                    for i in range(4):
                        dve.wait_ge(xt_ready, 5 * g + i + 1)
                        src = per_head(bank[6 + i % 2][:, :])
                        if i < 2:
                            if g and i == 0:
                                dve.wait_ge(y_ready, GH * g)
                            elif i == 0:
                                dve.wait_ge(sums_out, 16)
                            link(dve.tensor_tensor(per_head(yoff[:, i, :]), src,
                                                   spread(heads[:, SKIP0 + GH * g:SKIP0 + GH * g + GH]), ALU.mult))
                        for dr in range(2):
                            h = slice(32 * dr + GH * g, 32 * dr + GH * g + GH)
                            if i < 2:
                                ins = dve.tensor_tensor(per_head(xdt[:, dr, i, :]), src, spread(dtv[:, i, h]), ALU.mult)
                                if dr == 0:
                                    link(ins)
                            else:
                                ins = dve.tensor_tensor(per_head(xw[:, dr, i - 2, :]), src, spread(wctx[:, i - 2, h]), ALU.mult)
                                ins.then_inc(xw_done, 1)
                        if i >= 2:
                            dve.wait_ge(xw_done, 4 * g + 2 * (i - 1))
                            ins = dve.drain()
                        ins.then_inc(xt_done, 1)
                    dve.wait_ge(cb_ready, g + 1)
                    if g:
                        dve.wait_ge(seg_done, GH * g)
                    cb = bank[7]
                    le, ge = cm("le"), cm("ge")
                    link(dve.tensor_tensor(cbm[:, 0, :], cb[:, 0:P], le, ALU.mult))
                    link(dve.tensor_copy(cbm[:, 1, :], cb[:, P:L]))
                    link(dve.tensor_tensor(cbm[:, 2, :], cb[:, L + P:2 * L], le, ALU.mult))
                    link(dve.tensor_tensor(cbm[:, 3, :], cb[:, 0:P], ge, ALU.mult))
                    link(dve.tensor_copy(cbm[:, 4, :], cb[:, L:L + P]))
                    dve.tensor_tensor(cbm[:, 5, :], cb[:, L + P:2 * L], ge, ALU.mult).then_inc(cb_done, 1)
                if g:
                    dve.wait_ge(y_std, g)
                    link(dve.reciprocal(rstd, rstd))
                    for blk in range(GB):
                        nb = GB * (g - 1) + blk
                        dve.scalar_tensor_tensor(yT[:, nb, :], yT[:, nb, :], pc("ssd_norm", nb), rstd, ALU.mult, ALU.mult).then_inc(y_norm, 1)
                if g < SSD_G:
                    for t in range(TT):
                        dve.wait_ge(yoff_ready, 2 * g + t + 1)
                        for dr in range(2):
                            w = spread(eacs[:, t, 32 * dr + GH * g:32 * dr + GH * g + GH])
                            link(dve.tensor_tensor(per_head(yo2), per_head(bank[4 + 2 * t + dr][:, :]), w, ALU.mult))
                            ins = dve.tensor_tensor(yoff[:, t, :], yoff[:, t, :], yo2, ALU.add)
                            if dr == 0:
                                link(ins)
                        ins.then_inc(yoff_done, 1)
                        dve.wait_ge(yoff_done, 2 * g + t + 1)

        r4 = Region(AFTER_Y)
        gT = r4.take(16, L)
        uT = r4.take(KT, L)
        ut = r4.take(2, L)
        tmp4 = r4.take(4, 512)
        gdiag4 = r4.take(KT, P)
        merged = sem("merged")

        def merge_pe(pe):
            for i in range(4):
                feat_groups(pe, f"gates{i}", 0, hT, 0, L, GROUP["gates"] + 4 * i, 4)
            grow_pe(pe, 0, gdiag4)
            for i in range(2):
                feat_groups(pe, f"na{i}", 0, oT, 0, L, GROUP["na"] + 4 * i, 4)
            for i in range(2):
                for k in range(2):
                    w = slot(f"ssd{i}{k}")
                    wait_chunk(pe, f"ssd{i}{k}")
                    for b in range(4):
                        n = GROUP["ssd"] + 4 * i + b
                        if k == 0:
                            pe.wait_ge(gemm_freed, n - 3)
                        for kk in range(KT):
                            last = pe.matmul(bank[n % 4][:, 0:L], w[:, kk, b * P:(b + 1) * P], yT[:, KT * k + kk, :],
                                             start=k == 0 and kk == 0, stop=k == 1 and kk == KT - 1)
                        if k == 1:
                            last.then_inc(gemm_ready, 1)
                    if k == 0:
                        last.then_inc(chunk_used, 1)
            pe.wait_ge(grow_in, 2)
            pe.wait_ge(merged, 8)
            rows_product(pe, "out", uT, 1)

        def merge_act(act):
            for i in range(16):
                n = GROUP["gates"] + i
                act.wait_ge(gemm_ready, n + 1)
                act.activation(gT[:, i, :], bank[n % 4][:, 0:L], ACT.Sigmoid).then_inc(gemm_freed, 1)
            post_act(act, rows_ready, [ROWS["out"] + j + 1 for j in range(4)], tmp4)

        def merge_dve(dve):
            link = stepper(dve, dve_step)
            grow_dve_in(dve, 0, gdiag4)
            grow_dve_out(dve, 0)
            dve.wait_ge(gemm_freed, GROUP["na"])
            for i in range(8):
                n = GROUP["na"] + i
                dve.wait_ge(gemm_ready, n + 1)
                dve.tensor_tensor(uT[:, i, :], bank[n % 4][:, 0:L], gT[:, i, :], ALU.mult).then_inc(gemm_freed, 1)
            for i in range(8):
                n = GROUP["ssd"] + i
                dve.wait_ge(gemm_ready, n + 1)
                dve.tensor_tensor(ut[:, i % 2, :], bank[n % 4][:, 0:L], gT[:, 8 + i, :], ALU.mult).then_inc(gemm_freed, 1)
                dve.wait_ge(gemm_freed, n + 1)
                dve.tensor_tensor(uT[:, i, :], uT[:, i, :], ut[:, i % 2, :], ALU.add).then_inc(merged, 1)
            dve.wait_ge(merged, 8)
            post_dve(dve, tmp4)

        r5 = Region()
        hm = r5.take(KT, L)
        xn5 = r5.take(TT, D)
        junk5 = r5.take(TT, D)
        aff = r5.take(TT, NE)
        affT = r5.take(L)
        left = r5.take(L)
        top = r5.take(4, 8)
        place = r5.take(3, L)
        code = r5.take(TT, NE)
        pick5 = r5.take(TT, NE, CAP)
        pick_g = r5.take(NE, 4, CAP)
        xgT = r5.take(KT, NE * CAP)
        PgT = r5.take(NE, L)
        gdiag5 = r5.take(KT, P)
        xg = r5.take(2, KT, CAP)
        pg = r5.take(2, 2, L)
        sg = r5.take(2, 512)
        hid = r5.take(2, 512)
        hidT = r5.take(2, 512)
        yo = r5.take(2, 512)
        tmp5 = junk5.rearrange("p t (h n) -> p (t h) n", h=2)
        (logits_ready, aff_max, aff_exp, aff_done, affT_ready, place_ready, code_ready, pick_ready, gather_ready, gather_read,
         pgt_ready, pgt_done, pgate_done, zero_pg) = (sem(n) for n in (
             "logits_ready", "aff_max", "aff_exp", "aff_done", "affT_ready", "place_ready", "code_ready", "pick_ready",
             "gather_ready", "gather_read", "pgt_ready", "pgt_done", "pgate_done", "zero_pg"))
        (expert_used, gate_ready, up_ready, down_ready, xg_staged, pg_staged, gate_acted, hid_done, hid_turned, hid_copied,
         yo_done, scattered) = (sem(n) for n in (
             "expert_used", "gate_ready", "up_ready", "down_ready", "xg_staged", "pg_staged", "gate_acted", "hid_done",
             "hid_turned", "hid_copied", "yo_done", "scattered"))
        xn5_t = [xn5[:, t, :] for t in range(TT)]
        x_t = [xres[:, t, :] for t in range(TT)]

        def route_act(act):
            norm_act(act, x_t, [junk5[:, t, :] for t in range(TT)])
            act.wait_ge(aff_max, 2)
            for t in range(TT):
                act.activation(aff[:, t, :], bank[2][:, NE * t:NE * t + NE], ACT.Exp, bias=small[:, 26 + t:27 + t],
                               accum_out=small[:, 28 + t:29 + t]).then_inc(aff_exp, 1)
            for g in range(8):
                act.wait_ge(pgt_ready, g + 1)
                act.copy(PgT.rearrange("p e l -> p (e l)")[:, 512 * g:512 * g + 512], bank[4 + g % 2][:, :]).then_inc(pgt_done, 1)

        def route_pe(pe):
            turn_pe(pe, xn5_t)
            pe.wait_ge(tr_freed, nrm["pe"][1])
            for t in range(TT):
                for k in range(KT):
                    last = pe.matmul(bank[2][:, NE * t:NE * t + NE], hm[:, k, t * P:(t + 1) * P], router[:, k, :],
                                     start=k == 0, stop=k == KT - 1)
            last.then_inc(logits_ready, 1)
            pe.wait_ge(aff_done, 2)
            for t in range(TT):
                last = pe.transpose(bank[3][0:NE, t * P:(t + 1) * P], aff[:, t, :], ident)
            last.then_inc(affT_ready, 1)
            pe.wait_ge(place_ready, 1)
            for t in range(TT):
                last = pe.transpose(bank[2][:, NE * t:NE * t + NE], place[0:NE, 2, t * P:(t + 1) * P], ident[0:NE, 0:NE])
            last.then_inc(code_ready, 1)
            pe.wait_ge(pick_ready, 2)
            for k in range(KT):
                if k >= 2:
                    pe.wait_ge(gather_read, k - 1)
                for t in range(TT):
                    last = pe.matmul(bank[k % 2][:, :], xn5[:, t, k * P:(k + 1) * P], pick5[:, t], start=t == 0, stop=t == TT - 1)
                last.then_inc(gather_ready, 1)
            grow_pe(pe, 1, gdiag5)
            pe.wait_ge(grow_in, 4)
            for g in range(8):
                if g >= 2:
                    pe.wait_ge(pgt_done, g - 1)
                for i in range(4):
                    e, t = 2 * g + i // 2, i % 2
                    pe.wait_ge(pgate_done, 2 * e + t + 1)
                    last = pe.transpose(bank[4 + g % 2][:, i * P:(i + 1) * P], pick_g[:, (2 * e + t) % NE], ident)
                last.then_inc(pgt_ready, 1)

        def route_dve(dve):
            link = stepper(dve, dve_step)
            norm_dve(dve, x_t, xn5_t)
            turned_dve(dve, hm, mul2, mod[:, 24:32])
            link(dve.memset(pg, 0.0))
            dve.wait_ge(logits_ready, 1)
            for t in range(TT):
                link(dve.tensor_reduce(small[:, 24 + t:25 + t], bank[2][:, NE * t:NE * t + NE], AX.X, ALU.max))
                dve.tensor_scalar(small[:, 26 + t:27 + t], small[:, 24 + t:25 + t], -1.0, None, ALU.mult).then_inc(aff_max, 1)
            for t in range(TT):
                dve.wait_ge(aff_exp, t + 1)
                link(dve.reciprocal(small[:, 30 + t:31 + t], small[:, 28 + t:29 + t]))
                dve.tensor_scalar(aff[:, t, :], aff[:, t, :], small[:, 30 + t:31 + t], None, ALU.mult).then_inc(aff_done, 1)
            dve.wait_ge(affT_ready, 1)
            link(dve.tensor_copy(affT[0:NE, :], bank[3][0:NE, 0:L]))
            src = affT
            for r in range(CAP // 8):
                link(dve.max(top[0:NE, r, :], src[0:NE, :]))
                link(dve.match_replace(left[0:NE, :], top[0:NE, r, :], src[0:NE, :], -1.0))
                src = left
            link(dve.tensor_scalar(place[0:NE, 0, :], left[0:NE, :], -1.0, None, ALU.is_equal))
            link(dve.memset(place[0:NE, 1, :], 1.0))
            link(dve.tensor_tensor_scan(place[0:NE, 2, :], place[0:NE, 1, :], place[0:NE, 0, :], 0.0, ALU.mult, ALU.add))
            dve.tensor_tensor(place[0:NE, 2, :], place[0:NE, 2, :], place[0:NE, 0, :], ALU.mult).then_inc(place_ready, 1)
            dve.wait_ge(code_ready, 1)
            link(dve.tensor_copy(code, bank[2][:, 0:2 * NE].rearrange("p (t e) -> p t e", t=TT)))
            for t in range(TT):
                dve.tensor_tensor(pick5[:, t], code[:, t, :].unsqueeze(2).broadcast_to([P, NE, CAP]),
                                  numbers.unsqueeze(1).broadcast_to([P, NE, CAP]), ALU.is_equal).then_inc(pick_ready, 1)
            dve.wait_ge(pick_ready, 2)
            dve.wait_ge(aff_done, 2)
            grow_dve_in(dve, 1, gdiag5)
            for k in range(KT):
                dve.wait_ge(gather_ready, k + 1)
                dve.tensor_scalar(xgT[:, k, :], bank[k % 2][:, :], mul2[:, k:k + 1], mod[:, 24 + k:25 + k],
                                  ALU.mult, ALU.add).then_inc(gather_read, 1)
            grow_dve_out(dve, 1)
            for i in range(2 * NE):
                e, t = i // 2, i % 2
                if i >= NE:
                    dve.wait_ge(pgt_ready, (i - NE) // 4 + 1)
                dve.tensor_tensor(pick_g[:, i % NE], pick5[:, t, e, :].unsqueeze(1).broadcast_to([P, 4, CAP]),
                                  aff[:, t, e:e + 1].unsqueeze(2).broadcast_to([P, 4, CAP]), ALU.mult).then_inc(pgate_done, 1)

        FE = FIRST_EXPERT

        def expert_wait(pe, e, k):
            c = FE + k
            pe.wait_ge(slot_full[c % SLOTS], e * (16 * EXPERT_USES) + 16 * (c // SLOTS + 1))

        def expert_slot(k, kt):
            return ring[:, (FE + k) % SLOTS, :].rearrange("p (t n) -> p t n", t=kt)

        def experts_pe(pe):
            pe.wait_ge(hid_done, 1)
            for j in range(4):
                last = pe.matmul(bank[4 + j][:, :], yo_zero[:, 0:P], yo_zero, start=True, stop=False, skip_group_check=True)
            last.then_inc(zero_pg, 1)
            with pe.Fori(0, NE // 2) as i:
                for e2 in range(2):
                    e = 2 * i + e2
                    pe.wait_ge(xg_staged, e + 1)
                    for which, ready in ((0, gate_ready), (1, up_ready)):
                        if which == 0:
                            pe.wait_ge(gate_acted, e + 1)
                        else:
                            pe.wait_ge(hid_done, e + 1)
                        for c in range(4):
                            k = 4 * which + c
                            expert_wait(pe, e, k)
                            w = expert_slot(k, 2)
                            for k2 in range(2):
                                for n in range(4):
                                    last = pe.matmul(bank[which][32 * n:32 * n + 32, :], xg[:, e2, 2 * c + k2, :],
                                                     w[:, k2, 512 * n:512 * n + 512], start=c == 0 and k2 == 0,
                                                     stop=c == 3 and k2 == 1, tile_position=(0, 32 * n))
                            last.then_inc(expert_used if c < 3 else ready, 1)
                    pe.wait_ge(hid_done, e + 2)
                    for b in range(4):
                        last = pe.transpose(bank[2][:, b * P:(b + 1) * P], hid[:, e2, b * P:(b + 1) * P], ident)
                    last.then_inc(hid_turned, 1)
                    pe.wait_ge(hid_copied, e + 1)
                    pe.wait_ge(yo_done, e + 1)
                    for n in range(4):
                        k = 8 + n
                        expert_wait(pe, e, k)
                        w = expert_slot(k, 4)
                        for b in range(4):
                            for half in range(2):
                                q = 2 * half + b % 2
                                last = pe.matmul(bank[3][32 * q:32 * q + 32, :], hidT[:, e2, b * P + 32 * n:b * P + 32 * n + 32],
                                                 w[:, b, 512 * half:512 * half + 512], start=n == 0 and b < 2,
                                                 stop=n == 3 and b >= 2, tile_position=(0, 32 * q))
                        last.then_inc(expert_used if n < 3 else down_ready, 1)
                    pe.wait_ge(yo_done, e + 2)
                    pe.wait_ge(pg_staged, 2 * e + 2)
                    for t in range(TT):
                        for half in range(2):
                            last = pe.matmul(bank[4 + 2 * half + t][:, :], pg[:, e2, half, t * P:(t + 1) * P], yo[:, e2, :],
                                             start=False, stop=False, skip_group_check=True)
                    last.then_inc(scattered, 1)

        yo_zero = tmp5[:, 0, :]

        def experts_act(act):
            act.sem_inc(gate_acted, 1)
            act.sem_inc(yo_done, 1)
            with act.Fori(0, NE // 2) as i:
                for e2 in range(2):
                    e = 2 * i + e2
                    act.wait_ge(gate_ready, e + 1)
                    act.activation(sg[:, e2, :], bank[0][:, :], ACT.Silu).then_inc(gate_acted, 1)
                    act.wait_ge(hid_turned, e + 1)
                    act.copy(hidT[:, e2, :], bank[2][:, :]).then_inc(hid_copied, 1)
                    act.wait_ge(down_ready, e + 1)
                    act.copy(yo[:, e2, :], bank[3][:, :]).then_inc(yo_done, 1)

        def experts_dve(dve):
            link = stepper(dve, dve_step)
            dve.memset(yo_zero, 0.0).then_inc(hid_done, 1)
            dve.wait_ge(hid_done, 1)
            dve.sem_inc(scattered, 2)
            with dve.Fori(0, NE // 2) as i:
                for e2 in range(2):
                    e = 2 * i + e2
                    dve.wait_ge(scattered, e + 1)
                    dve.tensor_scalar(xg[:, e2], xgT[:, :, bass.ds(e * CAP, CAP)], 1.0, None, ALU.mult).then_inc(xg_staged, 1)
                    for half in range(2):
                        p0 = 64 * half
                        dve.tensor_scalar(pg[p0:p0 + 64, e2, half, :], PgT[p0:p0 + 64, bass.ds(e, 1), :].rearrange("p e l -> p (e l)"),
                                          1.0, None, ALU.mult).then_inc(pg_staged, 1)
                    dve.wait_ge(gate_acted, e + 2)
                    dve.wait_ge(up_ready, e + 1)
                    dve.tensor_tensor(hid[:, e2, :], bank[1][:, :], sg[:, e2, :], ALU.mult).then_inc(hid_done, 1)

        tab_in, pT_in = sem("tab_in"), sem("pT_in")
        relu_done, hid2_done, ple_gate, ple_term, ple_done = (sem(n) for n in (
            "relu_done", "hid2_done", "ple_gate", "ple_term", "ple_done"))
        rm = Region()
        hn = rm.take(KT, L)
        xnm = rm.take(TT, D)
        AFTER_N = rm.at
        hid2 = rm.take(DFF // P, L)
        tmpm = rm.take(4, 512)
        gs = rm.take(TT, D)
        gterm = rm.take(2, 512)
        pT = rm.take(2, L)
        xnm_t = [xnm[:, t, :] for t in range(TT)]

        def mlp_pe(pe, l):
            turn_pe(pe, xnm_t)
            pe.wait_ge(tr_freed, nrm["pe"][1])
            for i in range(8):
                feat_groups(pe, f"up{l}{i}", 0, hn, 0, L, GROUP[f"up{l}"] + 4 * i, 4)
            pe.wait_ge(hid2_done, 32 * (l + 1))
            rows_product(pe, f"dn{l}", hid2, 4)

        def mlp_act(act, l):
            norm_act(act, x_t, [tmpm.rearrange("p (t h) n -> p t (h n)", t=2)[:, t, :] for t in range(TT)])
            for i in range(32):
                n = GROUP[f"up{l}"] + i
                act.wait_ge(gemm_ready, n + 1)
                act.activation(hid2[:, i, :], bank[n % 4][:, 0:L], ACT.Relu).then_inc(gemm_freed, 1)
            post_act(act, rows_ready, [ROWS[f"dn{l}"] + j + 1 for j in range(4)], tmpm)

        def mlp_dve(dve, l):
            norm_dve(dve, x_t, xnm_t)
            turned_dve(dve, hn, pc("mlp_pre2", 8 * l, 8))
            dve.wait_ge(grow_loaded, 16 * (2 * l + 2))
            post_dve(dve, tmpm)

        def mlp_pool(pool, l):
            for i in range(32):
                pool.wait_ge(gemm_freed, GROUP[f"up{l}"] + i + 1)
                pool.tensor_tensor(hid2[:, i, :], hid2[:, i, :], hid2[:, i, :], ALU.mult).then_inc(hid2_done, 1)

        def load_grow(pool, i):
            pool.dma_start(grow[:, :], d["g_post"][i:i + 1, :].partition_broadcast(P).rearrange("q o n -> q (o n)")).then_inc(grow_loaded, 16)

        def ple_pe(pe, l):
            turn_pe(pe, x_t, normed=False)
            pe.wait_ge(tr_freed, nrm["pe"][1])
            for i in range(2):
                token_groups(pe, f"pg{l}{i}", hn, TT, 512, GROUP[f"ple{l}"] + 2 * i)
            wait_chunk(pe, f"pp{l}")
            pe.wait_ge(pT_in, 16 * (l + 1))
            w = slot(f"pp{l}")
            for i in range(4):
                h, t = i // 2, i % 2
                n = GROUP[f"ple{l}"] + 4 + i
                pe.wait_ge(gemm_freed, n - 3)
                for k in range(2):
                    last = pe.matmul(bank[n % 4][:, :], pT[:, k, t * P:(t + 1) * P], w[:, k, 512 * h:512 * h + 512], start=k == 0, stop=k == 1)
                last.then_inc(gemm_ready, 1)

        def ple_act(act, l):
            for i in range(4):
                h, t = i // 2, i % 2
                n = GROUP[f"ple{l}"] + i
                act.wait_ge(gemm_ready, n + 1)
                act.activation(gs[:, t, 512 * h:512 * h + 512], bank[n % 4][:, :], ACT.Sigmoid).then_inc(gemm_freed, 1)

        def ple_dve(dve, l):
            link = stepper(dve, dve_step)
            turned_dve(dve, hn)
            for i in range(4):
                h, t = i // 2, i % 2
                n = GROUP[f"ple{l}"] + 4 + i
                dve.wait_ge(gemm_ready, n + 1)
                dve.wait_ge(gemm_freed, n)
                dve.tensor_tensor(gterm[:, i % 2, :], bank[n % 4][:, :], gs[:, t, 512 * h:512 * h + 512], ALU.mult).then_inc(gemm_freed, 1)
                dve.wait_ge(gemm_freed, n + 1)
                x = xres[:, t, 512 * h:512 * h + 512]
                dve.tensor_tensor(x, x, gterm[:, i % 2, :], ALU.add).then_inc(ple_done, 1)
            dve.wait_ge(ple_done, 4 * (l + 1))

        def ple_pool(pool, l):
            pool.dma_start(pT, d["pT"][l].rearrange("(k p) n -> p k n", p=P)).then_inc(pT_in, 16)

        r6 = Region(AFTER_N, ROPE0)
        qz_ab = {t: r6.take(4, 2, L) for t in "ab"}
        k_ab = {t: r6.take(4, L) for t in "ab"}
        v_ab = {t: r6.take(TT, 512) for t in "ab"}
        s_ab, pr_ab = r6.take(AHEAD, L), r6.take(AHEAD, L)
        PT_a, PT_b = r6.take(2, TT, P), r6.take(2, TT, L)
        first_map = r6.take(L)
        oA, oA2 = r6.take(8, P), r6.take(8, P)
        obT = r6.take(KT, L)
        sub = r6.take(4, 8)
        lam_sum, lam_exp, av_ready, av_stored, sub_sum, sub_std, sub_done, sub_ready, sub_out = (sem(n) for n in (
            "lam_sum", "lam_exp", "av_ready", "av_stored", "sub_sum", "sub_std", "sub_done", "sub_ready", "sub_out"))
        causal_w = lambda u: P * (u % 2 + 1)

        def mask_of(m, qt):
            return masks[:, m, 0:P] if qt == 0 else masks[:, m, P:3 * P]

        AA = Attention(8, 2, causal_w, lambda u: mask_of(0, u % 2), 1.0, s_ab, pr_ab, lambda u: PT_a[:, u % 2, 0:u % 2 + 1, :], (3, 6))
        AB = Attention(16, 1, causal_w, lambda u: mask_of(1, u % 2), 1.0, s_ab, pr_ab,
                       lambda u: PT_b[:, (u // 2) % 2, 0:u % 2 + 1, (u % 2) * P:(u % 2 + 1) * P], (3, 6))
        AB.hooks = head_values(AB, v_ab["b"], PT_b, 8, True, counted["values"], lambda blk: obT[:, 4 + blk, :])

        def ab_proj_pe(pe):
            turn_pe(pe, xnm_t)
            pe.wait_ge(tr_freed, nrm["pe"][1])
            for t in "ab":
                for m in "qk":
                    feat_groups(pe, t + m, 0, hn, 0, L, GROUP[t + m], 4)
                    if t + m == "aq":
                        pe.wait_ge(tab_in, 16)
                    for b in range(4):
                        rope_pe(pe, GROUP[t + m] + b, "swap32")
                token_groups(pe, t + "v", hn, TT, 512, GROUP[t + "v"])

        def ab_proj_act(act):
            norm_act(act, x_t, [oA.rearrange("p u n -> p (u n)"), oA2.rearrange("p u n -> p (u n)")])
            for t in "ab":
                for m in "qk":
                    for b in range(4):
                        rope_act(act, GROUP[t + m] + b)
                for i in range(TT):
                    n = GROUP[t + "v"] + i
                    act.wait_ge(gemm_ready, n + 1)
                    act.copy(v_ab[t][:, i, :], bank[n % 4][:, :]).then_inc(gemm_freed, 1)
            act.wait_ge(lam_sum, 2)
            act.activation(lam[:, 2:4], lam[:, 0:2], ACT.Exp).then_inc(lam_exp, 1)

        def ab_proj_dve(dve):
            link = stepper(dve, dve_step)
            norm_dve(dve, x_t, xnm_t)
            link(dve.memset(qz_ab["a"], 0.0))
            link(dve.memset(qz_ab["b"], 0.0))
            turned_dve(dve, hn, pc("mix_pre2", 0, 8))
            dve.wait_ge(tab_in, 16)
            for t in "ab":
                for b in range(4):
                    q = qz_ab[t]
                    rope_dve(dve, tb("ab_qc"), tb("ab_qs"), [(q[0:64, b, 0, :], 0, 64), (q[64:128, b, 1, :], 64, 128)])
                for b in range(4):
                    rope_dve(dve, tb("ab_kc"), tb("ab_ks"), [(k_ab[t][:, b, :], 0, 128)])
            hv = heads[:, 128:SKIP0].rearrange("p (i d) -> p i d", i=4)
            for i in range(2):
                dve.tensor_tensor_reduce(out=oA[:, i, 0:HD], in0=hv[:, 2 * i, :], in1=hv[:, 2 * i + 1, :], scale=1.0, scalar=0.0,
                                         op0=ALU.mult, op1=ALU.add, accum_out=lam[:, i:i + 1]).then_inc(lam_sum, 1)
            dve.wait_ge(lam_exp, 1)
            link(dve.tensor_tensor(lam[:, 4:5], lam[:, 2:3], lam[:, 3:4], ALU.subtract))
            link(dve.tensor_scalar(lam[:, 5:6], lam[:, 4:5], -1.0, -LAM_INIT, ALU.mult, ALU.add))

        def ab_att_pe(pe):
            def scores_a(pe, i, b):
                u, m = i // 2, i % 2
                h, qt = u // 2, u % 2
                return pe.matmul(b[:, 0:causal_w(u)], qz_ab["a"][:, h, m, qt * P:(qt + 1) * P], k_ab["a"][:, h, 0:causal_w(u)],
                                 start=True, stop=True)

            def value_a(pe, u):
                h, qt = u // 2, u % 2
                pe.wait_ge(att_copied, AA.first + u + 1)
                if u >= 2:
                    pe.wait_ge(av_stored, u - 1)
                for k in range(qt + 1):
                    last = pe.matmul(bank[4 + u % 2][:, 0:P], PT_a[:, u % 2, k, :], v_ab["a"][:, k, h * P:(h + 1) * P],
                                     start=k == 0, stop=k == qt)
                last.then_inc(av_ready, 1)
            att_pe(pe, AA, scores_a, value_a)
            pe.wait_ge(sub_done, 1)
            for h in range(A_HEADS):
                for qt in range(TT):
                    last = pe.transpose(bank[6 + h % 2][:, (h // 2 * TT + qt) * P:(h // 2 * TT + qt + 1) * P], oA[:, 2 * h + qt, :], ident)
            last.then_inc(sub_ready, 1)
            pe.wait_ge(sub_out, 4)
            pe.wait_ge(av_stored, 8)

            def scores_b(pe, u, b):
                h, qt = u // 2, u % 2
                return pe.matmul(b[:, 0:causal_w(u)], qz_ab["b"][:, h // 2, h % 2, qt * P:(qt + 1) * P], k_ab["b"][:, h // 2, 0:causal_w(u)],
                                 start=True, stop=True)
            att_pe(pe, AB, scores_b, AB.hooks[0])
            pe.wait_ge(att_stored, (AB.values_first + 8) // 2)
            rows_product(pe, "o0", obT, 1)

        AB.values_first = counted["values"] - 8

        def ab_att_act(act):
            def free_a(act, u):
                if u >= 2:
                    act.wait_ge(av_ready, u - 1)
            att_act(act, AA, free_a)
            act.wait_ge(sub_sum, 1)
            act.activation(sub[:, 1, :], sub[:, 0, :], ACT.Sqrt, bias=epsc[:, :], scale=1.0 / P).then_inc(sub_std, 1)
            att_act(act, AB, AB.hooks[2])
            post_act(act, rows_ready, [ROWS["o0"] + j + 1 for j in range(4)], tmp_o)

        def ab_att_dve(dve):
            link = stepper(dve, dve_step)

            def after_a(dve, u):
                dve.wait_ge(av_ready, u + 1)
                dve.tensor_copy(oA[:, u, :], bank[4 + u % 2][:, 0:P]).then_inc(av_stored, 1)
            att_dve(dve, AA, after_a, lam_of=(lam[:, 5:6], first_map))
            dve.wait_ge(av_stored, 8)
            link(dve.tensor_tensor(oA2, oA, oA, ALU.mult))
            dve.tensor_reduce(sub[:, 0, :], oA2, AX.X, ALU.add).then_inc(sub_sum, 1)
            dve.wait_ge(sub_std, 1)
            link(dve.reciprocal(sub[:, 2, :], sub[:, 1, :]))
            link(dve.tensor_scalar(sub[:, 3, :], sub[:, 2, :], 1.0 - LAM_INIT, None, ALU.mult))
            dve.tensor_tensor(oA, oA, sub[:, 3, :].unsqueeze(2).broadcast_to([P, 8, P]), ALU.mult).then_inc(sub_done, 1)
            dve.wait_ge(sub_ready, 1)
            for h in range(A_HEADS):
                dve.tensor_scalar(obT[:, h, :], bank[6 + h % 2][:, h // 2 * L:h // 2 * L + L], pc("sub", 0), None, ALU.mult).then_inc(sub_out, 1)
            att_dve(dve, AB, AB.hooks[1])
            dve.wait_ge(grow_loaded, 16)
            post_dve(dve, tmp_o)

        ro = Region(r6.at)
        tmp_o = ro.take(4, 512)

        r9 = Region(AFTER_N)
        CW = CQ + CKV + CROPE + 64 + IDX_HEADS
        cct = r9.take(TT, CW)
        cqT = r9.take(3, L)
        ckvT = r9.take(2, L)
        krep = r9.take(TT, P)
        kirep = r9.take(TT, P)
        rot = r9.take(2, TT, 64)
        kiT = r9.take(L)
        wi = r9.take(TT, IDX_HEADS)
        qi = r9.take(IDX_HEADS, L)
        q_c = r9.take(C_HEADS, L)
        k_c = r9.take(C_HEADS, L)
        v_c = r9.take(TT, D)
        acc = r9.take(TT, L)
        bsel = r9.take(TT, L)
        top9 = r9.take(8)
        relu = r9.take(2, L)
        s_c, pr_c, PT_c = r9.take(AHEAD, L), r9.take(AHEAD, L), r9.take(2, TT, L)
        oTc = hn
        stc = r9.take(12)
        tmp_c = q_c.rearrange("p h l -> p (h l)")[:, 0:2 * D].rearrange("p (j n) -> p j n", j=4)
        (c_copied, c_sq, c_std, c_norm, c_rot, ct_ready, ct_out, ix_ready, ix_relu, ix_added) = (sem(n) for n in (
             "c_copied", "c_sq", "c_std", "c_norm", "c_rot", "ct_ready", "ct_out", "ix_ready", "ix_relu", "ix_added"))
        AC = Attention(2 * C_HEADS, 1, causal_w, lambda u: bsel[:, u % 2, 0:causal_w(u)], C_SCALE, s_c, pr_c,
                       lambda u: PT_c[:, (u // 2) % 2, 0:u % 2 + 1, (u % 2) * P:(u % 2 + 1) * P], (3, 6))
        AC.values_first = counted["values"]
        AC.hooks = head_values(AC, v_c, PT_c, C_HEADS, True, counted["values"], lambda blk: oTc[:, blk, :])
        N_TURNED = 7

        def c_pe(pe):
            turn_pe(pe, xnm_t)
            pe.wait_ge(tr_freed, nrm["pe"][1])
            token_groups(pe, "cin0", hn, TT, 512, GROUP["cin"])
            token_groups(pe, "cin1", hn, TT, 232, GROUP["cin"] + 2)
            srcs = [cct[:, :, i * P:(i + 1) * P] for i in range(5)] + [krep, kirep]
            for i, s in enumerate(srcs):
                if i == 0:
                    pe.wait_ge(c_norm, 4)
                if i == 5:
                    pe.wait_ge(c_rot, 2)
                if i >= 2:
                    pe.wait_ge(ct_out, i - 1)
                for t in range(TT):
                    last = pe.transpose(bank[6 + i % 2][:, t * P:(t + 1) * P], s[:, t, :], ident)
                last.then_inc(ct_ready, 1)
            pe.wait_ge(ct_out, 3)
            feat_groups(pe, "qi", 0, cqT, 0, L, GROUP["qi"], IDX_HEADS)
            pe.wait_ge(ct_out, N_TURNED)
            feat_groups(pe, "uk", 0, ckvT, 0, L, GROUP["uk"], C_HEADS // 2)
            for n in range(2 * IDX_HEADS):
                qt, h = n // IDX_HEADS, n % IDX_HEADS
                if n >= 2:
                    pe.wait_ge(ix_relu, n - 1)
                pe.matmul(bank[4 + n % 2][:, 0:causal_w(qt)], qi[:, h, qt * P:(qt + 1) * P], kiT[:, 0:causal_w(qt)],
                          start=True, stop=True).then_inc(ix_ready, 1)
            wait_chunk(pe, "uv")
            w = slot("uv")
            for i in range(4):
                h, t = i // 2, i % 2
                n = GROUP["uv"] + i
                pe.wait_ge(gemm_freed, n - 3)
                for k in range(2):
                    last = pe.matmul(bank[n % 4][:, :], ckvT[:, k, t * P:(t + 1) * P], w[:, k, 512 * h:512 * h + 512], start=k == 0, stop=k == 1)
                last.then_inc(gemm_ready, 1)
            for i in range(2):
                feat_groups(pe, f"uq{i}", 0, cqT, 0, L, GROUP["uq"] + 8 * i, C_HEADS // 2)
            pe.wait_ge(gemm_freed, GROUP["uq"] + C_HEADS)

            def scores(pe, u, b):
                h, qt = u // 2, u % 2
                return pe.matmul(b[:, 0:causal_w(u)], q_c[:, h, qt * P:(qt + 1) * P], k_c[:, h, 0:causal_w(u)], start=True, stop=True)
            att_pe(pe, AC, scores, AC.hooks[0])
            pe.wait_ge(att_stored, (AC.values_first + C_HEADS) // 2)
            rows_product(pe, "o1", oTc, 1)

        def c_act(act):
            link = stepper(act, act_step)
            norm_act(act, x_t, [q_c.rearrange("p h l -> p (h l)")[:, D * t:D * t + D] for t in range(TT)])
            for i in range(4):
                c, t = i // 2, i % 2
                n = GROUP["cin"] + i
                act.wait_ge(gemm_ready, n + 1)
                w = (512, CW - 512)[c]
                act.copy(cct[:, t, 512 * c:512 * c + w], bank[n % 4][:, 0:w]).then_inc(gemm_freed, 1)
            act.wait_ge(gemm_freed, GROUP["cin"] + 4)
            junk = acc.rearrange("p t l -> p (t l)")
            for t in range(TT):
                link(act.activation(junk[:, 0:CQ], cct[:, t, 0:CQ], ACT.Square, accum_out=stc[:, t:t + 1]))
                link(act.activation(junk[:, 0:CKV], cct[:, t, CQ:CQ + CKV], ACT.Square, accum_out=stc[:, 2 + t:3 + t]))
            act.activation(stc[:, 4:6], stc[:, 0:2], ACT.Sqrt, bias=epsc[:, :], scale=1.0 / CQ).then_inc(c_std, 1)
            act.activation(stc[:, 6:8], stc[:, 2:4], ACT.Sqrt, bias=epsc[:, :], scale=1.0 / CKV).then_inc(c_std, 1)
            act.wait_ge(gemm_freed, GROUP["uk"])
            for b in range(C_HEADS // 2):
                n = GROUP["uk"] + b
                act.wait_ge(gemm_ready, n + 1)
                link(act.copy(k_c[0:64, 2 * b, :], bank[n % 4][0:64, 0:L]))
                act.copy(k_c[64:128, 2 * b + 1, :], bank[n % 4][64:128, 0:L]).then_inc(gemm_freed, 1)
            for n in range(2 * IDX_HEADS):
                w = causal_w(n // IDX_HEADS)
                act.wait_ge(ix_ready, n + 1)
                if n >= 2:
                    act.wait_ge(ix_added, n - 1)
                act.activation(relu[:, n % 2, 0:w], bank[4 + n % 2][:, 0:w], ACT.Relu).then_inc(ix_relu, 1)
            for i in range(4):
                h, t = i // 2, i % 2
                n = GROUP["uv"] + i
                act.wait_ge(gemm_ready, n + 1)
                act.copy(v_c[:, t, 512 * h:512 * h + 512], bank[n % 4][:, :]).then_inc(gemm_freed, 1)
            att_act(act, AC, AC.hooks[2])
            post_act(act, rows_ready, [ROWS["o1"] + j + 1 for j in range(4)], tmp_c)

        def c_dve(dve):
            link = stepper(dve, dve_step)
            norm_dve(dve, x_t, xnm_t)
            turned_dve(dve, hn, pc("mix_pre2", 8, 8))
            dve.wait_ge(c_std, 2)
            link(dve.reciprocal(stc[:, 8:12], stc[:, 4:8]))
            for t in range(TT):
                q, kv = cct[:, t, 0:CQ], cct[:, t, CQ:CQ + CKV]
                dve.tensor_scalar(q, q, stc[:, 8 + t:9 + t], None, ALU.mult).then_inc(c_norm, 1)
                dve.tensor_scalar(kv, kv, stc[:, 10 + t:11 + t], None, ALU.mult).then_inc(c_norm, 1)

            def turned_block(i):
                b = bank[6 + i % 2]
                dve.wait_ge(ct_ready, i + 1)
                if i < 3:
                    ins = dve.tensor_scalar(cqT[:, i, :], b[:, 0:L], pc("cq", i), None, ALU.mult)
                elif i < 5:
                    ins = dve.tensor_scalar(ckvT[:, i - 3, :], b[:, 0:L], pc("ckv", i - 3), None, ALU.mult)
                elif i == 5:
                    for odd in range(2):
                        p = slice(64 - 64 * odd, 128 - 64 * odd)
                        ins = dve.tensor_copy(k_c[p, odd:C_HEADS:2, :], b[p, 0:L].unsqueeze(1).broadcast_to([64, C_HEADS // 2, L]))
                        if not odd:
                            link(ins)
                else:
                    ins = dve.tensor_copy(kiT, b[:, 0:L])
                ins.then_inc(ct_out, 1)
            for i in range(5):
                turned_block(i)
            r0 = CQ + CKV
            for t in range(TT):
                x = cct[:, t, r0:r0 + 64]
                xs = x.rearrange("p (g h j) -> p g h j", g=2, h=2)
                ys = rot[:, 1, t, :].rearrange("p (g h j) -> p g h j", g=2, h=2)
                ss = tokt[:, t, 1, :].rearrange("p (g h j) -> p g h j", g=2, h=2)
                link(dve.tensor_tensor(rot[:, 0, t, :], x, tokt[:, t, 0, :], ALU.mult))
                for h in range(2):
                    link(dve.tensor_tensor(ys[:, :, h, :], xs[:, :, 1 - h, :], ss[:, :, h, :], ALU.mult))
                link(dve.tensor_tensor(rot[:, 0, t, :], rot[:, 0, t, :], rot[:, 1, t, :], ALU.add))
                link(dve.tensor_copy(krep[:, t, :].rearrange("p (r j) -> p r j", r=4), rot[:, 0, t, 0:32].unsqueeze(1).broadcast_to([P, 4, 32])))
                kr = kirep[:, t, :].rearrange("p (r j) -> p r j", r=4)
                link(dve.tensor_copy(kr[:, 0:2, :], rot[:, 0, t, 32:64].unsqueeze(1).broadcast_to([P, 2, 32])))
                dve.tensor_copy(kr[:, 2:4, :], cct[:, t, r0 + 64:r0 + 96].unsqueeze(1).broadcast_to([P, 2, 32])).then_inc(c_rot, 1)
            link(dve.tensor_scalar(wi, cct[:, :, CW - IDX_HEADS:CW], IDX_HEADS ** -0.5 * HD ** -0.5, None, ALU.mult))
            dve.wait_ge(tab_in, 32)

            def rotate(name, g0, n, dst, table):
                for i in range(n):
                    g = GROUP[name] + g0 + i
                    dve.wait_ge(gemm_ready, g + 1)
                    if g0 + i == 0:
                        dve.wait_ge(gemm_freed, g)
                    dve.tensor_tensor(dst[:, g0 + i, :], bank[g % 4][:, 0:L], tb(table(i)), ALU.mult).then_inc(gemm_freed, 1)
            turned_block(5)
            turned_block(6)
            rotate("qi", 0, IDX_HEADS, qi, lambda i: "ci")
            for qt in range(TT):
                w = causal_w(qt)
                a, m = acc[:, qt, 0:w], mask_of(0, qt)
                for h in range(IDX_HEADS):
                    n = IDX_HEADS * qt + h
                    dve.wait_ge(ix_relu, n + 1)
                    dve.scalar_tensor_tensor(a, relu[:, n % 2, 0:w], wi[:, qt, h:h + 1], m if h == 0 else a, ALU.mult, ALU.add).then_inc(ix_added, 1)
                    dve.wait_ge(ix_added, n + 1)
            for qt in range(TT):
                w = causal_w(qt)
                a, m = acc[:, qt, 0:w], mask_of(0, qt)
                for r in range(TOPK // 8):
                    link(dve.max(top9, a))
                    link(dve.match_replace(a, top9, a, -3e38))
                link(dve.tensor_scalar(a, a, -2e38, NEG, ALU.is_gt, ALU.mult))
                link(dve.tensor_tensor(bsel[:, qt, 0:w], a, m, ALU.add))
            rotate("uq", 0, C_HEADS, q_c, lambda i: ("cq_even", "cq_odd")[i % 2])
            att_dve(dve, AC, AC.hooks[1])
            dve.wait_ge(grow_loaded, 48)
            post_dve(dve, tmp_c)

        out_in = sem("out_in")
        N_CONSTS, N_TABLES = 3, 5
        block = es.enter_context(nc.Block())

        @block.sync
        def _(sp):
            sp.dma_start(cc, d["cc"]).then_inc(consts_in, 16)
            sp.dma_start(cst[:, :], d["cst"]).then_inc(consts_in, 16)
            sp.dma_start(pcol[:, :], d["pcol"]).then_inc(consts_in, 16)

            def load(c):
                src, kt, n, _ = chunks[c]
                if c >= SLOTS and chunks[c - SLOTS] is not None:
                    sp.wait_ge(*chunks[c - SLOTS][3])
                dst = ring[:, c % SLOTS, 0:kt * n].rearrange("p (t n) -> p t n", t=kt)
                sp.dma_start(dst, src).then_inc(slot_full[c % SLOTS], 16)

            for c in range(FE):
                if c == ADA_FIRST:
                    sp.dma_start(heads[:, :], d["heads"].partition_broadcast(P).rearrange("q o n -> q (o n)")).then_inc(tables_in, 16)
                    sp.dma_start(tab[:, :, :], d["tab"][:, 0:4, :]).then_inc(tables_in, 16)
                    sp.dma_start(tokt[:, :, :, :], d["tokt"]).then_inc(tables_in, 16)
                    sp.dma_start(masks[:, :, :], d["masks"]).then_inc(tables_in, 16)
                    sp.dma_start(router[:, :, :], d["w_router"].rearrange("(t p) n -> p t n", p=P)).then_inc(tables_in, 16)
                load(c)

            def expert_sources(e):
                for w, rows, n in (("w_egate", 2 * P, FF), ("w_eup", 2 * P, FF), ("w_edown", 4 * P, D)):
                    for c in range(4):
                        s = d[w][bass.ds(e, 1), rows * c:rows * c + rows, :].rearrange("e (t p) n -> p (e t) n", p=P)
                        yield s, rows // P

            def expert_left(k, e):
                which, c = k // 4, k % 4
                if c == 3:
                    return (gate_ready, up_ready, down_ready)[which], e + 1
                return expert_used, e * 9 + (3 * which + c + 1)

            def load_expert(e, first):
                for k, (src, kt) in enumerate(expert_sources(e)):
                    if k < 4:
                        sp.wait_ge(*(chunks[FE - SLOTS + k][3] if first else expert_left(8 + k, e - 1)))
                    else:
                        sp.wait_ge(*expert_left(k - 4, e))
                    s = (FE + k) % SLOTS
                    sp.dma_start(ring[:, s, :].rearrange("p (t n) -> p t n", t=kt), src).then_inc(slot_full[s], 16)

            load_expert(0, True)
            with sp.Fori(1, NE) as e:
                load_expert(e, False)
            for c in range(FE + 12 * NE, len(chunks)):
                if c < FE + 12 * NE + SLOTS:
                    sp.wait_ge(*expert_left(8 + c - FE - 12 * NE, NE - 1))
                load(c)
            sp.wait_ge(ple_done, 8)
            sp.dma_start(out.rearrange("b (t p) n -> p (b t) n", p=P), xres[:, :, :]).then_inc(out_in, 16)
            sp.wait_ge(out_in, 16)

        @block.tensor
        def _(pe):
            ada_pe(pe)
            pe.wait_ge(tables_in, 16 * N_TABLES)
            end_stage(pe, "pe")
            for hf in range(2):
                na_proj_pe(pe, hf)
                end_stage(pe, "pe")
                att_pe(pe, NA[hf], na_scores_of(hf), NA[hf].hooks[0], {6: ada_rest_pe} if hf else {})
                end_stage(pe, "pe")
            ssd_pe(pe)
            end_stage(pe, "pe")
            merge_pe(pe)
            end_stage(pe, "pe")
            route_pe(pe)
            end_stage(pe, "pe")
            experts_pe(pe)
            end_stage(pe, "pe")
            for l in range(2):
                if l == 0:
                    end_stage(pe, "pe")
                    ab_proj_pe(pe)
                    end_stage(pe, "pe")
                    ab_att_pe(pe)
                else:
                    c_pe(pe)
                end_stage(pe, "pe")
                mlp_pe(pe, l)
                end_stage(pe, "pe")
                ple_pe(pe, l)
                end_stage(pe, "pe")

        @block.scalar
        def _(act):
            ada_act(act)
            act.wait_ge(tables_in, 16 * N_TABLES)
            end_stage(act, "act")
            for hf in range(2):
                na_proj_act(act, hf)
                end_stage(act, "act")
                att_act(act, NA[hf], NA[hf].hooks[2])
                end_stage(act, "act")
            ssd_act(act)
            end_stage(act, "act")
            merge_act(act)
            end_stage(act, "act")
            route_act(act)
            end_stage(act, "act")
            experts_act(act)
            end_stage(act, "act")
            for l in range(2):
                if l == 0:
                    post_act(act, scattered, [2 + NE] * 4, tmp5)
                    end_stage(act, "act")
                    ab_proj_act(act)
                    end_stage(act, "act")
                    ab_att_act(act)
                else:
                    c_act(act)
                end_stage(act, "act")
                mlp_act(act, l)
                end_stage(act, "act")
                ple_act(act, l)
                end_stage(act, "act")

        @block.vector
        def _(dve):
            ada_dve(dve)
            dve.wait_ge(tables_in, 16 * N_TABLES)
            end_stage(dve, "dve")
            for hf in range(2):
                na_proj_dve(dve, hf)
                end_stage(dve, "dve")
                att_dve(dve, NA[hf], NA[hf].hooks[1])
                if hf:
                    ada_rest_dve(dve)
                end_stage(dve, "dve")
            ssd_dve(dve)
            end_stage(dve, "dve")
            merge_dve(dve)
            end_stage(dve, "dve")
            route_dve(dve)
            end_stage(dve, "dve")
            experts_dve(dve)
            end_stage(dve, "dve")
            for l in range(2):
                if l == 0:
                    post_dve(dve, tmp5)
                    end_stage(dve, "dve")
                    ab_proj_dve(dve)
                    end_stage(dve, "dve")
                    ab_att_dve(dve)
                else:
                    c_dve(dve)
                end_stage(dve, "dve")
                mlp_dve(dve, l)
                end_stage(dve, "dve")
                ple_dve(dve, l)
                end_stage(dve, "dve")

        @block.gpsimd
        def _(pool):
            end_stage(pool, "pool")
            for hf in range(2):
                na_bias_pool(pool, hf, 0, 3)
                end_stage(pool, "pool")
                na_bias_pool(pool, hf, 3, 8)
                end_stage(pool, "pool")
            pool.dma_start(tab[:, :, :], d["tab"][:, 4:8, :]).then_inc(tab_in, 16)
            ssd_pool(pool)
            for _ in range(4):
                end_stage(pool, "pool")
            for l in range(2):
                if l == 0:
                    end_stage(pool, "pool")
                    load_grow(pool, 0)
                    end_stage(pool, "pool")
                    end_stage(pool, "pool")
                    pool.dma_start(tab[:, 0:3, :], d["tab"][:, 8:11, :]).then_inc(tab_in, 16)
                else:
                    load_grow(pool, 2)
                    end_stage(pool, "pool")
                load_grow(pool, 2 * l + 1)
                mlp_pool(pool, l)
                end_stage(pool, "pool")
                ple_pool(pool, l)
                end_stage(pool, "pool")


def kernel(**inputs):
    import concourse.bacc as bacc
    from concourse.bass_utils import run_bass_kernel_spmd

    nc = bacc.Bacc("TRN2", target_bir_lowering=False, num_devices=1)
    arrays = layouts(inputs)
    d = {n: nc.dram_tensor(f"in_{n}", a.shape, mybir.dt.from_np(a.dtype), kind="ExternalInput").ap() for n, a in arrays.items()}
    out = nc.dram_tensor("out", (1, L, D), F32, kind="ExternalOutput").ap()
    build(nc, d, out)
    r = run_bass_kernel_spmd(nc, [{f"in_{n}": a for n, a in arrays.items()}], core_ids=[0])
    return r.results[0]["out"]
```

```python
from contextlib import ExitStack

import numpy as np
import concourse.bass as bass
from concourse import mybir

F32 = mybir.dt.float32
F32R = mybir.dt.float32r
ALU = mybir.AluOpType
ACT = mybir.ActivationFunctionType
AX = mybir.AxisListType

P = 128
L = 256
TT = L // P
D = 1024
KT = D // P
EPS = 1e-6
NEG = -1e30
HD = 64
SLOTS = 4
SLOT = 4096
WORK = 29120

NA_HEADS, GRID_W, NA_KH, NA_KW = 16, 64, 8, 16
SSD_W, SSD_HEADS, SSD_G, SSD_N, CONV = 2048, 32, 4, 128, 5
GB = SSD_W // SSD_G // P
GH = SSD_HEADS // SSD_G
NE, FF, CAP = 16, 2048, 32
A_HEADS, B_HEADS = 4, 8
C_HEADS, CQ, CKV, CROPE, CNOPE = 16, 384, 256, 32, 64
IDX_HEADS, TOPK = 8, 64
C_SCALE = (CNOPE + CROPE) ** -0.5
DFF = 4096
SKIP0 = 4 * SSD_HEADS + 4 * HD
BIASES = 5
ADA_FIRST = 4
LAM_INIT = 0.2

PCOL = {}
_at = 0
for _name, _n in (("b_ada", 48), ("pre_mix", 8), ("post_mix", 8), ("pre_ffn", 8), ("post_ffn", 8),
                  ("conv_w", 24 * CONV), ("conv_b", 24), ("ssd_norm", 16),
                  ("mix_pre2", 16), ("mlp_pre2", 16), ("cq", 3), ("ckv", 2), ("sub", 1)):
    PCOL[_name] = _at
    _at += _n
NPCOL = _at

CST = ["ident", "ones", "le", "ge", "gt", "lt", "swap16", "swap32"]
NCST = len(CST) * P + CAP
TAB = ["na_qc", "na_qs", "na_kc", "na_ks", "ab_qc", "ab_qs", "ab_kc", "ab_ks",
       "cq_even", "cq_odd", "ci"]


def constants():
    f = np.float32
    i = np.arange(P)
    r, c = i[:, None], i[None, :]
    one = lambda m: m.astype(f)
    mats = {
        "ident": one(r == c), "ones": np.ones((P, P), f), "le": one(r <= c), "ge": one(r >= c),
        "gt": one(r > c), "lt": one(r < c), "swap16": one(r == (c ^ 16)), "swap32": one(r == (c ^ 32)),
    }
    cst = np.concatenate([mats[m] for m in CST] + [np.tile(np.arange(1, CAP + 1, dtype=f), (P, 1))], 1)
    tok = np.arange(L)

    def angles(pos, half):
        inv = (f(10000.0) ** (-np.arange(half, dtype=f) / f(half))).astype(f)
        a = pos.astype(f)[:, None] * inv[None, :]
        return np.cos(a).astype(f), np.sin(a).astype(f)

    def table(pos_of, half, width, rope_width):
        cs, sn = np.ones((P, L), f), np.zeros((P, L), f)
        for p in range(P):
            d = p % width
            if d < rope_width:
                cc, ss = angles(pos_of(d), half)
                j = d % (2 * half)
                cs[p] = cc[:, j % half]
                sn[p] = ss[:, j % half] * (-1 if j < half else 1)
        return cs, sn

    na = table(lambda d: tok // GRID_W if d < 32 else tok % GRID_W, 16, 64, 64)
    ab = table(lambda d: tok, 32, 64, 64)
    cr = table(lambda d: tok, 16, 32, 32)
    plain = np.ones((64, L), f)
    turned = np.concatenate([cr[0][:32], cr[1][:32]])
    cq_even, cq_odd = np.concatenate([plain, turned]), np.concatenate([turned, plain])
    ci = np.concatenate([turned, plain[:32], 0 * plain[:32]])
    s = f(HD ** -0.5)
    tab = np.stack([na[0] * s, na[1] * s, na[0], na[1], ab[0] * s, ab[1] * s, ab[0], ab[1],
                    cq_even, cq_odd, ci], 1)
    cc, ss = angles(tok, 16)
    tokt = np.stack([np.concatenate([cc] * 4, 1), np.concatenate([-ss, ss] * 2, 1)], 1)
    tokt = tokt.reshape(TT, P, 2, 64).transpose(1, 0, 2, 3)
    q, k = tok[:, None], tok[None, :]
    causal = q >= k
    count = ((causal & (q - k <= 128)).astype(int) + (causal & ((q - k) % 4 == 0))
             + (causal & ((q - k) % 16 == 0)))
    cmask = np.where(causal, 0, NEG)
    wmask = np.where(count > 0, np.log(np.maximum(count, 1)), NEG)
    masks = np.stack([np.concatenate([m[:P, :P], m[P:, :]], 1) for m in (cmask, wmask)], 1).astype(f)
    return {"cst": cst, "tab": np.ascontiguousarray(tab.astype(f)), "tokt": np.ascontiguousarray(tokt),
            "masks": np.ascontiguousarray(masks)}


def layouts(v):
    a = {k: np.asarray(x) for k, x in v.items()}
    f = np.float32
    out = constants()
    col = lambda x: np.ascontiguousarray(x.reshape(-1, P).T)
    out["x"], out["ctx"] = a["x"][0], a["ctx"][0]
    out["cc"] = np.stack([col(a["c"][0]), col(a["c_ctx"])], 2)
    gb = SSD_W // SSD_G
    order = np.concatenate([np.concatenate([np.arange(g * gb, (g + 1) * gb),
                                            SSD_W + np.arange(g * SSD_N, (g + 1) * SSD_N),
                                            SSD_W + SSD_G * SSD_N + np.arange(g * SSD_N, (g + 1) * SSD_N)])
                            for g in range(SSD_G)])
    cw = a["ssd_conv_w"][0][:, order]
    pc = [col(a["b_ada"][0])] + [col(a["norm_" + n][0]) for n in ("pre_mix", "post_mix", "pre_ffn", "post_ffn")]
    pc += [cw.reshape(CONV, -1, P).transpose(2, 1, 0).reshape(P, -1), col(a["ssd_conv_b"][0][order])]
    pc += [col(a["ssd_norm"][0])]
    pc += [col(a["g_mix_pre_2"].ravel()), col(a["g_mlp_pre_2"].ravel()), col(a["g_cq_2"][0]),
           col(a["g_ckv_2"][0]), col(a["g_diff_sub_2"][0])]
    out["pcol"] = np.ascontiguousarray(np.concatenate(pc, 1))
    out["heads"] = np.concatenate([a[n][0] for n in ("ssd_a_log_fwd", "ssd_a_log_bwd", "ssd_dt_bias_fwd",
                                                     "ssd_dt_bias_bwd", "diff_lq1_2", "diff_lk1_2",
                                                     "diff_lq2_2", "diff_lk2_2", "ssd_d_skip")])[None, :]
    out["g_post"] = np.stack([a["g_mix_post_2"][0], a["g_mlp_post_2"][0],
                              a["g_mix_post_2"][1], a["g_mlp_post_2"][1]])
    tok = np.arange(L)
    r, w = tok // GRID_W, tok % GRID_W
    start = np.clip(w - NA_KW // 2, 0, GRID_W - NA_KW)
    ok = (w[None, :] >= start[:, None]) & (w[None, :] < start[:, None] + NA_KW)
    dr = r[None, :] - r[:, None] + NA_KH - 1
    dc = np.clip(w[None, :] - w[:, None] + NA_KW - 1, 0, 2 * NA_KW - 2)
    bias = np.where(ok[None], a["na_rpb"][0][:, dr, dc], f(NEG)).astype(f)
    out["na_bias"] = np.ascontiguousarray(bias.reshape(NA_HEADS, TT, P, L).transpose(0, 2, 1, 3))
    out["w_ada"], out["w_in"] = a["w_ada"][0], a["w_in"][0]
    out["w_na"], out["w_ssd"], out["w_out"] = a["w_branch_na"][0], a["w_branch_ssd"][0], a["w_out"][0]
    out["w_router"] = a["w_router"][0]
    for n in ("gate", "up", "down"):
        out["w_e" + n] = a["w_exp_" + n][0]
    out["pT"] = np.ascontiguousarray(a["p_2"][:, 0].transpose(0, 2, 1))
    for n in ("mlp_in", "mlp_out", "ple_proj", "ple_gate"):
        out["w_" + n] = a["w_" + n + "_2"]
    out["w_ab"], out["w_oab"] = a["w_in_ab_2"][0], a["w_out_ab_2"][0]
    out["w_c"], out["w_oc"] = a["w_in_c_2"][0], a["w_out_c_2"][0]
    uq = a["w_uq_2"][0].reshape(CQ, C_HEADS // 2, 2, CNOPE + CROPE)
    plain, rotated = np.arange(CNOPE), np.arange(CROPE)
    even = np.concatenate([plain, CNOPE + rotated, CNOPE + (rotated ^ 16)])
    odd = np.concatenate([CNOPE + rotated, CNOPE + (rotated ^ 16), plain])
    out["w_uq"] = np.stack([uq[:, :, 0][:, :, even], uq[:, :, 1][:, :, odd]], 2).reshape(CQ, -1)
    qi = a["w_qi_2"][0].reshape(CQ, IDX_HEADS, 64)
    out["w_qi"] = qi[:, :, np.concatenate([rotated, rotated ^ 16, 32 + rotated, 32 + rotated])].reshape(CQ, -1)
    out["w_uk"] = a["w_uk_2"][0].reshape(CKV, -1)
    out["w_uv"] = a["w_uv_2"][0].reshape(CKV, -1)
    return {k: np.ascontiguousarray(x) for k, x in out.items()}


def build(nc, d, out):
    es = ExitStack()
    with es:
        def sb(name, shape, dt=F32):
            return es.enter_context(nc.sbuf_tensor(name, shape, dt))

        def sem(name):
            return es.enter_context(nc.semaphore(name))

        next_byte = lambda: -(-nc.sbuf_base // 32) * 32
        ring_at = next_byte()
        ring = sb("ring", [P, SLOTS, SLOT])
        ring_parts = nc.alloc_sbuf_tensor_at("ring_parts", [P, SLOTS, SLOT], F32R, offset=ring_at)
        work_at = next_byte()
        work = sb("work", [P, WORK])

        def parts_in_work(name, shape, at):
            return nc.alloc_sbuf_tensor_at(name, shape, F32R, offset=work_at + 4 * at)
        late_at = next_byte()
        late = sb("late", [P, 4 * D])
        hT_lo = nc.alloc_sbuf_tensor_at("hT_lo", [P, KT, 2 * L], F32R, offset=late_at)
        xres = late[:, 0:TT * D].rearrange("p (t n) -> p t n", t=TT)
        grow = late[:, TT * D:3 * D]
        tab = late[:, 3 * D:4 * D].rearrange("p (i l) -> p i l", l=L)
        cst = sb("cst", [P, NCST])
        tokt = sb("tokt", [P, TT, 2, 64])
        masks = sb("masks", [P, 2, 3 * P])
        pcol = sb("pcol", [P, NPCOL])
        heads = sb("heads", [P, SKIP0 + SSD_HEADS])
        router = sb("router", [P, KT, NE])
        mod = sb("mod", [P, 48])
        modc = sb("modc", [P, 16])
        mul1 = sb("mul1", [P, 2, KT])
        mul2 = sb("mul2", [P, KT])
        gain = sb("gain", [P, 2, KT])
        lam = sb("lam", [P, 8])
        sT = sb("sT", [P, KT, 32])
        small = sb("small", [P, 64])
        epsc = sb("epsc", [P, 1])
        bank = [es.enter_context(nc.psum_tensor(f"bank{i}", [P, 512], F32)) for i in range(8)]

        def cm(name):
            i = CST.index(name) * P
            return cst[:, i:i + P]

        tab_na = work[:, WORK - 8 * L:WORK - 4 * L].rearrange("p (i l) -> p i l", l=L)

        def tb(name):
            return (tab_na if name.startswith("na") else tab)[:, TAB.index(name) % 4, :]

        def pc(name, i, n=1):
            return pcol[:, PCOL[name] + i:PCOL[name] + i + n]

        ident, ones = cm("ident"), cm("ones")
        numbers = cst[:, len(CST) * P:NCST]

        class Region:

            def __init__(self, at=0, end=WORK):
                self.at, self.end = at, end

            def take(self, *dims):
                n = int(np.prod(dims))
                v = work[:, self.at:self.at + n]
                self.at += n
                assert self.at <= self.end, self.at
                if len(dims) == 1:
                    return v
                names = "abcde"[:len(dims)]
                return v.rearrange(f"p ({' '.join(names)}) -> p {' '.join(names)}", **dict(zip(names, dims)))

        consts_in = sem("consts_in")
        tables_in = sem("tables_in")
        x_in = sem("x_in")
        slot_full = [sem(f"slot_full{i}") for i in range(SLOTS)]
        chunk_used = sem("chunk_used")
        stage_end = sem("stage_end")
        eps_ready = sem("eps_ready")
        gemm_ready, gemm_freed = sem("gemm_ready"), sem("gemm_freed")
        rows_ready = sem("rows_ready")
        dve_step, act_step, pool_step = sem("dve_step"), sem("act_step"), sem("pool_step")
        grow_in, grow_loaded = sem("grow_in"), sem("grow_loaded")
        sT_ready, ada_ready, ada_copied, ada_cols, ada_done = (sem(n) for n in (
            "sT_ready", "ada_ready", "ada_copied", "ada_cols", "ada_done"))
        pads_ready, first_turned = sem("pads_ready"), sem("first_turned")
        gdiag_ready, grow_ready = sem("gdiag_ready"), sem("grow_ready")
        sq_done, std_done, xn_done, tr_ready = (sem(n) for n in ("sq_done", "std_done", "xn_done", "tr_ready"))
        post_std, x_done, norm_std, norm_done, turn_ready = (sem(n) for n in (
            "post_std", "x_done", "norm_std", "norm_done", "turn_ready"))
        raw_ready, swap_ready, swap_freed, rope_done = (sem(n) for n in (
            "raw_ready", "swap_ready", "swap_freed", "rope_done"))
        bias_in = [sem(f"bias_in{i}") for i in range(BIASES)]
        att_scores, att_biased, att_exp, att_probs, att_turned, att_copied, att_out, att_stored = (sem(n) for n in (
            "att_scores", "att_biased", "att_exp", "att_probs", "att_turned", "att_copied", "att_out", "att_stored"))

        counts = {}

        def stepper(eng, s):
            def link(ins):
                counts[id(s)] = counts.get(id(s), 0) + 1
                ins.then_inc(s, 1)
                eng.wait_ge(s, counts[id(s)])
            return link

        barriers = {}

        def end_stage(eng, who):
            barriers[who] = barriers.get(who, 0) + 1
            eng.drain().then_inc(stage_end, 1)
            eng.wait_ge(stage_end, 4 * barriers[who])

        ADA_AFTER = {"q0": (("ada4", 1),), "k0": (("ada5", 1),), "v0": (("ada6", 1), ("ada7", 1)),
                     "q1": (("ada8", 1),), "k1": (("ada9", 1),), "v1": (("ada10", 1), ("ada11", 1))}
        GROUP, groups = {}, 0
        for name, n in ([(n, c) for h in (0, 1) for t in "qkv" for n, c in ((f"{t}{h}", 4),) + ADA_AFTER[f"{t}{h}"]] + [("dt", 1)]
                        + [(f"{t}{g}", n) for g in range(SSD_G) for t, n in (("xs", 4), ("bc", 2), ("z", 4))]
                        + [("gates", 16), ("na", 8), ("ssd", 8)]
                        + [("aq", 4), ("ak", 4), ("av", 2), ("bq", 4), ("bk", 4), ("bv", 2), ("up0", 32), ("ple0", 8)]
                        + [("cin", 4), ("qi", 8), ("uk", 8), ("uv", 4), ("uq", 16), ("up1", 32), ("ple1", 8)]):
            GROUP[name] = groups
            groups += n

        CHUNK, chunks, NAME_OF = {}, [], {}
        used = [0]

        SPLIT = []

        def chunk(name, src, kt, n, released=None, split=False):
            if released is None:
                used[0] += 1
                released = (chunk_used, used[0])
            CHUNK[name] = len(chunks)
            NAME_OF[len(chunks)] = name
            chunks.append((src, kt, n, released))
            if split:
                assert kt * n <= SLOT // 2
                SPLIT.append(name)

        def rows_of(w, k0, k1, c0, c1):
            return w[k0:k1, c0:c1].rearrange("(t p) n -> p t n", p=P)

        def ada_chunk(i, released):
            chunk(f"ada{i}", rows_of(d["w_ada"], 0, D, 512 * i, 512 * i + 512), KT, 512, released)

        for i in range(ADA_FIRST):
            ada_chunk(i, (ada_ready, i + 1))

        def feature_chunks(name, w, c0, n, group):
            for u in range(n // 256):
                chunk(f"{name}_{u}", rows_of(w, 0, D, c0 + 256 * u, c0 + 256 * u + 256), KT, 256, (gemm_ready, group + 2 * u + 2), True)

        def token_chunks(name, w, c0, group_end):
            for u in range(2):
                chunk(f"{name}_{u}", rows_of(w, 512 * u, 512 * u + 512, c0, c0 + 512), 4, 512, (gemm_ready, group_end) if u else None, True)

        def narrow_chunk(name, c0, n, group_end):
            chunk(name, rows_of(d["w_in"], 0, D, c0, c0 + n), KT, n, (gemm_ready, group_end), True)

        for h in (0, 1):
            for i, t in enumerate("qkv"):
                if t == "v":
                    token_chunks(f"v{h}", d["w_in"], i * D + 512 * h, GROUP[f"v{h}"] + 4)
                else:
                    feature_chunks(f"{t}{h}", d["w_in"], i * D + 512 * h, 512, GROUP[f"{t}{h}"])
                for n, _ in ADA_AFTER[f"{t}{h}"]:
                    ada_chunk(int(n[3:]), (gemm_ready, GROUP[n] + 1))
        Z0, X0, DT0 = 3 * D, 3 * D + SSD_W, 3 * D + SSD_W + SSD_W + 2 * SSD_G * SSD_N
        G0 = DT0 + 2 * SSD_HEADS
        narrow_chunk("dt", DT0, 2 * SSD_HEADS, GROUP["dt"] + 1)
        for g in range(SSD_G):
            feature_chunks(f"xs{g}", d["w_in"], X0 + 512 * g, 512, GROUP[f"xs{g}"])
            b0 = X0 + SSD_W + SSD_N * g
            narrow_chunk(f"b{g}", b0, SSD_N, GROUP[f"bc{g}"] + 1)
            narrow_chunk(f"c{g}", b0 + SSD_G * SSD_N, SSD_N, GROUP[f"bc{g}"] + 2)
            feature_chunks(f"z{g}", d["w_in"], Z0 + 512 * g, 512, GROUP[f"z{g}"])
        feature_chunks("gates", d["w_in"], G0, 2 * D, GROUP["gates"])
        feature_chunks("na", d["w_na"], 0, D, GROUP["na"])
        for u in range(4):
            for k in range(2):
                chunk(f"ssd_{u}{k}", rows_of(d["w_ssd"], D * k, D * k + D, 256 * u, 256 * u + 256), KT, 256,
                      (gemm_ready, GROUP["ssd"] + 2 * u + 2) if k else None, True)
        ROWS = {}
        nrows = [0]

        def rows_chunks(name, w, split=False):
            ROWS[name] = nrows[0]
            nrows[0] += 4
            for h in range(2):
                for u in range(1 + split):
                    n = D // (1 + split)
                    chunk(f"{name}{h}{u}", rows_of(w, n * u, n * u + n, 512 * h, 512 * h + 512), n // P, 512,
                          (rows_ready, ROWS[name] + 3 + h), split)

        rows_chunks("out", d["w_out"], True)
        FIRST_EXPERT = len(chunks)
        UPS, DOWNS = DFF // 256, DFF // 512
        chunks.extend([None] * (12 * NE))

        DOWN_ORDER = ([(i, h) for i in range(DOWNS - 2) for h in range(2)]
                      + [(i, h) for h in range(2) for i in (DOWNS - 2, DOWNS - 1)])

        def second_layer_chunks(l, w_o):
            rows_chunks(f"o{l}", w_o)
            for i in range(UPS):
                chunk(f"up{l}{i}", rows_of(d["w_mlp_in"][l], 0, D, 256 * i, 256 * i + 256), KT, 256,
                      (gemm_ready, GROUP[f"up{l}"] + 2 * i + 2), True)
            ROWS[f"dn{l}"] = nrows[0]
            nrows[0] += 4
            for i, h in DOWN_ORDER:
                last = i - (DOWNS - 2)
                chunk(f"dn{l}{i}{h}", rows_of(d["w_mlp_out"][l], 512 * i, 512 * i + 512, 512 * h, 512 * h + 512), 4, 512,
                      None if last < 1 else (rows_ready, ROWS[f"dn{l}"] + 3 + h), True)
            for i in range(2):
                chunk(f"pg{l}{i}", rows_of(d["w_ple_gate"][l], 0, D, 512 * i, 512 * i + 512), KT, 512,
                      (gemm_ready, GROUP[f"ple{l}"] + 5 + i))
            chunk(f"pp{l}", rows_of(d["w_ple_proj"][l], 0, 256, 0, D), 2, D, (gemm_ready, GROUP[f"ple{l}"] + 8))

        for i, n in enumerate(("aq", "ak", "av", "bq", "bk", "bv")):
            if n[1] == "v":
                token_chunks(n, d["w_ab"], 512 * i, GROUP[n] + TT)
            else:
                feature_chunks(n, d["w_ab"], 512 * i, 512, GROUP[n])
        second_layer_chunks(0, d["w_oab"])
        chunk("cin1", rows_of(d["w_c"], 0, D, 512, 744), KT, 232, (gemm_ready, GROUP["cin"] + 2))
        chunk("cin0", rows_of(d["w_c"], 0, D, 0, 512), KT, 512, (gemm_ready, GROUP["cin"] + 4))
        chunk("qi", rows_of(d["w_qi"], 0, CQ, 0, D), 3, D, (gemm_ready, GROUP["qi"] + IDX_HEADS))
        chunk("uk", rows_of(d["w_uk"], 0, CKV, 0, D), 2, D, (gemm_ready, GROUP["uk"] + C_HEADS // 2))
        chunk("uv", rows_of(d["w_uv"], 0, CKV, 0, D), 2, D, (gemm_ready, GROUP["uv"] + 4))
        for i in range(2):
            chunk(f"uq{i}", rows_of(d["w_uq"], 0, CQ, D * i, D * i + D), 3, D, (gemm_ready, GROUP["uq"] + 8 * i + 8))
        second_layer_chunks(1, d["w_oc"])

        def slot(name):
            c = CHUNK[name]
            _, kt, n, _ = chunks[c]
            return ring[:, c % SLOTS, 0:kt * n].rearrange("p (t n) -> p t n", t=kt)

        hi_made, lo_made = sem("hi_made"), sem("lo_made")

        def halves_of(name, memory):
            c = CHUNK[name]
            _, kt, n, _ = chunks[c]
            return [memory[:, c % SLOTS, i * SLOT // 2:i * SLOT // 2 + kt * n] for i in range(2)]

        def split_upper(act, name):
            c = CHUNK[name]
            act.wait_ge(slot_full[c % SLOTS], slot_count(c))
            act.copy(halves_of(name, ring_parts)[1], halves_of(name, ring)[0]).then_inc(hi_made, 1)

        def split_lower(pool, name):
            lo, hi = halves_of(name, ring_parts)
            pool.wait_ge(hi_made, SPLIT.index(name) + 1)
            pool.tensor_tensor(lo, halves_of(name, ring)[0], hi, ALU.subtract).then_inc(lo_made, 1)

        def split_after(split, eng, name):
            later = NAME_OF.get(CHUNK[name] + 3)
            if later in SPLIT:
                split(eng, later)

        def split_chunk(pe, name):
            _, kt, n, _ = chunks[CHUNK[name]]
            pe.wait_ge(lo_made, SPLIT.index(name) + 1)
            lo, hi = (x.rearrange("p (t n) -> p t n", t=kt) for x in halves_of(name, ring_parts))
            return hi, lo

        def product3(pe, out, a, b, start, stop):
            pe.matmul(out, a[0], b[0], start=start, stop=False)
            pe.matmul(out, a[0], b[1], start=False, stop=False)
            return pe.matmul(out, a[1], b[0], start=False, stop=stop)

        EXPERT_USES = 12 // SLOTS
        assert 12 % SLOTS == 0

        def slot_count(c):
            return 16 * (c // SLOTS + 1)

        def wait_chunk(pe, name):
            c = CHUNK[name]
            pe.wait_ge(slot_full[c % SLOTS], slot_count(c))


        def feat_groups(pe, name, blocks, rows, t0, t1, first, n_groups):
            for i in range(n_groups):
                n, block = first + i, blocks + i
                w = split_chunk(pe, name if name in CHUNK else f"{name}_{block // 2}")
                c = block % 2 * P
                if n >= 4:
                    pe.wait_ge(gemm_freed, n - 3)
                for k in range(KT):
                    last = product3(pe, bank[n % 4][:, 0:t1 - t0], [x[:, k, c:c + P] for x in w], [x[:, k, t0:t1] for x in rows],
                                    k == 0, k == KT - 1)
                last.then_inc(gemm_ready, 1)

        def token_groups(pe, name, rows, tiles, first):
            for u in range(2):
                w = split_chunk(pe, f"{name}_{u}")
                for i in range(tiles):
                    n = first + i
                    if u == 0 and n >= 4:
                        pe.wait_ge(gemm_freed, n - 3)
                    for k in range(4):
                        last = product3(pe, bank[n % 4][:, :], [x[:, 4 * u + k, i * P:(i + 1) * P] for x in rows], [x[:, k, :] for x in w],
                                        u == 0 and k == 0, u == 1 and k == 3)
                    if u == 1:
                        last.then_inc(gemm_ready, 1)
                if u == 0:
                    last.then_inc(chunk_used, 1)

        def feat_groups_whole(pe, name, blocks, act, t0, t1, first, n_groups):
            w = slot(name)
            wait_chunk(pe, name)
            kt = chunks[CHUNK[name]][1]
            for i in range(n_groups):
                n = first + i
                if n >= 4:
                    pe.wait_ge(gemm_freed, n - 3)
                for k in range(kt):
                    last = pe.matmul(bank[n % 4][:, 0:t1 - t0], w[:, k, (blocks + i) * P:(blocks + i + 1) * P],
                                     act[:, k, t0:t1], start=k == 0, stop=k == kt - 1)
                last.then_inc(gemm_ready, 1)

        def token_groups_whole(pe, name, act, tiles, width, first):
            w = slot(name)
            wait_chunk(pe, name)
            kt = chunks[CHUNK[name]][1]
            for i in tiles:
                n = first + i
                if n >= 4:
                    pe.wait_ge(gemm_freed, n - 3)
                for k in range(kt):
                    last = pe.matmul(bank[n % 4][:, 0:width], act[:, k, i * P:(i + 1) * P], w[:, k, 0:width],
                                     start=k == 0, stop=k == kt - 1)
                last.then_inc(gemm_ready, 1)

        def rows_product(pe, name, rows, before_last):
            for t in range(TT):
                for h in range(2):
                    if t == 0:
                        wait_chunk(pe, f"{name}{h}0")
                    if t == TT - 1 and h == 1:
                        before_last(pe)
                    w = slot(f"{name}{h}0")
                    for k in range(KT):
                        last = pe.matmul(bank[4 + 2 * t + h][:, :], rows[:, k, t * P:(t + 1) * P], w[:, k, :], start=k == 0, stop=k == KT - 1)
                    last.then_inc(rows_ready, 1)

        def rows_product3(pe, name, rows):
            for t in range(TT):
                for h in range(2):
                    for u in range(2):
                        w = split_chunk(pe, f"{name}{h}{u}")
                        for k in range(4):
                            last = product3(pe, bank[4 + 2 * t + h][:, :], [x[:, 4 * u + k, t * P:(t + 1) * P] for x in rows],
                                            [x[:, k, :] for x in w], u == 0 and k == 0, u == 1 and k == 3)
                    last.then_inc(rows_ready, 1)

        nrm = {"act": [0, 0], "dve": [0, 0, 0], "pe": [0, 0, 0]}

        def first_norm_act(act, src, junk):
            link = stepper(act, act_step)
            n = len(src)
            for i, s in enumerate(src):
                act.activation(junk[i], s, ACT.Square, accum_out=small[:, i:i + 1]).then_inc(sq_done, 1)
            nrm["act"][0] += n
            act.wait_ge(sq_done, nrm["act"][0])
            act.activation(small[:, 8:8 + n], small[:, 0:n], ACT.Sqrt, bias=epsc[:, :], scale=1.0 / D).then_inc(std_done, 1)

        def first_norm_dve(dve, src, xn):
            link = stepper(dve, dve_step)
            n = len(src)
            nrm["dve"][0] += 1
            dve.wait_ge(std_done, nrm["dve"][0])
            link(dve.reciprocal(small[:, 16:16 + n], small[:, 8:8 + n]))
            for i, s in enumerate(src):
                dve.tensor_scalar(xn[i], s, small[:, 16 + i:17 + i], None, ALU.mult).then_inc(xn_done, 1)

        def first_turn_pe(pe, xn):
            n = len(xn)
            nrm["pe"][0] += n
            pe.wait_ge(xn_done, nrm["pe"][0])
            for k in range(KT):
                g = nrm["pe"][1]
                nrm["pe"][1] += 1
                if g >= 2:
                    pe.wait_ge(whole_made, 2 * g - 2)
                    pe.wait_ge(upper_made, 2 * g - 2)
                for i in range(n):
                    last = pe.transpose(bank[2 * (g % 2) + i // TT][:, i % TT * P:(i % TT + 1) * P], xn[i][:, k * P:(k + 1) * P], ident)
                last.then_inc(tr_ready, 1)

        MERGE, EXPERTS, ATTENTION, MLP, PLE, LATENT = range(6)
        POSTED, NORMED = [0, 1, 2, 3, 5, 6], [0, 1, 2, 4, 5]
        x_halves = [[xres[:, t, 512 * h:512 * h + 512] for h in range(2)] for t in range(TT)]
        hn = work[:, 0:KT * L].rearrange("p (k l) -> p k l", k=KT)
        hn_hi = parts_in_work("hn_hi", [P, KT, L], 0)
        xnm = work[:, KT * L:KT * L + TT * D].rearrange("p (t n) -> p t n", t=TT)
        AFTER_N = KT * L + TT * D
        hn_lo = parts_in_work("hn_lo", [P, KT, L], AFTER_N)

        def root_of_rows(act, halves, junk, c, done):
            link = stepper(act, act_step)
            for h, (ready, n, src) in enumerate(halves):
                act.wait_ge(ready, n)
                link(act.activation(junk[h], src, ACT.Square, accum_out=small[:, c + h:c + h + 1]))
                if h == 0:
                    link(act.activation(small[:, c + 2:c + 3], small[:, c:c + 1], ACT.Identity, bias=epsc[:, :], scale=1.0 / D))
            act.activation(small[:, c + 3:c + 4], small[:, c + 1:c + 2], ACT.Sqrt, bias=small[:, c + 2:c + 3], scale=1.0 / D).then_inc(done, 1)

        def norm_act(act, end, t):
            root_of_rows(act, [(x_done, 4 * end + 2 * t + h + 1, x_halves[t][h]) for h in range(2)],
                         [xnm[:, t, 512 * h:512 * h + 512] for h in range(2)], 48 + 8 * t, norm_std)

        def norm_dve(dve, end, t):
            link = stepper(dve, dve_step)
            c = 52 + 8 * t
            dve.wait_ge(x_done, 4 * end + 2 * t + 2)
            dve.wait_ge(norm_std, 2 * NORMED.index(end) + t + 1)
            link(dve.reciprocal(small[:, c:c + 1], small[:, c - 1:c]))
            dve.tensor_scalar(xnm[:, t, :], xres[:, t, :], small[:, c:c + 1], None, ALU.mult).then_inc(norm_done, 1)

        def turn_tile(pe, end, t):
            if end in NORMED:
                pe.wait_ge(norm_done, 2 * NORMED.index(end) + t + 1)
                src = xnm[:, t, :]
            else:
                pe.wait_ge(x_done, 4 * end + 2 * t + 2)
                src = xres[:, t, :]
            for j in range(2):
                for k in range(4):
                    last = pe.transpose(bank[2 * t + j][:, k * P:(k + 1) * P], src[:, (4 * j + k) * P:(4 * j + k + 1) * P], ident)
                last.then_inc(turn_ready, 1)

        def turned_tile(dve, end, t, mul=None, add=None, parts=False):
            link = stepper(dve, dve_step)
            for j in range(2):
                dve.wait_ge(turn_ready, 4 * end + 2 * t + j + 1)
                dst = hn[:, 4 * j:4 * j + 4, t * P:(t + 1) * P]
                src = bank[2 * t + j][:, :].rearrange("p (k q) -> p k q", k=4)
                if mul is None:
                    dve.tensor_copy(dst, src)
                elif add is None:
                    m = mul[:, 4 * j:4 * j + 4].unsqueeze(2).broadcast_to([P, 4, P])
                    if not parts:
                        dve.tensor_tensor(dst, src, m, ALU.mult)
                        continue
                    link(dve.tensor_tensor(hn_hi[:, 4 * j:4 * j + 4, t * P:(t + 1) * P], src, m, ALU.mult))
                    for k in range(4):
                        i = 4 * j + k
                        dve.scalar_tensor_tensor(hn_lo[:, i, t * P:(t + 1) * P], src[:, k, :], mul[:, i:i + 1],
                                                 hn_hi[:, i, t * P:(t + 1) * P], ALU.mult, ALU.subtract)
                else:
                    for k in range(4):
                        i = 4 * j + k
                        ins = dve.tensor_scalar(dst[:, k, :], src[:, k, :], mul[:, i:i + 1], add[:, i:i + 1], ALU.mult, ALU.add)
                    if t == 0 and j == 1:
                        ins.then_inc(first_turned, 1)

        def post_act(act, ready, counts_of, junk, t):
            root_of_rows(act, [(ready, counts_of[2 * t + h], bank[4 + 2 * t + h][:, :]) for h in range(2)],
                         [junk[:, 2 * t + h, :] for h in range(2)], 32 + 8 * t, post_std)

        def close_act(act, end, ready, counts_of, junk):
            for t in range(TT):
                post_act(act, ready, counts_of, junk, t)
                if end in NORMED:
                    norm_act(act, end, t)

        def close_dve(dve, end, tmp, mul=None, add=None, parts=False, together=False):
            link = stepper(dve, dve_step)

            def residual(t):
                c = 36 + 8 * t
                dve.wait_ge(post_std, 2 * POSTED.index(end) + t + 1)
                link(dve.reciprocal(small[:, c:c + 1], small[:, c - 1:c]))
                for h in range(2):
                    link(dve.scalar_tensor_tensor(tmp[:, 2 * t + h, :], bank[4 + 2 * t + h][:, :], small[:, c:c + 1],
                                                  grow[:, 512 * h:512 * h + 512], ALU.mult, ALU.mult))
                    x = x_halves[t][h]
                    dve.tensor_tensor(x, x, tmp[:, 2 * t + h, :], ALU.add).then_inc(x_done, 1)
            if together:
                for step in (residual, lambda t: norm_dve(dve, end, t), lambda t: turned_tile(dve, end, t, mul, add, parts)):
                    for t in range(TT):
                        step(t)
                return
            for t in range(TT):
                residual(t)
                if end in NORMED:
                    norm_dve(dve, end, t)
                turned_tile(dve, end, t, mul, add, parts)

        r1 = Region()
        AFTER_H = KT * 2 * L
        r1.take(AFTER_H)
        hT_hi = parts_in_work("hT_hi", [P, KT, 2 * L], 0)
        hT = hT_hi, hT_lo
        h_whole = r1.take(KT, 2 * L)
        xn1 = r1.take(4, D)
        x_early = r1.take(TT, D)
        ctx_in = r1.take(TT, D)
        cc = r1.take(KT, 2)
        ada_rows = r1.take(ADA_FIRST, 512)
        whole_made, upper_made = sem("whole_made"), sem("upper_made")
        mul1_ready = sem("mul1_ready")
        x_tiles = [x_early[:, t, :] for t in range(TT)] + [ctx_in[:, t, :] for t in range(TT)]

        def ada_act(act):
            act.dma_start(x_early, d["x"].rearrange("(t p) n -> p t n", p=P)).then_inc(x_in, 16)
            act.dma_start(ctx_in, d["ctx"].rearrange("(t p) n -> p t n", p=P)).then_inc(x_in, 16)
            act.wait_ge(consts_in, 16 * N_CONSTS)
            act.wait_ge(pads_ready, 1)
            act.activation(sT[:, :, 0:2], cc, ACT.Silu).then_inc(sT_ready, 1)
            act.wait_ge(x_in, 32)
            act.wait_ge(eps_ready, 1)
            first_norm_act(act, x_tiles, [xn1[:, i, :] for i in range(4)])
            split_after(split_upper, act, "ada1")
            act.wait_ge(mul1_ready, 1)
            for k in range(KT):
                act.wait_ge(tr_ready, k + 1)
                for i, m in ((1, modc), (0, mod)):
                    if i == 0:
                        act.wait_ge(whole_made, 2 * k + 1)
                    act.activation(hT_hi[:, k, i * L:(i + 1) * L], bank[2 * (k % 2) + i][:, 0:L], ACT.Identity,
                                   bias=m[:, k:k + 1], scale=mul1[:, i, k:k + 1]).then_inc(upper_made, 1)
            split_after(split_upper, act, "ada2")

        def lower_rows(eng, k):
            eng.wait_ge(upper_made, 2 * k + 2)
            eng.wait_ge(whole_made, 2 * k + 2)
            eng.tensor_tensor(hT_lo[:, k, :], h_whole[:, k, :], hT_hi[:, k, :], ALU.subtract)

        def ada_pool(pool):
            split_after(split_lower, pool, "ada1")
            for k in range(0, KT, 2):
                lower_rows(pool, k)

        def ada_set(pe, i, b):
            wait_chunk(pe, f"ada{i}")
            w = slot(f"ada{i}")
            for k in range(KT):
                j = k % 4
                last = pe.matmul(b[32 * j:32 * j + 32, :], sT[:, k, :], w[:, k, :], start=k < 4, stop=k >= 4, tile_position=(0, 32 * j))
            return last

        def ada_turn(pe, blocks, rows, b):
            for i in blocks:
                last = pe.matmul(b[:, 2 * i:2 * i + 2], rows[:, i // 4, (i % 4) * P:(i % 4 + 1) * P], pick[:, :], start=True, stop=True)
            return last

        def ada_pe(pe):
            pe.wait_ge(sT_ready, 1)
            for i in range(ADA_FIRST):
                ada_set(pe, i, bank[i]).then_inc(ada_ready, 1)
            pe.wait_ge(ada_copied, ADA_FIRST)
            ada_turn(pe, range(4 * ADA_FIRST), ada_rows, bank[4]).then_inc(ada_cols, 1)
            first_turn_pe(pe, [xn1[:, i, :] for i in range(4)])

        def ada_dve(dve):
            link = stepper(dve, dve_step)
            dve.memset(epsc[:, :], EPS).then_inc(eps_ready, 1)
            dve.memset(sT[:, :, :], 0.0).then_inc(pads_ready, 1)
            dve.wait_ge(consts_in, 16 * N_CONSTS)
            p4 = ident.rearrange("p (j i) -> p i j", i=32)
            link(dve.tensor_reduce(pick[:, :], p4[:, 0:2, :], AX.X, ALU.add))
            dve.wait_ge(x_in, 32)
            first_norm_dve(dve, x_tiles, [xn1[:, i, :] for i in range(4)])
            for i in range(ADA_FIRST):
                dve.wait_ge(ada_ready, i + 1)
                dve.tensor_copy(ada_rows[:, i, :], bank[i][:, :]).then_inc(ada_copied, 1)
            dve.wait_ge(ada_cols, 1)
            n = 4 * ADA_FIRST
            cols = bank[4][:, 0:2 * n].rearrange("p (b i) -> p i b", i=2)
            link(dve.tensor_tensor(mod[:, 0:n], cols[:, 0, :], pc("b_ada", 0, n), ALU.add))
            link(dve.tensor_tensor(modc[:, :], cols[:, 1, :], pc("b_ada", 0, n), ALU.add))
            link(dve.scalar_tensor_tensor(mul1[:, 0, :], mod[:, 8:16], 1.0, pc("pre_mix", 0, 8), ALU.add, ALU.mult))
            dve.scalar_tensor_tensor(mul1[:, 1, :], modc[:, 8:16], 1.0, pc("pre_mix", 0, 8), ALU.add, ALU.mult).then_inc(mul1_ready, 1)
            dve.wait_ge(mul1_ready, 1)
            for k in range(KT):
                g = nrm["dve"][1]
                nrm["dve"][1] += 1
                dve.wait_ge(tr_ready, g + 1)
                for i, m in enumerate((mod, modc)):
                    if i == 1:
                        dve.wait_ge(upper_made, 2 * k + 1)
                    dve.tensor_scalar(h_whole[:, k, i * L:(i + 1) * L], bank[2 * (k % 2) + i][:, 0:L], mul1[:, i, k:k + 1],
                                      m[:, k:k + 1], ALU.mult, ALU.add).then_inc(whole_made, 1)
                if k >= 2 and k % 2 == 0:
                    lower_rows(dve, k - 1)
            lower_rows(dve, KT - 1)

        def ada_rest_pe():
            n = 4 * (12 - ADA_FIRST)

            def turn(i):
                def some(pe):
                    if i == 0:
                        pe.wait_ge(gemm_freed, GROUP["ada11"] + 1)
                    last = ada_turn(pe, range(i, i + 2), ada_more, bank[7])
                    if i + 2 == n:
                        last.then_inc(ada_cols, 1)
                return some
            return {3 + i // 2: turn(i) for i in range(0, n, 2)}

        def ada_rest_dve(dve):
            link = stepper(dve, dve_step)
            dve.wait_ge(ada_cols, 2)
            n0 = 4 * ADA_FIRST
            cols = bank[7][:, 0:2 * (48 - n0)].rearrange("p (b i) -> p i b", i=2)
            link(dve.tensor_tensor(mod[:, n0:48], cols[:, 0, :], pc("b_ada", n0, 48 - n0), ALU.add))
            link(dve.scalar_tensor_tensor(mul2[:, :], mod[:, 32:40], 1.0, pc("pre_ffn", 0, 8), ALU.add, ALU.mult))
            link(dve.tensor_tensor(gain[:, 0, :], mod[:, 16:24], pc("post_mix", 0, 8), ALU.mult))
            link(dve.tensor_tensor(gain[:, 1, :], mod[:, 40:48], pc("post_ffn", 0, 8), ALU.mult))

        pick = sb("pick", [P, 2])

        def grow_dve_in(dve, i, gdiag):
            for k in range(KT):
                dve.tensor_scalar(gdiag[:, k, :], ident, gain[:, i, k:k + 1], None, ALU.mult).then_inc(gdiag_ready, 1)

        def grow_pe(pe, i, gdiag):
            pe.wait_ge(gdiag_ready, KT * (i + 1))
            for h in range(2):
                pe.matmul(bank[4 + h][:, :], ones, gdiag[:, 4 * h:4 * h + 4, :], start=True, stop=True).then_inc(grow_ready, 1)

        def grow_out(copy, eng, i):
            for h in range(2):
                eng.wait_ge(grow_ready, 2 * i + h + 1)
                copy(grow[:, 512 * h:512 * h + 512], bank[4 + h][:, :]).then_inc(grow_in, 1)

        rope_n = {"act": 0, "pe": 0, "dve": 0}
        ROPE0 = WORK - 4 * L
        raw = work[:, ROPE0:ROPE0 + 2 * L].rearrange("p (i l) -> p i l", i=2)
        rp = work[:, ROPE0 + 2 * L:WORK].rearrange("p (i l) -> p i l", i=2)

        def rope_act(act, group, extra=None):
            n = rope_n["act"]
            rope_n["act"] += 1
            act.wait_ge(gemm_ready, group + 1)
            if n >= 2:
                act.wait_ge(rope_done, n - 1)
            if extra is not None:
                dst, src = extra
                link = stepper(act, act_step)
                link(act.copy(dst, src))
            act.copy(raw[:, n % 2, :], bank[group % 4][:, 0:L]).then_inc(gemm_freed, 1)

        def rope_pe(pe, group, swap):
            n = rope_n["pe"]
            rope_n["pe"] += 1
            pe.wait_ge(gemm_freed, group + 1)
            if n >= 2:
                pe.wait_ge(swap_freed, n - 1)
            pe.matmul(bank[4 + n % 2][:, 0:L], cm(swap), raw[:, n % 2, :], start=True, stop=True).then_inc(swap_ready, 1)

        def roped_groups(pe, name, rows, t1, swap, between):
            n = GROUP[name]
            for b in range(4):
                feat_groups(pe, name, b, rows, 0, t1, n + b, 1)
                if b:
                    rope_pe(pe, n + b - 1, swap)
            between()
            rope_pe(pe, n + 3, swap)

        def rope_dve(dve, cos, sin, outs):
            link = stepper(dve, dve_step)
            n = rope_n["dve"]
            rope_n["dve"] += 1
            dve.wait_ge(swap_ready, n + 1)
            if n:
                dve.wait_ge(rope_done, n)
            link(dve.tensor_tensor(rp[:, 0, :], raw[:, n % 2, :], cos, ALU.mult))
            dve.tensor_tensor(rp[:, 1, :], bank[4 + n % 2][:, 0:L], sin, ALU.mult).then_inc(swap_freed, 1)
            dve.wait_ge(swap_freed, n + 1)
            for i, (dst, p0, p1) in enumerate(outs):
                ins = dve.tensor_tensor(dst, rp[p0:p1, 0, :], rp[p0:p1, 1, :], ALU.add)
                if i < len(outs) - 1:
                    link(ins)
            ins.then_inc(rope_done, 1)

        AHEAD = 3
        stat = sb("stat", [P, AHEAD, 4])
        counted = {"sets": 0, "units": 0, "values": 0}

        class Attention:

            def __init__(self, units, parts, width, bias, scale, s, pr, turned, turned_banks):
                self.units, self.parts, self.width, self.bias = units, parts, width, bias
                self.scale, self.s, self.pr, self.turned, self.turned_banks = scale, s, pr, turned, turned_banks
                self.sets, self.first = counted["sets"], counted["units"]
                counted["sets"] += units * parts
                counted["units"] += units

            def turned_bank(self, u):
                return bank[self.turned_banks[u % len(self.turned_banks)]]

            before_bias = staticmethod(lambda dve, i: None)

        def att_pe(pe, A, scores, value, between={}):
            n = A.units * A.parts
            for step in range(n + AHEAD + 2):
                if step in between:
                    between[step](pe)
                if step < n:
                    if step >= AHEAD:
                        pe.wait_ge(att_biased, A.sets + step - AHEAD + 1)
                    scores(pe, step, bank[step % AHEAD]).then_inc(att_scores, 1)
                i = step - AHEAD
                if 0 <= i < n and i % A.parts == A.parts - 1:
                    u = i // A.parts
                    pe.wait_ge(att_probs, A.first + u + 1)
                    back = len(A.turned_banks)
                    if u >= back:
                        pe.wait_ge(att_copied, A.first + u - back + 1)
                    for k in range(A.width(u) // P):
                        last = pe.transpose(A.turned_bank(u)[:, k * P:(k + 1) * P], A.pr[:, u % AHEAD, k * P:(k + 1) * P], ident)
                    last.then_inc(att_turned, 1)
                i = step - AHEAD - 2
                if 0 <= i < n and i % A.parts == A.parts - 1:
                    value(pe, i // A.parts)

        def att_dve(dve, A, after, lam_of=None, between={}):
            link = stepper(dve, dve_step)
            n = A.units * A.parts
            for step in range(n + AHEAD + 4):
                if step in between:
                    between[step](dve)
                i = step
                if i < n:
                    A.before_bias(dve, i)
                    u, w = i // A.parts, A.width(i // A.parts)
                    dve.wait_ge(att_scores, A.sets + i + 1)
                    j = i - AHEAD
                    if j >= 0 and j % A.parts == A.parts - 1:
                        dve.wait_ge(att_probs, A.first + j // A.parts + 1)
                    st = stat[:, i % AHEAD, :]
                    link(dve.tensor_tensor_reduce(out=A.s[:, i % AHEAD, 0:w], in0=bank[i % AHEAD][:, 0:w], in1=A.bias(u), scale=1.0,
                                                  scalar=-3e38, op0=ALU.add, op1=ALU.max, accum_out=st[:, 0:1]))
                    dve.tensor_scalar(st[:, 1:2], st[:, 0:1], -A.scale, None, ALU.mult).then_inc(att_biased, 1)
                i = step - 1
                if 0 <= i < n:
                    u, w = i // A.parts, A.width(i // A.parts)
                    st = stat[:, i % AHEAD, :]
                    dve.wait_ge(att_exp, A.sets + i + 1)
                    link(dve.reciprocal(st[:, 3:4], st[:, 2:3]))
                    if i % A.parts == A.parts - 1 and u >= AHEAD:
                        dve.wait_ge(att_turned, A.first + u - AHEAD + 1)
                    e, pr = A.s[:, i % AHEAD, 0:w], A.pr[:, u % AHEAD, 0:w]
                    if A.parts == 1:
                        dve.tensor_scalar(pr, e, st[:, 3:4], None, ALU.mult).then_inc(att_probs, 1)
                    elif i % 2 == 0:
                        link(dve.tensor_scalar(lam_of[1][:, 0:w], e, st[:, 3:4], None, ALU.mult))
                    else:
                        link(dve.tensor_tensor(st[:, 3:4], st[:, 3:4], lam_of[0], ALU.mult))
                        dve.scalar_tensor_tensor(pr, e, st[:, 3:4], lam_of[1][:, 0:w], ALU.mult, ALU.add).then_inc(att_probs, 1)
                i = step - AHEAD - 4
                if 0 <= i < n and i % A.parts == A.parts - 1:
                    after(dve, i // A.parts)

        def att_act(act, A, turned_free, between={}):
            n = A.units * A.parts
            for step in range(n + AHEAD):
                if step in between:
                    between[step](act)
                i = step
                if i < n:
                    u, w = i // A.parts, A.width(i // A.parts)
                    st = stat[:, i % AHEAD, :]
                    act.wait_ge(att_biased, A.sets + i + 1)
                    s = A.s[:, i % AHEAD, 0:w]
                    act.activation(s, s, ACT.Exp, bias=st[:, 1:2], scale=A.scale, accum_out=st[:, 2:3]).then_inc(att_exp, 1)
                i = step - AHEAD
                if 0 <= i < n and i % A.parts == A.parts - 1:
                    u = i // A.parts
                    act.wait_ge(att_turned, A.first + u + 1)
                    turned_free(act, u)
                    k = A.width(u) // P
                    act.copy(A.turned(u), A.turned_bank(u)[:, 0:k * P].rearrange("p (k q) -> p k q", q=P)).then_inc(att_copied, 1)

        def head_values(A, v, PT, heads, causal, first, store):
            def value(pe, u):
                h, qt = u // 2, u % 2
                if qt == 0:
                    return
                blk, side = h // 2, h % 2
                pe.wait_ge(att_copied, A.first + u + 1)
                if side == 0 and blk >= 2:
                    pe.wait_ge(att_stored, first // 2 + blk - 1)
                n = A.width(1) // P
                o = bank[4 + blk % 2][64 * side:64 * side + 64, :]
                for k in range(n):
                    q0 = P if causal and k == 1 else 0
                    last = pe.matmul(o[:, q0:L], v[:, k, HD * h:HD * h + HD], PT[:, h % 2, k, q0:L], start=k == 0, stop=k == n - 1)
                last.then_inc(att_out, 1)

            def after(dve, u):
                h, qt = u // 2, u % 2
                if qt == 0 or h % 2 == 0:
                    return
                dve.wait_ge(att_out, first + h + 1)
                dve.tensor_copy(store(h // 2), bank[4 + (h // 2) % 2][:, 0:L]).then_inc(att_stored, 1)

            def turned_free(act, u):
                h = u // 2
                if h >= 2:
                    act.wait_ge(att_out, first + h - 1)
            counted["values"] += heads
            return value, after, turned_free

        r2 = Region(AFTER_H, ROPE0 - 4 * L)
        oT = r2.take(KT, L)
        AFTER_O = r2.at
        qz = r2.take(4, 2, L)
        kT = r2.take(4, 2 * L)
        v_na = r2.take(4, 512)
        na_bias = r2.take(BIASES, TT, 2 * L)
        s_na, pr_na, PT_na = r2.take(AHEAD, 512), r2.take(AHEAD, 512), r2.take(2, 4, L)
        ada_more = r2.take(12 - ADA_FIRST, 512)
        zero_ready = sem("zero_ready")

        NA = []
        for hf in (0, 1):
            A = Attention(16, 1, lambda u: 2 * L, lambda u, hf=hf: na_bias[:, (8 * hf + u // 2) % BIASES, u % 2, :], 1.0, s_na, pr_na,
                          lambda u: PT_na[:, (u // 2) % 2, :, (u % 2) * P:(u % 2 + 1) * P], (3, 6))

            def before(dve, i, hf=hf):
                h = 8 * hf + i // 2
                if i % 2 == 0:
                    dve.wait_ge(bias_in[h % BIASES], 16 * (h // BIASES + 1))
            A.before_bias = before
            A.hooks = head_values(A, v_na, PT_na, 8, False, counted["values"], lambda blk, hf=hf: oT[:, 4 * hf + blk, :])
            NA.append(A)

        def na_proj_pe(pe, hf):
            def ada_sets(t):
                for name, _ in ADA_AFTER[f"{t}{hf}"]:
                    n = GROUP[name]
                    pe.wait_ge(gemm_freed, n - 3)
                    ada_set(pe, int(name[3:]), bank[n % 4]).then_inc(gemm_ready, 1)

            for t, t1 in (("q", L), ("k", 2 * L)):
                roped_groups(pe, f"{t}{hf}", hT, t1, "swap16", lambda: ada_sets(t))
            token_groups(pe, f"v{hf}", hT, 4, GROUP[f"v{hf}"])
            ada_sets("v")

        def na_proj_act(act, hf):
            def ada_sets(t):
                for name, _ in ADA_AFTER[f"{t}{hf}"]:
                    n = GROUP[name]
                    act.wait_ge(gemm_ready, n + 1)
                    act.copy(ada_more[:, int(name[3:]) - ADA_FIRST, :], bank[n % 4][:, :]).then_inc(gemm_freed, 1)

            for b in range(4):
                rope_act(act, GROUP[f"q{hf}"] + b)
                if b % 2:
                    split_after(split_upper, act, f"q{hf}_{b // 2}")
            ada_sets("q")
            for b in range(4):
                g = GROUP[f"k{hf}"] + b
                rope_act(act, g, (kT[:, b, L:2 * L], bank[g % 4][:, L:2 * L]))
                if b % 2:
                    split_after(split_upper, act, f"k{hf}_{b // 2}")
            ada_sets("k")
            for i in range(4):
                g = GROUP[f"v{hf}"] + i
                act.wait_ge(gemm_ready, g + 1)
                act.copy(v_na[:, i, :], bank[g % 4][:, :]).then_inc(gemm_freed, 1)
            ada_sets("v")

        def na_proj_pool(pool, hf):
            for t in "qk":
                for u in range(2):
                    split_after(split_lower, pool, f"{t}{hf}_{u}")

        def next_splits(hf):
            return [n for n in (NAME_OF[CHUNK[f"v{hf}_0"] + i] for i in range(3, 7)) if n in SPLIT]

        def na_splits_act(hf):
            def split(name):
                return lambda act: split_upper(act, name)
            return {6 + 3 * i: split(name) for i, name in enumerate(next_splits(hf))}

        def na_proj_dve(dve, hf):
            link = stepper(dve, dve_step)
            if hf == 0:
                link(dve.memset(qz, 0.0))
            for b in range(4):
                rope_dve(dve, tb("na_qc"), tb("na_qs"), [(qz[0:64, b, 0, :], 0, 64), (qz[64:128, b, 1, :], 64, 128)])
            for b in range(4):
                rope_dve(dve, tb("na_kc"), tb("na_ks"), [(kT[:, b, 0:L], 0, 128)])

        def na_bias_pool(pool, hf, first, last):
            if hf == 0 and first == 0:
                pool.memset(na_bias, 0.0).then_inc(zero_ready, 1)
                pool.wait_ge(zero_ready, 1)
            for h in range(8 * hf + first, 8 * hf + last):
                if h >= BIASES:
                    pool.wait_ge(att_biased, 2 * (h - BIASES + 1))
                pool.dma_start(na_bias[:, h % BIASES, :, 0:L], d["na_bias"][h]).then_inc(bias_in[h % BIASES], 16)

        def na_scores_of(hf):
            def scores(pe, u, b):
                h, qt = u // 2, u % 2
                return pe.matmul(b[:, :], qz[:, h // 2, h % 2, qt * P:(qt + 1) * P], kT[:, h // 2, :], start=True, stop=True)
            return scores

        r3 = Region(AFTER_O)
        yT = r3.take(16, L)
        AFTER_Y = r3.at
        dtv = r3.take(4, 64)
        nacs = r3.take(TT, 64)
        eacs = r3.take(TT, 64)
        wctx = r3.take(TT, 64)
        zs = r3.take(GB, L)
        GATES_AT = r3.at
        cin = r3.take(2, 2, L + 4)
        cacc = r3.take(3, 2, L)
        conv = r3.take(5, 2, L)
        convC = r3.take(L)
        bst = r3.take(TT, P)
        xdt = r3.take(2, TT, GB * P)
        xw = r3.take(2, TT, GB * P)
        h0 = r3.take(2, GB * P)
        yoff = r3.take(TT, GB * P)
        yo2 = r3.take(GB * P)
        EMS = 3
        cbm = r3.take(6, P)
        Em = r3.take(EMS, 6, P)
        abc = r3.take(2, 2, L)
        ysq, rstd = r3.take(2, L), r3.take(L)
        sp = xdt.rearrange("p d t n -> p (d t n)")[:, 0:6 * 256].rearrange("p (i t h) -> p i t h", i=6, t=4)
        free = xw.rearrange("p d t n -> p (d t n)")
        av = free[:, 0:256].rearrange("p (t h) -> p t h", t=4)
        acs = free[:, 256:512].rearrange("p (t h) -> p t h", t=TT)
        AT = free[:, 512:768]
        nega = free[:, 768:832]
        sums = nc.dram_tensor("sums", (2, SSD_HEADS, L), F32).ap()
        TILES_OF = (((0, 0, 2, 0), (1, 2, 3, P)), ((0, 3, 4, 0), (1, 4, 6, 0)))
        (dt_abs, dt_exp, dt_one, dt_ln, dt_ready, acs_ready, acs_done, at_ready, wct_done, at_done, negA_done, ctxw_done,
         sums_out) = (sem(n) for n in (
            "dt_abs", "dt_exp", "dt_one", "dt_ln", "dt_ready", "acs_ready", "acs_done", "at_ready", "wct_done", "at_done",
            "negA_done", "ctxw_done", "sums_out"))
        (pad_zero, conv_done, conv_silu, xt_ready, xt_done, xw_done, h0_ready, h0_done, yoff_ready, yoff_done, cb_ready,
         cb_done, seg_added, seg_exp, seg_done, y_ready, y_gated, y_sq, y_tot, y_std, y_norm) = (sem(n) for n in (
             "pad_zero", "conv_done", "conv_silu", "xt_ready", "xt_done", "xw_done", "h0_ready", "h0_done", "yoff_ready",
             "yoff_done", "cb_ready", "cb_done", "seg_added", "seg_exp", "seg_done", "y_ready", "y_gated", "y_sq",
             "y_tot", "y_std", "y_norm"))
        seg_added_b = sem("seg_added_b")
        abc_in = [sem(f"abc_in{i}") for i in range(2)]
        XB = GB + 2

        def conv_of(b):
            return conv[:, b] if b < 5 else convC.unsqueeze(1)

        def x_block(pe, g, b):
            name, i, t1 = ((f"xs{g}", b, 2 * L), (f"b{g}", 0, 2 * L), (f"c{g}", 0, L))[max(0, b - GB + 1)]
            feat_groups(pe, name, i, hT, 0, t1, GROUP[f"xs{g}"] + b, 1)

        def dt_product(pe):
            w, n = split_chunk(pe, "dt"), GROUP["dt"]
            if n >= 4:
                pe.wait_ge(gemm_freed, n - 3)
            for i in range(4):
                for k in range(KT):
                    last = product3(pe, bank[n % 4][:, 64 * i:64 * i + 64], [x[:, k, i * P:(i + 1) * P] for x in hT], [x[:, k, :] for x in w],
                                    k == 0, k == KT - 1)
            last.then_inc(gemm_ready, 1)

        def dt_sums(pe):
            pe.wait_ge(dt_ready, 1)
            F, B = slice(0, 32), slice(32, 64)

            def total(col, terms):
                for i, (m, tile, cols) in enumerate(terms):
                    r = pe.matmul(bank[4][:, col:col + 32], m, av[:, tile, cols], start=i == 0, stop=i == len(terms) - 1)
                return r
            le, ge, gt, lt = cm("le"), cm("ge"), cm("gt"), cm("lt")
            total(0, [(le, 0, F)])
            total(32, [(ge, 0, B), (ones, 1, B)])
            total(64, [(le, 1, F), (ones, 0, F)])
            total(96, [(ge, 1, B)])
            total(128, [(gt, 2, F), (ones, 3, F)])
            total(160, [(lt, 2, B)])
            total(192, [(gt, 3, F)])
            total(224, [(lt, 3, B), (ones, 2, B)]).then_inc(acs_ready, 1)

        def dt_turn(pe):
            pe.wait_ge(acs_done, 1)
            for t in range(TT):
                last = pe.transpose(bank[5][:, t * P:(t + 1) * P], acs[:, t, :], ident)
            last.then_inc(at_ready, 1)

        def dt_act(act):
            act.activation(nega, heads[:, 0:64], ACT.Exp).then_inc(negA_done, 1)
            act.wait_ge(dt_abs, 1)
            act.activation(sp[:, 2], sp[:, 1], ACT.Exp).then_inc(dt_exp, 1)
            act.wait_ge(dt_one, 1)
            act.activation(sp[:, 4], sp[:, 3], ACT.Ln).then_inc(dt_ln, 1)

        def sums_act(act):
            act.wait_ge(acs_ready, 1)
            act.wait_ge(acs_done, 1)
            b = bank[4]
            act.activation(eacs, b[:, 0:128].rearrange("p (t h) -> p t h", t=TT), ACT.Exp).then_inc(ctxw_done, 1)
            act.activation(wctx, b[:, 128:256].rearrange("p (t h) -> p t h", t=TT), ACT.Exp).then_inc(ctxw_done, 1)

        def dt_dve(dve):
            link = stepper(dve, dve_step)
            n = GROUP["dt"]
            x, na, e, u, ln, t = (sp[:, i] for i in range(6))
            link(dve.memset(acs, 0.0))
            dve.wait_ge(gemm_ready, n + 1)
            ps = bank[n % 4][:, 0:256].rearrange("p (t h) -> p t h", t=4)
            dve.tensor_tensor(x, ps, heads[:, 64:128].unsqueeze(1).broadcast_to([P, 4, 64]), ALU.add).then_inc(gemm_freed, 1)
            dve.wait_ge(gemm_freed, n + 1)
            dve.scalar_tensor_tensor(na, x, -1.0, x, ALU.mult, ALU.min).then_inc(dt_abs, 1)
            dve.wait_ge(dt_exp, 1)
            dve.tensor_scalar(u, e, 1.0, None, ALU.add).then_inc(dt_one, 1)
            dve.wait_ge(dt_one, 1)
            link(dve.tensor_scalar(t, u, 1.0, None, ALU.is_equal))
            link(dve.scalar_tensor_tensor(na, u, -1.0, t, ALU.add, ALU.add))
            link(dve.reciprocal(na, na))
            link(dve.tensor_tensor(na, na, e, ALU.mult))
            dve.wait_ge(dt_ln, 1)
            link(dve.tensor_tensor(na, na, ln, ALU.mult))
            link(dve.tensor_tensor(t, t, e, ALU.mult))
            link(dve.tensor_tensor(na, na, t, ALU.add))
            link(dve.scalar_tensor_tensor(dtv, x, 0.0, na, ALU.max, ALU.add))
            dve.wait_ge(negA_done, 1)
            dve.scalar_tensor_tensor(av, dtv, -1.0, nega.unsqueeze(1).broadcast_to([P, 4, 64]), ALU.mult, ALU.mult).then_inc(dt_ready, 1)

        def sums_dve(dve):
            link = stepper(dve, dve_step)
            dve.wait_ge(acs_ready, 1)
            ps = bank[4][:, 0:128].rearrange("p (t h) -> p t h", t=TT)
            link(dve.tensor_scalar(nacs, ps, -1.0, None, ALU.mult))
            dve.tensor_copy(acs[:, :, 0:64], ps).then_inc(acs_done, 1)
            dve.wait_ge(ctxw_done, 2)
            dve.tensor_tensor(wctx, wctx, dtv[:, 2:4, :], ALU.mult).then_inc(wct_done, 1)
            dve.wait_ge(at_ready, 1)
            dve.tensor_copy(AT, bank[5][:, 0:L]).then_inc(at_done, 1)

        def add_decays(eng, n, dr, done):
            eng.wait_ge(abc_in[n % 2], 16 * (n // 2 + 1))
            if n >= EMS:
                eng.wait_ge(y_ready, n - EMS + 1)
            for s, c0, c1, l0 in TILES_OF[dr]:
                c = 32 * dr + n
                eng.tensor_scalar(Em[:, n % EMS, c0:c1, :].rearrange("p c l -> p (c l)"), abc[:, n % 2, dr, l0:l0 + (c1 - c0) * P],
                                  nacs[:, s, c:c + 1], 0.0, ALU.add, ALU.min).then_inc(done, 1)

        SPLIT_AT = {4: "xs{}_0", 6: "xs{}_1"}

        EARLY_GATES = 12

        def ssd_pool(pool):
            split_after(split_lower, pool, "dt")
            split_after(split_lower, pool, "xs0_0")
            pool.wait_ge(at_done, 1)
            pool.dma_start(sums.rearrange("d h l -> (d h) l"), AT[0:64, :]).then_inc(sums_out, 16)
            pool.wait_ge(sums_out, 16)
            for n in range(SSD_HEADS + 2):
                if n == 2:
                    for name in ("xs0_1", "b0", "c0"):
                        split_after(split_lower, pool, name)
                if n >= 2:
                    add_decays(pool, n - 2, 1, seg_added_b)
                    g, i = divmod(n - 2, GH)
                    if i == 0 and 0 < g:
                        split_after(split_lower, pool, f"b{g}")
                        split_after(split_lower, pool, f"c{g}")
                    if i in (1, 2) and g + 1 < SSD_G:
                        split_after(split_lower, pool, f"z{g}_{i - 1}")
                    elif i in SPLIT_AT and g + 1 < SSD_G:
                        split_after(split_lower, pool, SPLIT_AT[i].format(g + 1))
                if n < SSD_HEADS:
                    if n >= 2:
                        pool.wait_ge(seg_added, 2 * n - 2)
                        pool.wait_ge(seg_added_b, 2 * n - 2)
                    pool.dma_start(abc[:, n % 2], sums[:, n, :].partition_broadcast(P)).then_inc(abc_in[n % 2], 16)
            pool.wait_ge(lo_made, SPLIT.index("gates_5"))
            for u in range(2, EARLY_GATES // 2 - 1):
                split_after(split_lower, pool, f"gates_{u}")

        def product(pe, g, r):
            n = GH * g + r
            blk, side = r // 2, r % 2
            nb = GB * g + blk
            o = bank[4 + blk % 2]
            if side == 0:
                pe.wait_ge(yoff_done, 2 * g + 2)
                if blk >= 2:
                    pe.wait_ge(y_gated, nb - 1)
                for t in range(TT):
                    pe.matmul(o[:, t * P:(t + 1) * P], yoff[:, t, blk * P:(blk + 1) * P], ident, start=t == 0, stop=False,
                              skip_group_check=True)
            pe.wait_ge(seg_done, n + 1)
            oh = o[64 * side:64 * side + 64, :]
            for dr in range(2):
                for s, c0, c1, l0 in TILES_OF[dr]:
                    last = pe.matmul(oh[:, l0:l0 + (c1 - c0) * P], xdt[:, dr, s, r * HD:(r + 1) * HD], Em[:, n % EMS, c0:c1, :],
                                     start=False, stop=True, skip_group_check=True)
            last.then_inc(y_ready, 1)

        def squares_bank(g):
            return bank[4 if g < SSD_G - 1 else 6]

        def squares_sum(pe, g):
            for blk in range(GB):
                pe.wait_ge(y_sq, GB * g + blk + 1)
                pe.matmul(squares_bank(g)[:, 0:L], ones, ysq[:, blk % 2, :], start=blk == 0, stop=blk == GB - 1).then_inc(y_tot, 1)

        def ssd_pe(pe):
            dt_product(pe)
            for g in range(SSD_G + 1):
                for i in range(GH):
                    if g < SSD_G and i < XB:
                        x_block(pe, g, i)
                    elif g == SSD_G:
                        feat_groups(pe, "gates", i, hT, 0, L, GROUP["gates"] + i, 1)
                    if g:
                        product(pe, g - 1, i)
                    elif i == 1:
                        dt_sums(pe)
                    elif i == 2:
                        dt_turn(pe)
                if g == SSD_G:
                    for i in range(GH, EARLY_GATES):
                        feat_groups(pe, "gates", i, hT, 0, L, GROUP["gates"] + i, 1)
                        if i == GH:
                            squares_sum(pe, g - 1)
                    break

                def gate_block(b, g=g):
                    feat_groups(pe, f"z{g}", b, hT, 0, L, GROUP[f"z{g}"] + b, 1)

                def turn(i, g=g):
                    n = 5 * g + i
                    pe.wait_ge(conv_silu, XB * g + (GB + 1 if i == 4 else GB))
                    if i >= 2:
                        pe.wait_ge(xt_done, n - 1)
                    elif g:
                        pe.wait_ge(yoff_done, 2 * g)
                    for b in range(GB if i < 4 else TT):
                        src = conv[:, b, i // 2, (i % 2) * P:(i % 2 + 1) * P] if i < 4 else conv[:, 4, 1, b * P:(b + 1) * P]
                        last = pe.transpose(bank[6 + i % 2][:, b * P:(b + 1) * P], src, ident)
                    last.then_inc(xt_ready, 1)

                gate_block(0)
                turn(0)
                turn(1)
                gate_block(1)
                if g:
                    pe.wait_ge(y_gated, GB * g)
                    squares_sum(pe, g - 1)
                turn(2)
                turn(3)
                turn(4)
                gate_block(2)
                pe.wait_ge(conv_silu, XB * g + XB)
                pe.wait_ge(xt_done, 5 * g + 4)
                for s in range(TT):
                    last = pe.matmul(bank[7][:, s * L:(s + 1) * L], conv[:, 4, 0, s * P:(s + 1) * P], convC, start=True, stop=True)
                last.then_inc(cb_ready, 1)
                pe.wait_ge(xt_done, 5 * g + 5)
                for dr in range(2):
                    if dr == 1:
                        pe.wait_ge(cb_done, g + 1)
                    for t in range(TT):
                        pe.wait_ge(xw_done, 4 * g + 2 * t + dr + 1)
                        last = pe.matmul(bank[6 + dr][:, :], bst[:, t, :], xw[:, dr, t, :], start=t == 0, stop=t == TT - 1)
                    last.then_inc(h0_ready, 1)
                gate_block(3)
                pe.wait_ge(h0_done, 2 * g + 2)
                if g:
                    pe.wait_ge(y_std, g)
                for t in range(TT):
                    for dr in range(2):
                        last = pe.matmul(bank[4 + 2 * t + dr][:, :], convC[:, t * P:(t + 1) * P], h0[:, dr, :], start=True, stop=True)
                    last.then_inc(yoff_ready, 1)

        def ssd_act(act):
            def head_exp(n):
                act.wait_ge(seg_added, 2 * n + 2)
                act.wait_ge(seg_added_b, 2 * n + 2)
                act.activation(Em[:, n % EMS], Em[:, n % EMS], ACT.Exp).then_inc(seg_exp, 1)

            def take_block(g, b):
                m = XB * g + b
                n = GROUP[f"xs{g}"] + b
                act.wait_ge(gemm_ready, n + 1)
                act.wait_ge(pad_zero, 1)
                if m >= 2:
                    act.wait_ge(conv_done, m - 1)
                s = 2 if b < 5 else 1
                act.copy(cin[:, m % 2, 0:s, 2:L + 2], bank[n % 4][:, 0:s * L].rearrange("p (s l) -> p s l", s=s)).then_inc(gemm_freed, 1)

            def silu(g, b):
                m = XB * g + b
                act.wait_ge(conv_done, m + 1)
                if g:
                    act.wait_ge(yoff_ready, 2 * g)
                s = 2 if b < 5 else 1
                act.activation(conv_of(b), cacc[:, m % 3, 0:s], ACT.Silu).then_inc(conv_silu, 1)

            def squares(g):
                for blk in range(GB):
                    nb = GB * g + blk
                    act.wait_ge(y_gated, nb + 1)
                    if nb >= 2:
                        act.wait_ge(y_tot, nb - 1)
                    act.activation(ysq[:, blk % 2, :], yT[:, nb, :], ACT.Square).then_inc(y_sq, 1)
                act.wait_ge(y_tot, GB * g + GB)
                if g:
                    act.wait_ge(y_norm, GB * g)
                act.activation(rstd, squares_bank(g)[:, 0:L], ACT.Sqrt, bias=epsc[:, :], scale=1.0 / (GB * P)).then_inc(y_std, 1)

            def take_gate(i):
                n = GROUP["gates"] + i
                act.wait_ge(gemm_ready, n + 1)
                act.copy(gT[:, i, :], bank[n % 4][:, 0:L]).then_inc(gemm_freed, 1)
                if i % 2 and i + 1 < EARLY_GATES:
                    split_after(split_upper, act, f"gates_{i // 2}")

            dt_act(act)
            split_after(split_upper, act, "dt")
            for g in range(SSD_G + 1):
                for i in range(GH):
                    if g and i + 1 < GH:
                        head_exp(GH * (g - 1) + i + 1)
                    if g < SSD_G and i < XB:
                        take_block(g, i)
                        if i in (2, 4):
                            silu(g, i - 2)
                            silu(g, i - 1)
                        if i + 3 in SPLIT_AT:
                            split_after(split_upper, act, SPLIT_AT[i + 3].format(g))
                    if g < SSD_G and i >= XB:
                        split_after(split_upper, act, f"{'bc'[i - XB]}{g}")
                    if g == SSD_G:
                        take_gate(i)
                    if g == 0 and i == 1:
                        sums_act(act)
                if g == SSD_G:
                    squares(g - 1)
                    for i in range(GH, EARLY_GATES):
                        take_gate(i)
                    break
                silu(g, XB - 2)
                silu(g, XB - 1)

                def gate(b, g=g):
                    n = GROUP[f"z{g}"] + b
                    act.wait_ge(gemm_ready, n + 1)
                    if b == 0 and g:
                        act.wait_ge(y_gated, GB * g)
                    act.activation(zs[:, b, :], bank[n % 4][:, 0:L], ACT.Silu).then_inc(gemm_freed, 1)
                gate(0)
                gate(1)
                if g:
                    squares(g - 1)
                split_after(split_upper, act, f"z{g}_0")
                act.wait_ge(xt_ready, 5 * g + 5)
                act.wait_ge(xt_done, 5 * g + 4)
                act.copy(bst, bank[6][:, 0:2 * P].rearrange("p (t n) -> p t n", t=TT)).then_inc(xt_done, 1)
                gate(2)
                for dr in range(2):
                    act.wait_ge(h0_ready, 2 * g + dr + 1)
                    act.copy(h0[:, dr, :], bank[6 + dr][:, :]).then_inc(h0_done, 1)
                gate(3)
                split_after(split_upper, act, f"z{g}_1")
                head_exp(GH * g)

        def ssd_dve(dve):
            link = stepper(dve, dve_step)

            def mask_head(n):
                dve.wait_ge(seg_exp, n + 1)
                dve.tensor_tensor(Em[:, n % EMS], Em[:, n % EMS], cbm, ALU.mult).then_inc(seg_done, 1)

            def convolve(g, b):
                m = XB * g + b
                dve.wait_ge(gemm_freed, GROUP[f"xs{g}"] + b + 1)
                if m >= 3:
                    dve.wait_ge(conv_silu, m - 2)
                s = 2 if b < 5 else 1
                c, x = cacc[:, m % 3, 0:s], cin[:, m % 2, 0:s]
                link(dve.tensor_scalar(c, x[:, :, 0:L], pc("conv_w", m * CONV), pc("conv_b", m), ALU.mult, ALU.add))
                for k in range(1, CONV):
                    ins = dve.scalar_tensor_tensor(c, x[:, :, k:k + L], pc("conv_w", m * CONV + k), c, ALU.mult, ALU.add)
                    if k < CONV - 1:
                        link(ins)
                ins.then_inc(conv_done, 1)

            def gate_heads(g, blk):
                nb = GB * g + blk
                dve.wait_ge(y_ready, GH * g + 2 * blk + 2)
                dve.tensor_tensor(yT[:, nb, :], bank[4 + blk % 2][:, 0:L], zs[:, blk, :], ALU.mult).then_inc(y_gated, 1)

            def per_head(v):
                return v.rearrange("p (r d) -> p r d", r=GH)

            def spread(v):
                return v.unsqueeze(2).broadcast_to([P, GH, HD])

            def normalise(g):
                dve.wait_ge(y_std, g + 1)
                link(dve.reciprocal(rstd, rstd))
                for nb in range(GB * g, GB * g + GB):
                    dve.scalar_tensor_tensor(yT[:, nb, :], yT[:, nb, :], pc("ssd_norm", nb), rstd, ALU.mult, ALU.mult).then_inc(y_norm, 1)

            LAST_SPLITS = {0: "gates_1", 2: "gates_2", 4: "gates_3", 6: "gates_4"}

            dve.memset(cin, 0.0).then_inc(pad_zero, 1)
            dt_dve(dve)
            for g in range(SSD_G + 1):
                for i in range(GH):
                    if g:
                        if i == 0:
                            mask_head(GH * (g - 1))
                        if i >= 3 and i % 2 == 1:
                            gate_heads(g - 1, (i - 3) // 2)
                        if i + 2 < GH:
                            add_decays(dve, GH * (g - 1) + i + 2, 0, seg_added)
                        if i + 1 < GH:
                            mask_head(GH * (g - 1) + i + 1)
                    if g > 1 and i == (1 if g == SSD_G else XB):
                        normalise(g - 2)
                    if g == SSD_G and i in LAST_SPLITS:
                        if i == 0:
                            dve.wait_ge(lo_made, SPLIT.index("gates_1"))
                        split_lower(dve, LAST_SPLITS[i])
                    if g < SSD_G and i < XB:
                        convolve(g, i)
                    if g == 0 and i == 1:
                        sums_dve(dve)
                if g:
                    gate_heads(g - 1, GB - 1)
                if g < SSD_G:
                    for i in range(4):
                        dve.wait_ge(xt_ready, 5 * g + i + 1)
                        src = per_head(bank[6 + i % 2][:, :])
                        if i < 2:
                            if g and i == 0:
                                dve.wait_ge(y_ready, GH * g)
                            elif i == 0:
                                dve.wait_ge(sums_out, 16)
                            link(dve.tensor_tensor(per_head(yoff[:, i, :]), src,
                                                   spread(heads[:, SKIP0 + GH * g:SKIP0 + GH * g + GH]), ALU.mult))
                        for dr in range(2):
                            h = slice(32 * dr + GH * g, 32 * dr + GH * g + GH)
                            if i < 2:
                                ins = dve.tensor_tensor(per_head(xdt[:, dr, i, :]), src, spread(dtv[:, i, h]), ALU.mult)
                                if dr == 0:
                                    link(ins)
                            else:
                                ins = dve.tensor_tensor(per_head(xw[:, dr, i - 2, :]), src, spread(wctx[:, i - 2, h]), ALU.mult)
                                ins.then_inc(xw_done, 1)
                        if i >= 2:
                            dve.wait_ge(xw_done, 4 * g + 2 * (i - 1))
                            ins = dve.drain()
                        ins.then_inc(xt_done, 1)
                    dve.wait_ge(cb_ready, g + 1)
                    if g:
                        dve.wait_ge(seg_done, GH * g)
                    cb = bank[7]
                    le, ge = cm("le"), cm("ge")
                    link(dve.tensor_tensor(cbm[:, 0, :], cb[:, 0:P], le, ALU.mult))
                    link(dve.tensor_copy(cbm[:, 1, :], cb[:, P:L]))
                    link(dve.tensor_tensor(cbm[:, 2, :], cb[:, L + P:2 * L], le, ALU.mult))
                    link(dve.tensor_tensor(cbm[:, 3, :], cb[:, 0:P], ge, ALU.mult))
                    link(dve.tensor_copy(cbm[:, 4, :], cb[:, L:L + P]))
                    dve.tensor_tensor(cbm[:, 5, :], cb[:, L + P:2 * L], ge, ALU.mult).then_inc(cb_done, 1)
                if g < SSD_G:
                    for i in range(2):
                        add_decays(dve, GH * g + i, 0, seg_added)
                    for t in range(TT):
                        dve.wait_ge(yoff_ready, 2 * g + t + 1)
                        for dr in range(2):
                            w = spread(eacs[:, t, 32 * dr + GH * g:32 * dr + GH * g + GH])
                            link(dve.tensor_tensor(per_head(yo2), per_head(bank[4 + 2 * t + dr][:, :]), w, ALU.mult))
                            ins = dve.tensor_tensor(yoff[:, t, :], yoff[:, t, :], yo2, ALU.add)
                            if dr == 0:
                                link(ins)
                        ins.then_inc(yoff_done, 1)
                        dve.wait_ge(yoff_done, 2 * g + t + 1)
            normalise(SSD_G - 1)

        r4 = Region(AFTER_Y)
        r4.take(GATES_AT - AFTER_Y)
        assert r4.at == GATES_AT
        gT = r4.take(16, L)
        UT_AT = r4.at
        uT = r4.take(KT, L)
        ut = r4.take(2, L)
        tmp4 = r4.take(4, 512)
        gdiag4 = r4.take(KT, P)
        merged = sem("merged")
        o_rounded, o_made, y_rounded, y_made = sem("o_rounded"), sem("o_made"), sem("y_rounded"), sem("y_made")
        oT_hi, oT_lo = parts_in_work("oT_hi", [P, KT, L], r4.at), parts_in_work("oT_lo", [P, KT, L], AFTER_H)
        r4.take(KT * L)
        uT_hi, uT_lo = oT_hi, parts_in_work("uT_lo", [P, KT, L], UT_AT)
        yT_hi, yT_lo = parts_in_work("yT_hi", [P, 16, L], r4.at), parts_in_work("yT_lo", [P, 16, L], AFTER_O)
        r4.take(16 * L)

        def logits(pe, t):
            for k in range(KT):
                last = pe.matmul(bank[0][:, NE * t:NE * t + NE], hn[:, k, t * P:(t + 1) * P], router[:, k, :],
                                 start=k == 0, stop=k == KT - 1)
            return last

        def merge_pe(pe):
            feat_groups(pe, "gates", EARLY_GATES, hT, 0, L, GROUP["gates"] + EARLY_GATES, 16 - EARLY_GATES)
            grow_pe(pe, 0, gdiag4)
            pe.wait_ge(o_made, 1)
            feat_groups(pe, "na", 0, (oT_hi, oT_lo), 0, L, GROUP["na"], 8)
            pe.wait_ge(y_made, 2)
            y = yT_hi, yT_lo
            for u in range(4):
                for k in range(2):
                    w = split_chunk(pe, f"ssd_{u}{k}")
                    for b in range(2):
                        n = GROUP["ssd"] + 2 * u + b
                        if k == 0:
                            pe.wait_ge(gemm_freed, n - 3)
                        for kk in range(KT):
                            last = product3(pe, bank[n % 4][:, 0:L], [x[:, kk, b * P:(b + 1) * P] for x in w],
                                            [x[:, KT * k + kk, :] for x in y], k == 0 and kk == 0, k == 1 and kk == KT - 1)
                        if k == 1:
                            last.then_inc(gemm_ready, 1)
                    if k == 0:
                        last.then_inc(chunk_used, 1)
            pe.wait_ge(grow_in, 2)
            pe.wait_ge(merged, 8)
            rows_product3(pe, "out", (uT_hi, uT_lo))
            turn_tile(pe, MERGE, 0)
            pe.wait_ge(first_turned, 1)
            logits(pe, 0)
            turn_tile(pe, MERGE, 1)

        MERGE_UNITS = [n for n in SPLIT if n.startswith(("na_", "ssd_", "out"))][3:]

        def merge_pool(pool):
            for u in range(EARLY_GATES // 2 - 1, 8):
                split_after(split_lower, pool, f"gates_{u}")
            for name in MERGE_UNITS:
                split_lower(pool, name)

        def merge_act(act):
            act.copy(oT_hi[:, :, :], oT).then_inc(o_rounded, 1)
            split_after(split_upper, act, f"gates_{EARLY_GATES // 2 - 1}")
            act.activation(gT[:, 0:EARLY_GATES, :], gT[:, 0:EARLY_GATES, :], ACT.Sigmoid)
            for i in range(EARLY_GATES, 16):
                n = GROUP["gates"] + i
                act.wait_ge(gemm_ready, n + 1)
                act.activation(gT[:, i, :], bank[n % 4][:, 0:L], ACT.Sigmoid).then_inc(gemm_freed, 1)
                if i % 2:
                    split_after(split_upper, act, f"gates_{i // 2}")
            act.dma_start(xres, d["x"].rearrange("(t p) n -> p t n", p=P)).then_inc(x_in, 16)
            for i in range(2):
                h = slice(8 * i, 8 * i + 8)
                act.copy(yT_hi[:, h, :], yT[:, h, :]).then_inc(y_rounded, 1)
            for name in MERGE_UNITS:
                split_upper(act, name)
            close_act(act, MERGE, rows_ready, [ROWS["out"] + j + 1 for j in range(4)], tmp4)

        def merge_dve(dve):
            link = stepper(dve, dve_step)
            grow_dve_in(dve, 0, gdiag4)
            dve.wait_ge(o_rounded, 1)
            dve.tensor_tensor(oT_lo[:, :, :], oT, oT_hi[:, :, :], ALU.subtract).then_inc(o_made, 1)
            for i in range(2):
                h = slice(8 * i, 8 * i + 8)
                dve.wait_ge(y_rounded, i + 1)
                dve.tensor_tensor(yT_lo[:, h, :], yT[:, h, :], yT_hi[:, h, :], ALU.subtract).then_inc(y_made, 1)
            grow_out(dve.tensor_copy, dve, 0)
            dve.wait_ge(gemm_freed, GROUP["na"])
            for i in range(8):
                n = GROUP["na"] + i
                dve.wait_ge(gemm_ready, n + 1)
                dve.tensor_tensor(uT[:, i, :], bank[n % 4][:, 0:L], gT[:, i, :], ALU.mult).then_inc(gemm_freed, 1)
            for i in range(8):
                n = GROUP["ssd"] + i
                dve.wait_ge(gemm_ready, n + 1)
                dve.tensor_tensor(ut[:, i % 2, :], bank[n % 4][:, 0:L], gT[:, 8 + i, :], ALU.mult).then_inc(gemm_freed, 1)
                dve.wait_ge(gemm_freed, n + 1)
                link(dve.tensor_tensor(uT[:, i, :], uT[:, i, :], ut[:, i % 2, :], ALU.add))
                link(dve.tensor_copy(uT_hi[:, i, :], uT[:, i, :]))
                dve.tensor_tensor(uT_lo[:, i, :], uT[:, i, :], uT_hi[:, i, :], ALU.subtract).then_inc(merged, 1)
            dve.wait_ge(merged, 8)
            dve.wait_ge(x_in, 48)
            close_dve(dve, MERGE, tmp4, mul2, mod[:, 24:32])

        r5 = Region(AFTER_N + KT * L)
        tmp5 = r5.take(4, 512)
        aff = r5.take(TT, NE)
        affT = r5.take(L)
        left = r5.take(L)
        top = r5.take(4, 8)
        place = r5.take(3, L)
        code = r5.take(TT, NE)
        pick5 = parts_in_work("pick5", [P, TT, NE, CAP], r5.at)
        r5.take(TT, NE, CAP)
        pick_g = r5.take(NE, 4, CAP)
        xgT = r5.take(KT, NE * CAP)
        PgT = r5.take(NE, L)
        gdiag5 = r5.take(KT, P)
        xg = r5.take(2, KT, CAP)
        pg = r5.take(2, 2, L)
        xn_hi, xn_lo = parts_in_work("xn_hi", [P, TT, D], r5.at), parts_in_work("xn_lo", [P, TT, D], KT * L)
        sg = r5.take(2, 512)
        hid = r5.take(2, 512)
        hidT = r5.take(2, 512)
        yo = r5.take(2, 512)
        (logits_ready, aff_max, aff_exp, aff_done, affT_ready, place_ready, code_ready, pick_ready, gather_ready, gather_read,
         pgt_ready, pgt_done, pgate_done, zero_pg, xn_rounded, xn_split) = (sem(n) for n in (
             "logits_ready", "aff_max", "aff_exp", "aff_done", "affT_ready", "place_ready", "code_ready", "pick_ready",
             "gather_ready", "gather_read", "pgt_ready", "pgt_done", "pgate_done", "zero_pg", "xn_rounded", "xn_split"))
        (expert_used, gate_ready, up_ready, down_ready, xg_staged, pg_staged, gate_acted, hid_done, hid_turned, hid_copied,
         yo_done, scattered) = (sem(n) for n in (
             "expert_used", "gate_ready", "up_ready", "down_ready", "xg_staged", "pg_staged", "gate_acted", "hid_done",
             "hid_turned", "hid_copied", "yo_done", "scattered"))

        def route_act(act):
            act.wait_ge(aff_max, 2)
            for t in range(TT):
                act.activation(aff[:, t, :], bank[0][:, NE * t:NE * t + NE], ACT.Exp, bias=small[:, 26 + t:27 + t],
                               accum_out=small[:, 28 + t:29 + t]).then_inc(aff_exp, 1)
            act.copy(xn_hi[:, :, :], xnm).then_inc(xn_rounded, 1)
            grow_out(act.copy, act, 1)
            for g in range(8):
                act.wait_ge(pgt_ready, g + 1)
                act.copy(PgT.rearrange("p e l -> p (e l)")[:, 512 * g:512 * g + 512], bank[4 + g % 2][:, :]).then_inc(pgt_done, 1)

        def route_pe(pe):
            logits(pe, 1).then_inc(logits_ready, 1)
            grow_pe(pe, 1, gdiag5)
            pe.wait_ge(aff_done, 2)
            for t in range(TT):
                last = pe.transpose(bank[3][0:NE, t * P:(t + 1) * P], aff[:, t, :], ident)
            last.then_inc(affT_ready, 1)
            pe.wait_ge(place_ready, 1)
            for t in range(TT):
                last = pe.transpose(bank[2][:, NE * t:NE * t + NE], place[0:NE, 2, t * P:(t + 1) * P], ident[0:NE, 0:NE])
            last.then_inc(code_ready, 1)
            pe.wait_ge(pick_ready, 2)
            pe.wait_ge(xn_split, 1)
            pe.wait_ge(grow_in, 4)
            for k in range(KT):
                if k >= 4:
                    pe.wait_ge(gather_read, k - 3)
                for t in range(TT):
                    pe.matmul(bank[k % 4][:, :], xn_hi[:, t, k * P:(k + 1) * P], pick5[:, t], start=t == 0, stop=False)
                    last = pe.matmul(bank[k % 4][:, :], xn_lo[:, t, k * P:(k + 1) * P], pick5[:, t], start=False, stop=t == TT - 1)
                last.then_inc(gather_ready, 1)
                if k >= 2:
                    pe.wait_ge(pgt_done, k - 1)
                for i in range(4):
                    e, t = 2 * k + i // 2, i % 2
                    pe.wait_ge(pgate_done, 2 * e + t + 1)
                    last = pe.transpose(bank[4 + k % 2][:, i * P:(i + 1) * P], pick_g[:, (2 * e + t) % NE], ident)
                last.then_inc(pgt_ready, 1)

        def route_pool(pool):
            pool.memset(pg, 0.0)
            pool.wait_ge(xn_rounded, 1)
            pool.tensor_tensor(xn_lo[:, :, :], xnm, xn_hi[:, :, :], ALU.subtract).then_inc(xn_split, 1)
            pool.wait_ge(pick_ready, 2)
            for i in range(2 * NE):
                e, t = i // 2, i % 2
                if i >= NE:
                    pool.wait_ge(pgt_ready, (i - NE) // 4 + 1)
                pool.tensor_tensor(pick_g[:, i % NE], pick5[:, t, e, :].unsqueeze(1).broadcast_to([P, 4, CAP]),
                                   aff[:, t, e:e + 1].unsqueeze(2).broadcast_to([P, 4, CAP]), ALU.mult).then_inc(pgate_done, 1)

        def route_dve(dve):
            link = stepper(dve, dve_step)
            grow_dve_in(dve, 1, gdiag5)
            dve.wait_ge(logits_ready, 1)
            for t in range(TT):
                link(dve.tensor_reduce(small[:, 24 + t:25 + t], bank[0][:, NE * t:NE * t + NE], AX.X, ALU.max))
                dve.tensor_scalar(small[:, 26 + t:27 + t], small[:, 24 + t:25 + t], -1.0, None, ALU.mult).then_inc(aff_max, 1)
            for t in range(TT):
                dve.wait_ge(aff_exp, t + 1)
                link(dve.reciprocal(small[:, 30 + t:31 + t], small[:, 28 + t:29 + t]))
                dve.tensor_scalar(aff[:, t, :], aff[:, t, :], small[:, 30 + t:31 + t], None, ALU.mult).then_inc(aff_done, 1)
            dve.wait_ge(affT_ready, 1)
            link(dve.tensor_copy(affT[0:NE, :], bank[3][0:NE, 0:L]))
            src = affT
            for r in range(CAP // 8):
                link(dve.max(top[0:NE, r, :], src[0:NE, :]))
                link(dve.match_replace(left[0:NE, :], top[0:NE, r, :], src[0:NE, :], -1.0))
                src = left
            link(dve.tensor_scalar(place[0:NE, 0, :], left[0:NE, :], -1.0, None, ALU.is_equal))
            link(dve.memset(place[0:NE, 1, :], 1.0))
            link(dve.tensor_tensor_scan(place[0:NE, 2, :], place[0:NE, 1, :], place[0:NE, 0, :], 0.0, ALU.mult, ALU.add))
            dve.tensor_tensor(place[0:NE, 2, :], place[0:NE, 2, :], place[0:NE, 0, :], ALU.mult).then_inc(place_ready, 1)
            dve.wait_ge(code_ready, 1)
            link(dve.tensor_copy(code, bank[2][:, 0:2 * NE].rearrange("p (t e) -> p t e", t=TT)))
            for t in range(TT):
                dve.tensor_tensor(pick5[:, t], code[:, t, :].unsqueeze(2).broadcast_to([P, NE, CAP]),
                                  numbers.unsqueeze(1).broadcast_to([P, NE, CAP]), ALU.is_equal).then_inc(pick_ready, 1)
            for k in range(KT):
                dve.wait_ge(gather_ready, k + 1)
                dve.tensor_scalar(xgT[:, k, :], bank[k % 4][:, :], mul2[:, k:k + 1], mod[:, 24 + k:25 + k],
                                  ALU.mult, ALU.add).then_inc(gather_read, 1)

        FE = FIRST_EXPERT

        def expert_wait(pe, e, k):
            c = FE + k
            pe.wait_ge(slot_full[c % SLOTS], e * (16 * EXPERT_USES) + 16 * (c // SLOTS + 1))

        def expert_slot(k, kt):
            return ring[:, (FE + k) % SLOTS, :].rearrange("p (t n) -> p t n", t=kt)

        def experts_pe(pe):
            pe.wait_ge(hid_done, 1)
            for j in range(4):
                last = pe.matmul(bank[4 + j][:, :], yo_zero[:, 0:P], yo_zero, start=True, stop=False, skip_group_check=True)
            last.then_inc(zero_pg, 1)
            with pe.Fori(0, NE // 2) as i:
                for e2 in range(2):
                    e = 2 * i + e2
                    pe.wait_ge(xg_staged, e + 1)
                    for which, ready in ((0, gate_ready), (1, up_ready)):
                        if which == 0:
                            pe.wait_ge(gate_acted, e + 1)
                        else:
                            pe.wait_ge(hid_done, e + 1)
                        for c in range(4):
                            k = 4 * which + c
                            expert_wait(pe, e, k)
                            w = expert_slot(k, 2)
                            for k2 in range(2):
                                for n in range(4):
                                    last = pe.matmul(bank[which][32 * n:32 * n + 32, :], xg[:, e2, 2 * c + k2, :],
                                                     w[:, k2, 512 * n:512 * n + 512], start=c == 0 and k2 == 0,
                                                     stop=c == 3 and k2 == 1, tile_position=(0, 32 * n))
                            last.then_inc(expert_used if c < 3 else ready, 1)
                    pe.wait_ge(hid_done, e + 2)
                    for b in range(4):
                        last = pe.transpose(bank[2][:, b * P:(b + 1) * P], hid[:, e2, b * P:(b + 1) * P], ident)
                    last.then_inc(hid_turned, 1)
                    pe.wait_ge(hid_copied, e + 1)
                    pe.wait_ge(yo_done, e + 1)
                    for n in range(4):
                        k = 8 + n
                        expert_wait(pe, e, k)
                        w = expert_slot(k, 4)
                        for b in range(4):
                            for half in range(2):
                                q = 2 * half + b % 2
                                last = pe.matmul(bank[3][32 * q:32 * q + 32, :], hidT[:, e2, b * P + 32 * n:b * P + 32 * n + 32],
                                                 w[:, b, 512 * half:512 * half + 512], start=n == 0 and b < 2,
                                                 stop=n == 3 and b >= 2, tile_position=(0, 32 * q))
                        last.then_inc(expert_used if n < 3 else down_ready, 1)
                    pe.wait_ge(yo_done, e + 2)
                    pe.wait_ge(pg_staged, 2 * e + 2)
                    for t in range(TT):
                        for half in range(2):
                            last = pe.matmul(bank[4 + 2 * t + half][:, :], pg[:, e2, half, t * P:(t + 1) * P], yo[:, e2, :],
                                             start=False, stop=False, skip_group_check=True)
                    last.then_inc(scattered, 1)

        yo_zero = tmp5[:, 0, :]

        def experts_act(act):
            act.sem_inc(gate_acted, 1)
            act.sem_inc(yo_done, 1)
            with act.Fori(0, NE // 2) as i:
                for e2 in range(2):
                    e = 2 * i + e2
                    act.wait_ge(gate_ready, e + 1)
                    act.activation(sg[:, e2, :], bank[0][:, :], ACT.Silu).then_inc(gate_acted, 1)
                    act.wait_ge(hid_turned, e + 1)
                    act.copy(hidT[:, e2, :], bank[2][:, :]).then_inc(hid_copied, 1)
                    act.wait_ge(down_ready, e + 1)
                    act.copy(yo[:, e2, :], bank[3][:, :]).then_inc(yo_done, 1)

        def experts_dve(dve):
            link = stepper(dve, dve_step)
            dve.memset(yo_zero, 0.0).then_inc(hid_done, 1)
            dve.wait_ge(hid_done, 1)
            dve.sem_inc(scattered, 2)
            with dve.Fori(0, NE // 2) as i:
                for e2 in range(2):
                    e = 2 * i + e2
                    dve.wait_ge(scattered, e + 1)
                    dve.tensor_scalar(xg[:, e2], xgT[:, :, bass.ds(e * CAP, CAP)], 1.0, None, ALU.mult).then_inc(xg_staged, 1)
                    for half in range(2):
                        p0 = 64 * half
                        dve.tensor_scalar(pg[p0:p0 + 64, e2, half, :], PgT[p0:p0 + 64, bass.ds(e, 1), :].rearrange("p e l -> p (e l)"),
                                          1.0, None, ALU.mult).then_inc(pg_staged, 1)
                    dve.wait_ge(gate_acted, e + 2)
                    dve.wait_ge(up_ready, e + 1)
                    dve.tensor_tensor(hid[:, e2, :], bank[1][:, :], sg[:, e2, :], ALU.mult).then_inc(hid_done, 1)

        tab_in, pT_in = sem("tab_in"), sem("pT_in")
        hid_squared, hid_rounded, hid_made = sem("hid_squared"), sem("hid_rounded"), sem("hid_made")
        HID = AFTER_N + KT * L
        hid_hi = parts_in_work("hid_hi", [P, DFF // P, L], HID)
        hid_lo = parts_in_work("hid_lo", [P, DFF // P, L], HID + DFF // P * L)
        rm = Region(HID + 2 * DFF // P * L)
        hid_r, hid_sq = rm.take(2, L), rm.take(2, L)
        tmpm = xnm.rearrange("p t (h n) -> p (t h) n", h=2)
        rm = Region(AFTER_N)
        gs = rm.take(TT, D)
        gterm = rm.take(2, 512)
        pT = rm.take(2, L)

        def mlp_pe(pe, l):
            rows = hn_hi, hn_lo
            for i in range(UPS):
                w = split_chunk(pe, f"up{l}{i}")
                for b in range(2):
                    n = GROUP[f"up{l}"] + 2 * i + b
                    pe.wait_ge(gemm_freed, n - 3)
                    for k in range(KT):
                        last = product3(pe, bank[n % 4][:, 0:L], [x[:, k, b * P:(b + 1) * P] for x in w], [x[:, k, :] for x in rows],
                                        k == 0, k == KT - 1)
                    last.then_inc(gemm_ready, 1)
            hid = hid_hi, hid_lo

            def part(i, h, t):
                w = split_chunk(pe, f"dn{l}{i}{h}")
                for k in range(4):
                    last = product3(pe, bank[4 + 2 * t + h][:, :], [x[:, 4 * i + k, t * P:(t + 1) * P] for x in hid], [x[:, k, :] for x in w],
                                    i == 0 and k == 0, i == DOWNS - 1 and k == 3)
                return last
            for i in range(DOWNS - 2):
                pe.wait_ge(hid_made, 32 * l + 4 * i + 4)
                for h in range(2):
                    for t in range(TT):
                        last = part(i, h, t)
                    last.then_inc(chunk_used, 1)
            pe.wait_ge(hid_made, 32 * l + 32)
            for t in range(TT):
                for h in range(2):
                    if t == 1 and h == 1:
                        turn_tile(pe, MLP + 3 * l, 0)
                    last = part(DOWNS - 2, h, t)
                    if t == 1:
                        last.then_inc(chunk_used, 1)
                    part(DOWNS - 1, h, t).then_inc(rows_ready, 1)
            turn_tile(pe, MLP + 3 * l, 1)

        def units_of(l):
            return [f"up{l}{i}" for i in range(UPS)] + [f"dn{l}{i}{h}" for i, h in DOWN_ORDER]

        SPLIT_EARLY = 2

        def mlp_act(act, l):
            units = units_of(l)
            split_upper(act, units[SPLIT_EARLY])
            for i in range(UPS):
                split_upper(act, units[i + SPLIT_EARLY + 1])
                for b in range(2):
                    m = 2 * i + b
                    n = GROUP[f"up{l}"] + m
                    act.wait_ge(gemm_ready, n + 1)
                    if m >= 2:
                        act.wait_ge(hid_squared, 32 * l + m - 1)
                    act.activation(hid_r[:, m % 2, :], bank[n % 4][:, 0:L], ACT.Relu).then_inc(gemm_freed, 1)
                    if m >= 1:
                        act.wait_ge(hid_squared, 32 * l + m)
                        act.copy(hid_hi[:, m - 1, :], hid_sq[:, (m - 1) % 2, :]).then_inc(hid_rounded, 1)
            act.wait_ge(hid_squared, 32 * l + 32)
            act.copy(hid_hi[:, 31, :], hid_sq[:, 1, :]).then_inc(hid_rounded, 1)
            for u in units[UPS + SPLIT_EARLY + 1:]:
                split_upper(act, u)
            close_act(act, MLP + 3 * l, rows_ready, [ROWS[f"dn{l}"] + j + 1 for j in range(4)], tmpm)

        def mlp_dve(dve, l):
            for m in range(33):
                if m < 32:
                    dve.wait_ge(gemm_freed, GROUP[f"up{l}"] + m + 1)
                    if m >= 2:
                        dve.wait_ge(hid_made, 32 * l + m - 1)
                    dve.tensor_tensor(hid_sq[:, m % 2, :], hid_r[:, m % 2, :], hid_r[:, m % 2, :], ALU.mult).then_inc(hid_squared, 1)
                if m >= 1:
                    dve.wait_ge(hid_rounded, 32 * l + m)
                    dve.wait_ge(hid_squared, 32 * l + m)
                    dve.tensor_tensor(hid_lo[:, m - 1, :], hid_sq[:, (m - 1) % 2, :], hid_hi[:, m - 1, :], ALU.subtract).then_inc(hid_made, 1)
            last = units_of(l)[-2:]
            dve.wait_ge(lo_made, SPLIT.index(last[0]))
            for u in last:
                split_lower(dve, u)
            dve.wait_ge(grow_loaded, 16 * (2 * l + 2))
            close_dve(dve, MLP + 3 * l, tmpm)

        def mlp_pool(pool, l):
            for u in units_of(l)[SPLIT_EARLY:-2]:
                split_lower(pool, u)

        def split_early_act(act, l):
            for u in units_of(l)[:SPLIT_EARLY]:
                split_upper(act, u)

        def split_early_pool(pool, l):
            for u in units_of(l)[:SPLIT_EARLY]:
                split_lower(pool, u)

        def load_grow(pool, i):
            pool.dma_start(grow[:, :], d["g_post"][i:i + 1, :].partition_broadcast(P).rearrange("q o n -> q (o n)")).then_inc(grow_loaded, 16)

        def ple_pe(pe, l):
            w = slot(f"pp{l}")
            n = GROUP[f"ple{l}"]
            for t in range(TT):
                for h in range(2):
                    wait_chunk(pe, f"pg{l}{h}")
                    wg = slot(f"pg{l}{h}")
                    pe.wait_ge(gemm_freed, n - 3)
                    for k in range(KT):
                        last = pe.matmul(bank[n % 4][:, :], hn[:, k, t * P:(t + 1) * P], wg[:, k, :], start=k == 0, stop=k == KT - 1)
                    last.then_inc(gemm_ready, 1)
                    n += 1
                pe.wait_ge(pT_in, 16 * (l + 1))
                for h in range(2):
                    wait_chunk(pe, f"pp{l}")
                    pe.wait_ge(gemm_freed, n - 3)
                    for k in range(2):
                        last = pe.matmul(bank[n % 4][:, :], pT[:, k, t * P:(t + 1) * P], w[:, k, 512 * h:512 * h + 512], start=k == 0, stop=k == 1)
                    last.then_inc(gemm_ready, 1)
                    n += 1
            if l == 0:
                for t in range(TT):
                    if t == 0:
                        pe.wait_ge(gemm_freed, n - 2)
                    else:
                        pe.wait_ge(gemm_freed, n)
                    turn_tile(pe, PLE, t)

        def ple_act(act, l):
            n = GROUP[f"ple{l}"]
            for t in range(TT):
                for h in range(2):
                    act.wait_ge(gemm_ready, n + 4 * t + h + 1)
                    act.wait_ge(gemm_freed, n + 4 * t)
                    act.activation(gs[:, t, 512 * h:512 * h + 512], bank[(n + 4 * t + h) % 4][:, :], ACT.Sigmoid).then_inc(gemm_freed, 1)
            if l == 0:
                for t in range(TT):
                    norm_act(act, PLE, t)

        def ple_dve(dve, l):
            for t in range(TT):
                for h in range(2):
                    n = GROUP[f"ple{l}"] + 4 * t + 2 + h
                    dve.wait_ge(gemm_ready, n + 1)
                    dve.wait_ge(gemm_freed, n)
                    dve.tensor_tensor(gterm[:, h, :], bank[n % 4][:, :], gs[:, t, 512 * h:512 * h + 512], ALU.mult).then_inc(gemm_freed, 1)
                    dve.wait_ge(gemm_freed, n + 1)
                    x = x_halves[t][h]
                    dve.tensor_tensor(x, x, gterm[:, h, :], ALU.add).then_inc(x_done, 1)
                dve.wait_ge(x_done, 4 * (PLE + 3 * l) + 2 * t + 2)
            if l == 0:
                for t in range(TT):
                    norm_dve(dve, PLE, t)
                    turned_tile(dve, PLE, t, pc("mix_pre2", 8, 8))

        def ple_pool(pool, l):
            pool.dma_start(pT, d["pT"][l].rearrange("(k p) n -> p k n", p=P)).then_inc(pT_in, 16)

        r6 = Region(AFTER_N + KT * L, ROPE0)
        qz_ab = {t: r6.take(4, 2, L) for t in "ab"}
        k_ab = {t: r6.take(4, L) for t in "ab"}
        v_ab = {t: r6.take(TT, 512) for t in "ab"}
        s_ab, pr_ab = r6.take(AHEAD, L), r6.take(AHEAD, L)
        PT_a, PT_b = r6.take(2, TT, P), r6.take(2, TT, L)
        first_map = r6.take(L)
        oA, oA2 = r6.take(8, P), r6.take(8, P)
        obT = r6.take(KT, L)
        sub = r6.take(4, 8)
        lam_sum, lam_exp, av_ready, av_stored, sub_sum, sub_std, sub_done, sub_ready, sub_out = (sem(n) for n in (
            "lam_sum", "lam_exp", "av_ready", "av_stored", "sub_sum", "sub_std", "sub_done", "sub_ready", "sub_out"))
        causal_w = lambda u: P * (u % 2 + 1)

        def mask_of(m, qt):
            return masks[:, m, 0:P] if qt == 0 else masks[:, m, P:3 * P]

        AA = Attention(8, 2, causal_w, lambda u: mask_of(0, u % 2), 1.0, s_ab, pr_ab, lambda u: PT_a[:, u % 2, 0:u % 2 + 1, :], (3, 6))
        AB = Attention(16, 1, causal_w, lambda u: mask_of(1, u % 2), 1.0, s_ab, pr_ab,
                       lambda u: PT_b[:, (u // 2) % 2, 0:u % 2 + 1, (u % 2) * P:(u % 2 + 1) * P], (3, 6))
        AB.hooks = head_values(AB, v_ab["b"], PT_b, 8, True, counted["values"], lambda blk: obT[:, 4 + blk, :])

        def ab_proj_pe(pe):
            for t in "ab":
                for m in "qk":
                    roped_groups(pe, t + m, (hn_hi, hn_lo), L, "swap32", lambda: None)
                token_groups(pe, t + "v", (hn_hi, hn_lo), TT, GROUP[t + "v"])

        def ab_split(split, eng, name):
            if CHUNK[name] + 3 <= CHUNK["bv_1"]:
                split_after(split, eng, name)

        def ab_proj_pool(pool):
            split_lower(pool, "ak_0")
            for t in "ab":
                for m in "qkv":
                    for u in range(2):
                        ab_split(split_lower, pool, f"{t}{m}_{u}")

        def ab_proj_act(act):
            split_upper(act, "ak_0")
            for t in "ab":
                for m in "qk":
                    for b in range(4):
                        rope_act(act, GROUP[t + m] + b)
                        if b % 2:
                            ab_split(split_upper, act, f"{t}{m}_{b // 2}")
                for i in range(TT):
                    n = GROUP[t + "v"] + i
                    act.wait_ge(gemm_ready, n + 1)
                    act.copy(v_ab[t][:, i, :], bank[n % 4][:, :]).then_inc(gemm_freed, 1)
                for u in range(2):
                    ab_split(split_upper, act, f"{t}v_{u}")
            act.wait_ge(lam_sum, 2)
            act.activation(lam[:, 2:4], lam[:, 0:2], ACT.Exp).then_inc(lam_exp, 1)

        def ab_proj_dve(dve):
            link = stepper(dve, dve_step)
            link(dve.memset(qz_ab["a"], 0.0))
            link(dve.memset(qz_ab["b"], 0.0))
            dve.wait_ge(tab_in, 16)
            for t in "ab":
                for b in range(4):
                    q = qz_ab[t]
                    rope_dve(dve, tb("ab_qc"), tb("ab_qs"), [(q[0:64, b, 0, :], 0, 64), (q[64:128, b, 1, :], 64, 128)])
                for b in range(4):
                    rope_dve(dve, tb("ab_kc"), tb("ab_ks"), [(k_ab[t][:, b, :], 0, 128)])
            hv = heads[:, 128:SKIP0].rearrange("p (i d) -> p i d", i=4)
            for i in range(2):
                dve.tensor_tensor_reduce(out=oA[:, i, 0:HD], in0=hv[:, 2 * i, :], in1=hv[:, 2 * i + 1, :], scale=1.0, scalar=0.0,
                                         op0=ALU.mult, op1=ALU.add, accum_out=lam[:, i:i + 1]).then_inc(lam_sum, 1)
            dve.wait_ge(lam_exp, 1)
            link(dve.tensor_tensor(lam[:, 4:5], lam[:, 2:3], lam[:, 3:4], ALU.subtract))
            link(dve.tensor_scalar(lam[:, 5:6], lam[:, 4:5], -1.0, -LAM_INIT, ALU.mult, ALU.add))

        def ab_att_pe(pe):
            def scores_a(pe, i, b):
                u, m = i // 2, i % 2
                h, qt = u // 2, u % 2
                return pe.matmul(b[:, 0:causal_w(u)], qz_ab["a"][:, h, m, qt * P:(qt + 1) * P], k_ab["a"][:, h, 0:causal_w(u)],
                                 start=True, stop=True)

            def value_a(pe, u):
                h, qt = u // 2, u % 2
                pe.wait_ge(att_copied, AA.first + u + 1)
                if u >= 2:
                    pe.wait_ge(av_stored, u - 1)
                for k in range(qt + 1):
                    last = pe.matmul(bank[4 + u % 2][:, 0:P], PT_a[:, u % 2, k, :], v_ab["a"][:, k, h * P:(h + 1) * P],
                                     start=k == 0, stop=k == qt)
                last.then_inc(av_ready, 1)
            att_pe(pe, AA, scores_a, value_a)

            def turn_a(pe, r):
                pe.wait_ge(sub_done, 1)
                if r:
                    pe.wait_ge(sub_out, 2)
                for i in range(4):
                    last = pe.transpose(bank[7][:, i * P:(i + 1) * P], oA[:, 4 * r + i, :], ident)
                last.then_inc(sub_ready, 1)
            pe.wait_ge(av_stored, 8)

            def scores_b(pe, u, b):
                h, qt = u // 2, u % 2
                return pe.matmul(b[:, 0:causal_w(u)], qz_ab["b"][:, h // 2, h % 2, qt * P:(qt + 1) * P], k_ab["b"][:, h // 2, 0:causal_w(u)],
                                 start=True, stop=True)
            att_pe(pe, AB, scores_b, AB.hooks[0], {6: lambda pe: turn_a(pe, 0), 9: lambda pe: turn_a(pe, 1)})
            pe.wait_ge(sub_out, 4)
            pe.wait_ge(att_stored, (AB.values_first + 8) // 2)
            rows_product(pe, "o0", obT, lambda pe: turn_tile(pe, ATTENTION, 0))
            turn_tile(pe, ATTENTION, 1)

        AB.values_first = counted["values"] - 8

        def ab_att_act(act):
            def free_a(act, u):
                if u >= 2:
                    act.wait_ge(av_ready, u - 1)
            att_act(act, AA, free_a)
            act.wait_ge(sub_sum, 1)
            act.activation(sub[:, 1, :], sub[:, 0, :], ACT.Sqrt, bias=epsc[:, :], scale=1.0 / P).then_inc(sub_std, 1)
            att_act(act, AB, AB.hooks[2])
            split_early_act(act, 0)
            close_act(act, ATTENTION, rows_ready, [ROWS["o0"] + j + 1 for j in range(4)], tmp_o)

        def ab_att_dve(dve):
            link = stepper(dve, dve_step)

            def after_a(dve, u):
                dve.wait_ge(av_ready, u + 1)
                dve.tensor_copy(oA[:, u, :], bank[4 + u % 2][:, 0:P]).then_inc(av_stored, 1)
            att_dve(dve, AA, after_a, lam_of=(lam[:, 5:6], first_map))
            dve.wait_ge(av_stored, 8)
            link(dve.tensor_tensor(oA2, oA, oA, ALU.mult))
            dve.tensor_reduce(sub[:, 0, :], oA2, AX.X, ALU.add).then_inc(sub_sum, 1)

            def scale_a(dve):
                dve.wait_ge(sub_std, 1)
                link(dve.reciprocal(sub[:, 2, :], sub[:, 1, :]))
                link(dve.tensor_scalar(sub[:, 3, :], sub[:, 2, :], 1.0 - LAM_INIT, None, ALU.mult))
                dve.tensor_tensor(oA, oA, sub[:, 3, :].unsqueeze(2).broadcast_to([P, 8, P]), ALU.mult).then_inc(sub_done, 1)

            def take_a(dve, r):
                dve.wait_ge(sub_ready, r + 1)
                for i in range(2):
                    dve.tensor_scalar(obT[:, 2 * r + i, :], bank[7][:, i * L:i * L + L], pc("sub", 0), None, ALU.mult).then_inc(sub_out, 1)
            att_dve(dve, AB, AB.hooks[1], between={3: scale_a, 8: lambda dve: take_a(dve, 0), 11: lambda dve: take_a(dve, 1)})
            dve.wait_ge(grow_loaded, 16)
            close_dve(dve, ATTENTION, tmp_o, pc("mlp_pre2", 0, 8), parts=True)

        ro = Region(r6.at)
        tmp_o = ro.take(4, 512)

        r9 = Region(AFTER_N)
        CW = CQ + CKV + CROPE + 64 + IDX_HEADS
        cct = r9.take(TT, CW)
        cqT = r9.take(3, L)
        ckvT = r9.take(2, L)
        krep = r9.take(TT, P)
        kirep = r9.take(TT, P)
        rot = r9.take(2, TT, 64)
        kiT = r9.take(L)
        wi = r9.take(TT, IDX_HEADS)
        qi = r9.take(IDX_HEADS, L)
        q_c = r9.take(C_HEADS, L)
        k_c = r9.take(C_HEADS, L)
        v_c = r9.take(TT, D)
        acc = r9.take(TT, L)
        bsel = r9.take(TT, L)
        top9 = r9.take(8)
        relu = r9.take(2, L)
        s_c, pr_c, PT_c = r9.take(AHEAD, L), r9.take(AHEAD, L), r9.take(2, TT, L)
        oTc = r9.take(KT, L)
        stc = r9.take(12)
        tmp_c = q_c.rearrange("p h l -> p (h l)")[:, 0:2 * D].rearrange("p (j n) -> p j n", j=4)
        q_rotated, sel_done = sem("q_rotated"), sem("sel_done")
        (c_std, c_norm, c_rot, ct_ready, ct_out, ix_ready, ix_relu, ix_added) = (sem(n) for n in (
             "c_std", "c_norm", "c_rot", "ct_ready", "ct_out", "ix_ready", "ix_relu", "ix_added"))
        AC = Attention(2 * C_HEADS, 1, causal_w, lambda u: bsel[:, u % 2, 0:causal_w(u)], C_SCALE, s_c, pr_c,
                       lambda u: PT_c[:, (u // 2) % 2, 0:u % 2 + 1, (u % 2) * P:(u % 2 + 1) * P], (3, 6))
        AC.values_first = counted["values"]
        AC.hooks = head_values(AC, v_c, PT_c, C_HEADS, True, counted["values"], lambda blk: oTc[:, blk, :])
        N_TURNED = 7

        def c_pe(pe):
            token_groups_whole(pe, "cin1", hn, range(TT), 232, GROUP["cin"])
            token_groups_whole(pe, "cin0", hn, [0], 512, GROUP["cin"] + 2)
            srcs = [krep, kirep] + [cct[:, :, i * P:(i + 1) * P] for i in range(5)]
            for i, s in enumerate(srcs):
                if i == 0:
                    pe.wait_ge(c_rot, 2)
                if i == 2:
                    token_groups_whole(pe, "cin0", hn, [1], 512, GROUP["cin"] + 2)
                    pe.wait_ge(c_norm, 4)
                if i >= 2:
                    pe.wait_ge(ct_out, i - 1)
                for t in range(TT):
                    last = pe.transpose(bank[6 + i % 2][:, t * P:(t + 1) * P], s[:, t, :], ident)
                last.then_inc(ct_ready, 1)
            pe.wait_ge(ct_out, 5)
            feat_groups_whole(pe, "qi", 0, cqT, 0, L, GROUP["qi"], IDX_HEADS)
            pe.wait_ge(ct_out, N_TURNED)
            feat_groups_whole(pe, "uk", 0, ckvT, 0, L, GROUP["uk"], C_HEADS // 2)
            for n in range(2 * IDX_HEADS):
                qt, h = n // IDX_HEADS, n % IDX_HEADS
                if n >= 2:
                    pe.wait_ge(ix_relu, n - 1)
                pe.matmul(bank[4 + n % 2][:, 0:causal_w(qt)], qi[:, h, qt * P:(qt + 1) * P], kiT[:, 0:causal_w(qt)],
                          start=True, stop=True).then_inc(ix_ready, 1)
            wait_chunk(pe, "uv")
            w = slot("uv")
            for i in range(4):
                h, t = i // 2, i % 2
                n = GROUP["uv"] + i
                pe.wait_ge(gemm_freed, n - 3)
                for k in range(2):
                    last = pe.matmul(bank[n % 4][:, :], ckvT[:, k, t * P:(t + 1) * P], w[:, k, 512 * h:512 * h + 512], start=k == 0, stop=k == 1)
                last.then_inc(gemm_ready, 1)
            for i in range(2):
                feat_groups_whole(pe, f"uq{i}", 0, cqT, 0, L, GROUP["uq"] + 8 * i, C_HEADS // 2)
            pe.wait_ge(gemm_freed, GROUP["uq"] + C_HEADS)
            pe.wait_ge(q_rotated, C_HEADS)
            pe.wait_ge(sel_done, 1)

            def scores(pe, u, b):
                h, qt = u // 2, u % 2
                return pe.matmul(b[:, 0:causal_w(u)], q_c[:, h, qt * P:(qt + 1) * P], k_c[:, h, 0:causal_w(u)], start=True, stop=True)
            att_pe(pe, AC, scores, AC.hooks[0])
            pe.wait_ge(att_stored, (AC.values_first + C_HEADS) // 2)
            rows_product(pe, "o1", oTc, lambda pe: turn_tile(pe, LATENT, 0))
            turn_tile(pe, LATENT, 1)

        def c_act(act):
            link = stepper(act, act_step)
            junk = acc.rearrange("p t l -> p (t l)")
            for i in range(4):
                c, t = 1 - i // 2, i % 2
                n = GROUP["cin"] + i
                act.wait_ge(gemm_ready, n + 1)
                w = (512, CW - 512)[c]
                act.copy(cct[:, t, 512 * c:512 * c + w], bank[n % 4][:, 0:w]).then_inc(gemm_freed, 1)
                if c == 0:
                    act.wait_ge(gemm_freed, n + 1)
                    for j, (at, n) in enumerate(((0, CQ), (CQ, CKV))):
                        link(act.activation(junk[:, 0:n], cct[:, t, at:at + n], ACT.Square, accum_out=stc[:, 2 * j + t:2 * j + t + 1]))
                    for j, n in enumerate((CQ, CKV)):
                        act.activation(stc[:, 4 + 2 * j + t:5 + 2 * j + t], stc[:, 2 * j + t:2 * j + t + 1], ACT.Sqrt, bias=epsc[:, :],
                                       scale=1.0 / n).then_inc(c_std, 1)
            act.wait_ge(gemm_freed, GROUP["uk"])
            for b in range(C_HEADS // 2):
                n = GROUP["uk"] + b
                act.wait_ge(gemm_ready, n + 1)
                link(act.copy(k_c[0:64, 2 * b, :], bank[n % 4][0:64, 0:L]))
                act.copy(k_c[64:128, 2 * b + 1, :], bank[n % 4][64:128, 0:L]).then_inc(gemm_freed, 1)
            for n in range(2 * IDX_HEADS):
                w = causal_w(n // IDX_HEADS)
                act.wait_ge(ix_ready, n + 1)
                if n >= 2:
                    act.wait_ge(ix_added, n - 1)
                act.activation(relu[:, n % 2, 0:w], bank[4 + n % 2][:, 0:w], ACT.Relu).then_inc(ix_relu, 1)
            for i in range(4):
                h, t = i // 2, i % 2
                n = GROUP["uv"] + i
                act.wait_ge(gemm_ready, n + 1)
                act.copy(v_c[:, t, 512 * h:512 * h + 512], bank[n % 4][:, :]).then_inc(gemm_freed, 1)
            for h in range(C_HEADS):
                n = GROUP["uq"] + h
                act.wait_ge(gemm_ready, n + 1)
                act.copy(q_c[:, h, :], bank[n % 4][:, 0:L]).then_inc(gemm_freed, 1)
            att_act(act, AC, AC.hooks[2])
            split_early_act(act, 1)
            close_act(act, LATENT, rows_ready, [ROWS["o1"] + j + 1 for j in range(4)], tmp_c)

        def c_pool(pool):
            pool.wait_ge(tab_in, 32)
            for h in range(C_HEADS):
                pool.wait_ge(gemm_freed, GROUP["uq"] + h + 1)
                pool.tensor_tensor(q_c[:, h, :], q_c[:, h, :], tb(("cq_even", "cq_odd")[h % 2]), ALU.mult).then_inc(q_rotated, 1)

        def c_dve(dve):
            link = stepper(dve, dve_step)

            def turned_block(i):
                b = bank[6 + i % 2]
                dve.wait_ge(ct_ready, i + 1)
                if 2 <= i < 5:
                    ins = dve.tensor_scalar(cqT[:, i - 2, :], b[:, 0:L], pc("cq", i - 2), None, ALU.mult)
                elif i >= 5:
                    ins = dve.tensor_scalar(ckvT[:, i - 5, :], b[:, 0:L], pc("ckv", i - 5), None, ALU.mult)
                elif i == 0:
                    for odd in range(2):
                        p = slice(64 - 64 * odd, 128 - 64 * odd)
                        ins = dve.tensor_copy(k_c[p, odd:C_HEADS:2, :], b[p, 0:L].unsqueeze(1).broadcast_to([64, C_HEADS // 2, L]))
                        if not odd:
                            link(ins)
                else:
                    ins = dve.tensor_copy(kiT, b[:, 0:L])
                ins.then_inc(ct_out, 1)
            r0 = CQ + CKV
            dve.wait_ge(gemm_freed, GROUP["cin"] + TT)
            for t in range(TT):
                x = cct[:, t, r0:r0 + 64]
                xs = x.rearrange("p (g h j) -> p g h j", g=2, h=2)
                ys = rot[:, 1, t, :].rearrange("p (g h j) -> p g h j", g=2, h=2)
                ss = tokt[:, t, 1, :].rearrange("p (g h j) -> p g h j", g=2, h=2)
                link(dve.tensor_tensor(rot[:, 0, t, :], x, tokt[:, t, 0, :], ALU.mult))
                for h in range(2):
                    link(dve.tensor_tensor(ys[:, :, h, :], xs[:, :, 1 - h, :], ss[:, :, h, :], ALU.mult))
                link(dve.tensor_tensor(rot[:, 0, t, :], rot[:, 0, t, :], rot[:, 1, t, :], ALU.add))
                link(dve.tensor_copy(krep[:, t, :].rearrange("p (r j) -> p r j", r=4), rot[:, 0, t, 0:32].unsqueeze(1).broadcast_to([P, 4, 32])))
                kr = kirep[:, t, :].rearrange("p (r j) -> p r j", r=4)
                link(dve.tensor_copy(kr[:, 0:2, :], rot[:, 0, t, 32:64].unsqueeze(1).broadcast_to([P, 2, 32])))
                dve.tensor_copy(kr[:, 2:4, :], cct[:, t, r0 + 64:r0 + 96].unsqueeze(1).broadcast_to([P, 2, 32])).then_inc(c_rot, 1)
            link(dve.tensor_scalar(wi, cct[:, :, CW - IDX_HEADS:CW], IDX_HEADS ** -0.5 * HD ** -0.5, None, ALU.mult))
            turned_block(0)
            turned_block(1)
            for t in range(TT):
                dve.wait_ge(c_std, 2 * t + 2)
                link(dve.reciprocal(stc[:, 8 + t:12:2], stc[:, 4 + t:8:2]))
                q, kv = cct[:, t, 0:CQ], cct[:, t, CQ:CQ + CKV]
                dve.tensor_scalar(q, q, stc[:, 8 + t:9 + t], None, ALU.mult).then_inc(c_norm, 1)
                dve.tensor_scalar(kv, kv, stc[:, 10 + t:11 + t], None, ALU.mult).then_inc(c_norm, 1)
            for i in range(2, N_TURNED):
                turned_block(i)
            dve.wait_ge(tab_in, 32)
            for h in range(IDX_HEADS):
                g = GROUP["qi"] + h
                dve.wait_ge(gemm_ready, g + 1)
                if h == 0:
                    dve.wait_ge(gemm_freed, g)
                dve.tensor_tensor(qi[:, h, :], bank[g % 4][:, 0:L], tb("ci"), ALU.mult).then_inc(gemm_freed, 1)
            for qt in range(TT):
                w = causal_w(qt)
                a, m = acc[:, qt, 0:w], mask_of(0, qt)
                for h in range(IDX_HEADS):
                    n = IDX_HEADS * qt + h
                    dve.wait_ge(ix_relu, n + 1)
                    dve.scalar_tensor_tensor(a, relu[:, n % 2, 0:w], wi[:, qt, h:h + 1], m if h == 0 else a, ALU.mult, ALU.add).then_inc(ix_added, 1)
                    dve.wait_ge(ix_added, n + 1)
            for qt in range(TT):
                w = causal_w(qt)
                a, m = acc[:, qt, 0:w], mask_of(0, qt)
                for r in range(TOPK // 8):
                    link(dve.max(top9, a))
                    link(dve.match_replace(a, top9, a, -3e38))
                link(dve.tensor_scalar(a, a, -2e38, NEG, ALU.is_gt, ALU.mult))
                link(dve.tensor_tensor(bsel[:, qt, 0:w], a, m, ALU.add))
            dve.sem_inc(sel_done, 1)
            att_dve(dve, AC, AC.hooks[1])
            dve.wait_ge(grow_loaded, 48)
            close_dve(dve, LATENT, tmp_c, pc("mlp_pre2", 8, 8), parts=True)

        out_in = sem("out_in")
        N_CONSTS, N_TABLES = 3, 5
        block = es.enter_context(nc.Block())

        @block.sync
        def _(sp):
            sp.dma_start(cc, d["cc"]).then_inc(consts_in, 16)
            sp.dma_start(cst[:, :], d["cst"]).then_inc(consts_in, 16)
            sp.dma_start(pcol[:, :], d["pcol"]).then_inc(consts_in, 16)

            def load(c):
                src, kt, n, _ = chunks[c]
                if c >= SLOTS and chunks[c - SLOTS] is not None:
                    sp.wait_ge(*chunks[c - SLOTS][3])
                dst = ring[:, c % SLOTS, 0:kt * n].rearrange("p (t n) -> p t n", t=kt)
                sp.dma_start(dst, src).then_inc(slot_full[c % SLOTS], 16)

            for c in range(FE):
                if c == ADA_FIRST:
                    sp.dma_start(heads[:, :], d["heads"].partition_broadcast(P).rearrange("q o n -> q (o n)")).then_inc(tables_in, 16)
                    sp.dma_start(tab_na, d["tab"][:, 0:4, :]).then_inc(tables_in, 16)
                    sp.dma_start(tokt[:, :, :, :], d["tokt"]).then_inc(tables_in, 16)
                    sp.dma_start(masks[:, :, :], d["masks"]).then_inc(tables_in, 16)
                    sp.dma_start(router[:, :, :], d["w_router"].rearrange("(t p) n -> p t n", p=P)).then_inc(tables_in, 16)
                load(c)

            def expert_sources(e):
                for w, rows, n in (("w_egate", 2 * P, FF), ("w_eup", 2 * P, FF), ("w_edown", 4 * P, D)):
                    for c in range(4):
                        s = d[w][bass.ds(e, 1), rows * c:rows * c + rows, :].rearrange("e (t p) n -> p (e t) n", p=P)
                        yield s, rows // P

            def expert_left(k, e):
                which, c = k // 4, k % 4
                if c == 3:
                    return (gate_ready, up_ready, down_ready)[which], e + 1
                return expert_used, e * 9 + (3 * which + c + 1)

            def load_expert(e, first):
                for k, (src, kt) in enumerate(expert_sources(e)):
                    if k < 4:
                        sp.wait_ge(*(chunks[FE - SLOTS + k][3] if first else expert_left(8 + k, e - 1)))
                    else:
                        sp.wait_ge(*expert_left(k - 4, e))
                    s = (FE + k) % SLOTS
                    sp.dma_start(ring[:, s, :].rearrange("p (t n) -> p t n", t=kt), src).then_inc(slot_full[s], 16)

            load_expert(0, True)
            with sp.Fori(1, NE) as e:
                load_expert(e, False)
            for c in range(FE + 12 * NE, len(chunks)):
                if c < FE + 12 * NE + SLOTS:
                    sp.wait_ge(*expert_left(8 + c - FE - 12 * NE, NE - 1))
                load(c)
            sp.wait_ge(x_done, 4 * 8)
            sp.dma_start(out.rearrange("b (t p) n -> p (b t) n", p=P), xres[:, :, :]).then_inc(out_in, 16)
            sp.wait_ge(out_in, 16)

        @block.tensor
        def _(pe):
            ada_pe(pe)
            pe.wait_ge(tables_in, 16 * N_TABLES)
            end_stage(pe, "pe")
            for hf in range(2):
                na_proj_pe(pe, hf)
                end_stage(pe, "pe")
                att_pe(pe, NA[hf], na_scores_of(hf), NA[hf].hooks[0], ada_rest_pe() if hf else {})
                end_stage(pe, "pe")
            ssd_pe(pe)
            end_stage(pe, "pe")
            merge_pe(pe)
            end_stage(pe, "pe")
            route_pe(pe)
            end_stage(pe, "pe")
            experts_pe(pe)
            for l in range(2):
                if l == 0:
                    for t in range(TT):
                        turn_tile(pe, EXPERTS, t)
                    end_stage(pe, "pe")
                    ab_proj_pe(pe)
                    end_stage(pe, "pe")
                    ab_att_pe(pe)
                else:
                    c_pe(pe)
                end_stage(pe, "pe")
                mlp_pe(pe, l)
                end_stage(pe, "pe")
                ple_pe(pe, l)
                end_stage(pe, "pe")

        @block.scalar
        def _(act):
            ada_act(act)
            act.wait_ge(tables_in, 16 * N_TABLES)
            end_stage(act, "act")
            for hf in range(2):
                na_proj_act(act, hf)
                end_stage(act, "act")
                att_act(act, NA[hf], NA[hf].hooks[2], na_splits_act(hf))
                end_stage(act, "act")
            ssd_act(act)
            end_stage(act, "act")
            merge_act(act)
            end_stage(act, "act")
            route_act(act)
            end_stage(act, "act")
            experts_act(act)
            for l in range(2):
                if l == 0:
                    split_upper(act, "aq_0")
                    for t in range(TT):
                        post_act(act, scattered, [2 + NE] * 4, tmp5, t)
                    for t in range(TT):
                        norm_act(act, EXPERTS, t)
                    split_upper(act, "aq_1")
                    end_stage(act, "act")
                    ab_proj_act(act)
                    end_stage(act, "act")
                    ab_att_act(act)
                else:
                    c_act(act)
                end_stage(act, "act")
                mlp_act(act, l)
                end_stage(act, "act")
                ple_act(act, l)
                end_stage(act, "act")

        @block.vector
        def _(dve):
            ada_dve(dve)
            dve.wait_ge(tables_in, 16 * N_TABLES)
            end_stage(dve, "dve")
            for hf in range(2):
                na_proj_dve(dve, hf)
                end_stage(dve, "dve")
                att_dve(dve, NA[hf], NA[hf].hooks[1])
                if hf:
                    ada_rest_dve(dve)
                end_stage(dve, "dve")
            ssd_dve(dve)
            end_stage(dve, "dve")
            merge_dve(dve)
            end_stage(dve, "dve")
            route_dve(dve)
            end_stage(dve, "dve")
            experts_dve(dve)
            for l in range(2):
                if l == 0:
                    close_dve(dve, EXPERTS, tmp5, pc("mix_pre2", 0, 8), parts=True, together=True)
                    end_stage(dve, "dve")
                    ab_proj_dve(dve)
                    end_stage(dve, "dve")
                    ab_att_dve(dve)
                else:
                    c_dve(dve)
                end_stage(dve, "dve")
                mlp_dve(dve, l)
                end_stage(dve, "dve")
                ple_dve(dve, l)
                end_stage(dve, "dve")

        @block.gpsimd
        def _(pool):
            ada_pool(pool)
            end_stage(pool, "pool")
            for hf in range(2):
                if hf == 0:
                    split_after(split_lower, pool, "ada2")
                na_proj_pool(pool, hf)
                na_bias_pool(pool, hf, 0, BIASES)
                end_stage(pool, "pool")
                na_bias_pool(pool, hf, BIASES, 8)
                for name in next_splits(hf):
                    split_lower(pool, name)
                end_stage(pool, "pool")
            ssd_pool(pool)
            end_stage(pool, "pool")
            merge_pool(pool)
            end_stage(pool, "pool")
            pool.dma_start(tab, d["tab"][:, 4:8, :]).then_inc(tab_in, 16)
            route_pool(pool)
            end_stage(pool, "pool")
            for l in range(2):
                if l == 0:
                    split_lower(pool, "aq_0")
                    end_stage(pool, "pool")
                    split_lower(pool, "aq_1")
                    load_grow(pool, 0)
                    ab_proj_pool(pool)
                    end_stage(pool, "pool")
                    split_early_pool(pool, 0)
                    end_stage(pool, "pool")
                    pool.dma_start(tab[:, 0:3, :], d["tab"][:, 8:11, :]).then_inc(tab_in, 16)
                else:
                    load_grow(pool, 2)
                    c_pool(pool)
                    split_early_pool(pool, 1)
                    end_stage(pool, "pool")
                load_grow(pool, 2 * l + 1)
                mlp_pool(pool, l)
                end_stage(pool, "pool")
                ple_pool(pool, l)
                end_stage(pool, "pool")


def kernel(**inputs):
    import concourse.bacc as bacc
    from concourse.bass_utils import run_bass_kernel_spmd

    nc = bacc.Bacc("TRN2", target_bir_lowering=False, num_devices=1)
    arrays = layouts(inputs)
    d = {n: nc.dram_tensor(f"in_{n}", a.shape, mybir.dt.from_np(a.dtype), kind="ExternalInput").ap() for n, a in arrays.items()}
    out = nc.dram_tensor("out", (1, L, D), F32, kind="ExternalOutput").ap()
    build(nc, d, out)
    r = run_bass_kernel_spmd(nc, [{f"in_{n}": a for n, a in arrays.items()}], core_ids=[0])
    return r.results[0]["out"]
```
